# Optimizing a Trainium2 kernel written in Bass

```python
import math
import jax, jax.numpy as jnp
from jax import lax
import numpy as np

D_MODEL = 2048
BATCH = 1
SEQ = 256
DEPTH = 2

GRID_W = 64
CTX_LEN = 256
N_ADA = 6
EPS = 1e-6
GDN_DK = 128
GDN_DV = 128
GDN_HEADS = (D_MODEL // 2) // GDN_DV
GDN_CHUNK = 64
SHORT_CONV = 5
GDN_QK = GDN_HEADS * GDN_DK
GDN_VW = GDN_HEADS * GDN_DV
GDN_QKV = 2 * GDN_QK + GDN_VW
GDN_IN = GDN_QKV + 4 * GDN_HEADS
POOL_GROUPS = 4
POOL_RADII = (1, 2, 4, 8)
POOL_W = D_MODEL // 2
POOL_GC = POOL_W // POOL_GROUPS
EVEN_IN = GDN_IN + GDN_VW + POOL_W
EVEN_MIX = GDN_VW + POOL_W
SGU_W = D_MODEL
SGU_GROUPS = 4
SGU_CHUNK = 128
D_FF = 4 * D_MODEL
N_EVEN = (DEPTH + 1) // 2
N_ODD = DEPTH // 2
ADA_SCALE = 0.5

kernel_name = "hybrid_gdn_pool_sgu_dit_block"

F32 = jnp.float32

def _rmsnorm(x, g):
    xf = x.astype(F32)
    y = xf * lax.rsqrt(jnp.mean(xf * xf, axis=-1, keepdims=True) + EPS)
    return (y * g.astype(F32)).astype(x.dtype)

def _layernorm(x, g, b):
    xf = x.astype(F32)
    mu = jnp.mean(xf, axis=-1, keepdims=True)
    var = jnp.mean(jnp.square(xf - mu), axis=-1, keepdims=True)
    return ((xf - mu) * lax.rsqrt(var + EPS) * g.astype(F32) + b.astype(F32)).astype(x.dtype)

def _l2norm(t):
    tf = t.astype(F32)
    return tf * lax.rsqrt(jnp.sum(tf * tf, axis=-1, keepdims=True) + EPS)

def _ada(cvec, w, b):
    mod = jax.nn.silu(cvec) @ w + b
    return mod.reshape(cvec.shape[:-1] + (N_ADA, w.shape[0]))

def _modulate(h, g, shift, scale):
    return _rmsnorm(h, g) * (1 + scale) + shift

def _grid_pos_embed(L, d):
    rows = L // GRID_W
    nf = d // 4
    omega = 1.0 / (10000.0 ** (jnp.arange(nf, dtype=F32) / nf))
    r = jnp.repeat(jnp.arange(rows, dtype=F32), GRID_W)
    col = jnp.tile(jnp.arange(GRID_W, dtype=F32), rows)
    ar = r[:, None] * omega
    ac = col[:, None] * omega
    return jnp.concatenate([jnp.sin(ar), jnp.cos(ar), jnp.sin(ac), jnp.cos(ac)], axis=-1)

def _short_conv(x, w):
    pad = (SHORT_CONV - 1) // 2
    return lax.conv_general_dilated(
        x, w[:, None, :].astype(x.dtype), window_strides=(1,), padding=[(pad, pad)],
        dimension_numbers=("NWC", "WIO", "NWC"), feature_group_count=x.shape[-1])

def _gdn_inputs(p, conv_w):
    B, L, _ = p.shape
    qkv = jax.nn.silu(_short_conv(p[..., :GDN_QKV], conv_w))
    q = _l2norm(qkv[..., :GDN_QK].reshape(B, L, GDN_HEADS, GDN_DK)) * (GDN_DK ** -0.5)
    k = _l2norm(qkv[..., GDN_QK:2 * GDN_QK].reshape(B, L, GDN_HEADS, GDN_DK))
    v = qkv[..., 2 * GDN_QK:].reshape(B, L, GDN_HEADS, GDN_DV)
    ab = p[..., GDN_QKV:].reshape(B, L, 2, 2, GDN_HEADS)
    return q, k, v, ab[:, :, 0], ab[:, :, 1]

def _gdn_chunk_scan(q, k, v, g, beta, s0, with_output):
    B, L, H, DK = q.shape
    DV = v.shape[-1]
    C = GDN_CHUNK
    N = L // C

    def blk(t):
        t = t.astype(F32).reshape((B, N, C, H) + t.shape[3:])
        return jnp.moveaxis(t, (1, 3), (0, 2))

    qc, kc, vc, gc, bc = blk(q), blk(k), blk(v), blk(g), blk(beta)
    gam = jnp.cumsum(gc, axis=-1)
    idx = jnp.arange(C)
    incl = idx[:, None] >= idx[None, :]
    strict = idx[:, None] > idx[None, :]
    diff = gam[..., :, None] - gam[..., None, :]
    dmat = jnp.where(incl, jnp.exp(jnp.where(incl, diff, 0.0)), 0.0)
    kb = kc * bc[..., None]
    a_mat = jnp.where(strict, jnp.einsum("nbhid,nbhjd->nbhij", kb, kc) * dmat, 0.0) + jnp.eye(C, dtype=F32)
    rhs = jnp.concatenate([vc * bc[..., None], kb * jnp.exp(gam)[..., None]], axis=-1)
    sol = lax.linalg.triangular_solve(a_mat, rhs, left_side=True, lower=True, unit_diagonal=True)
    u, w = sol[..., :DV], sol[..., DV:]
    g_last = gam[..., -1]
    k_dec = kc * jnp.exp(g_last[..., None] - gam)[..., None]
    d_last = jnp.exp(g_last)
    s0 = s0.astype(F32)
    if with_output:
        q_dec = qc * jnp.exp(gam)[..., None]
        qk = jnp.where(incl, jnp.einsum("nbhid,nbhjd->nbhij", qc, kc) * dmat, 0.0)

        def step(s, xs):
            u_n, w_n, kd_n, dl_n, qd_n, qk_n = xs
            v_new = u_n - jnp.einsum("bhck,bhkv->bhcv", w_n, s)
            o = jnp.einsum("bhck,bhkv->bhcv", qd_n, s) + jnp.einsum("bhij,bhjv->bhiv", qk_n, v_new)
            s = s * dl_n[..., None, None] + jnp.einsum("bhck,bhcv->bhkv", kd_n, v_new)
            return s, o

        s_fin, o = lax.scan(step, s0, (u, w, k_dec, d_last, q_dec, qk))
        o = jnp.moveaxis(o, (0, 2), (1, 3)).reshape(B, L, H, DV)
        return o, s_fin

    def step_state(s, xs):
        u_n, w_n, kd_n, dl_n = xs
        v_new = u_n - jnp.einsum("bhck,bhkv->bhcv", w_n, s)
        s = s * dl_n[..., None, None] + jnp.einsum("bhck,bhcv->bhkv", kd_n, v_new)
        return s, None

    s_fin, _ = lax.scan(step_state, s0, (u, w, k_dec, d_last))
    return None, s_fin

def _gdn_bidir(q, k, v, a, b, a_log, dt_bias, s0f, s0b, with_output):
    g = -jnp.exp(a_log.astype(F32)) * jax.nn.softplus(a.astype(F32) + dt_bias.astype(F32))
    beta = jax.nn.sigmoid(b.astype(F32))
    rev = lambda t: jnp.flip(t, axis=1)
    of, sf = _gdn_chunk_scan(q, k, v, g[:, :, 0], beta[:, :, 0], s0f, with_output)
    ob, sb = _gdn_chunk_scan(rev(q), rev(k), rev(v), rev(g[:, :, 1]), rev(beta[:, :, 1]), s0b, with_output)
    if with_output:
        return of + rev(ob), sf, sb
    return None, sf, sb

def _zero_state(batch):
    return jnp.zeros((batch, GDN_HEADS, GDN_DK, GDN_DV), F32)

def _multiscale_pool(h):
    B, L, _ = h.shape
    hf = h.astype(F32)
    csum = jnp.pad(jnp.cumsum(hf, axis=1), ((0, 0), (1, 0), (0, 0)))
    t = jnp.arange(L)
    means = []
    for gi, r in enumerate(POOL_RADII):
        hi = jnp.minimum(t + r + 1, L)
        lo = jnp.maximum(t - r, 0)
        seg = csum[..., gi * POOL_GC:(gi + 1) * POOL_GC]
        means.append((seg[:, hi] - seg[:, lo]) / (hi - lo).astype(F32)[:, None])
    return (jnp.concatenate(means, axis=-1) - hf).astype(h.dtype)

def _even_mixer(h, w_in, conv_w, a_log, dt_bias, onorm_g, pool_w, pool_scale, w_out, s0f, s0b):
    B, L, _ = h.shape
    p = h @ w_in
    q, k, v, a, b = _gdn_inputs(p[..., :GDN_IN], conv_w)
    o, sf, sb = _gdn_bidir(q, k, v, a, b, a_log, dt_bias, s0f, s0b, True)
    z = p[..., GDN_IN:GDN_IN + GDN_VW].reshape(B, L, GDN_HEADS, GDN_DV)
    y_a = (_rmsnorm(o, onorm_g) * jax.nn.silu(z.astype(F32))).reshape(B, L, GDN_VW).astype(h.dtype)
    pooled = _multiscale_pool(p[..., GDN_IN + GDN_VW:]).reshape(B, L, POOL_GROUPS, POOL_GC)
    y_b = jnp.einsum("blgc,gcd->blgd", pooled, pool_w).reshape(B, L, POOL_W) * pool_scale
    y = jnp.concatenate([y_a, y_b], axis=-1) @ w_out
    return y, sf, sb

def _context_states(hc, w_in, conv_w, a_log, dt_bias):
    p = hc @ w_in[:, :GDN_IN]
    q, k, v, a, b = _gdn_inputs(p, conv_w)
    z0 = _zero_state(hc.shape[0])
    _, sf, sb = _gdn_bidir(q, k, v, a, b, a_log, dt_bias, z0, z0, False)
    return sf, sb

def _odd_mixer(h, w_in, ln_g, ln_b, w_s, b_s, w_out):
    B, L, _ = h.shape
    zz = jax.nn.gelu(h @ w_in, approximate=False)
    u, v = zz[..., :SGU_W], zz[..., SGU_W:]
    v = _layernorm(v, ln_g, ln_b).reshape(B, L // SGU_CHUNK, SGU_CHUNK, SGU_GROUPS, SGU_W // SGU_GROUPS)
    mixed = jnp.einsum("bnsgc,gts->bntgc", v, w_s) + b_s.T[None, None, :, :, None]
    return (u * mixed.reshape(B, L, SGU_W)) @ w_out

def _mlp(h, w1, w2):
    return jnp.square(jax.nn.relu(h @ w1)) @ w2

def setup_inputs(seed: int = 0) -> dict:
    key = jax.random.key(seed)
    ks = jax.random.split(key, 32)
    D = D_MODEL

    def nrm(k, shape, fan):
        return jax.random.normal(k, shape, F32) * (fan ** -0.5)

    def gain(k, shape):
        return 1.0 + 0.05 * jax.random.normal(k, shape, F32)

    dt = jnp.exp(jax.random.uniform(ks[13], (N_EVEN, 2, GDN_HEADS), F32,
                                    math.log(1e-3), math.log(1e-1)))
    return {
        "x": jax.random.normal(ks[0], (BATCH, SEQ, D), F32),
        "c": jax.random.normal(ks[1], (BATCH, D), F32),
        "ctx": jax.random.normal(ks[2], (BATCH, CTX_LEN, D), F32),
        "c_ctx": jax.random.normal(ks[3], (D,), F32),
        "ada_w": nrm(ks[4], (DEPTH, D, N_ADA * D), D) * ADA_SCALE,
        "ada_b": 0.01 * jax.random.normal(ks[5], (DEPTH, N_ADA * D), F32),
        "norm1_g": gain(ks[6], (DEPTH, D)),
        "norm2_g": gain(ks[7], (DEPTH, D)),
        "mlp_w1": nrm(ks[8], (DEPTH, D, D_FF), D),
        "mlp_w2": nrm(ks[9], (DEPTH, D_FF, D), D_FF),
        "ev_w_in": nrm(ks[10], (N_EVEN, D, EVEN_IN), D),
        "ev_conv_w": nrm(ks[11], (N_EVEN, SHORT_CONV, GDN_QKV), SHORT_CONV),
        "ev_a_log": jnp.log(jax.random.uniform(ks[12], (N_EVEN, 2, GDN_HEADS), F32, 1.0, 16.0)),
        "ev_dt_bias": dt + jnp.log(-jnp.expm1(-dt)),
        "ev_onorm_g": gain(ks[14], (N_EVEN, GDN_DV)),
        "ev_pool_w": nrm(ks[15], (N_EVEN, POOL_GROUPS, POOL_GC, POOL_GC), POOL_GC),
        "ev_pool_scale": gain(ks[16], (N_EVEN, POOL_W)),
        "ev_w_out": nrm(ks[17], (N_EVEN, EVEN_MIX, D), EVEN_MIX),
        "od_w_in": nrm(ks[18], (N_ODD, D, 2 * SGU_W), D),
        "od_ln_g": gain(ks[19], (N_ODD, SGU_W)),
        "od_ln_b": 0.01 * jax.random.normal(ks[20], (N_ODD, SGU_W), F32),
        "od_ws": nrm(ks[21], (N_ODD, SGU_GROUPS, SGU_CHUNK, SGU_CHUNK), SGU_CHUNK),
        "od_bs": 1.0 + 0.02 * jax.random.normal(ks[22], (N_ODD, SGU_GROUPS, SGU_CHUNK), F32),
        "od_w_out": nrm(ks[23], (N_ODD, SGU_W, D), SGU_W),
        "final_g": gain(ks[24], (D,)),
    }

def reference(x, c, ctx, c_ctx, ada_w, ada_b, norm1_g, norm2_g, mlp_w1, mlp_w2,
              ev_w_in, ev_conv_w, ev_a_log, ev_dt_bias, ev_onorm_g, ev_pool_w, ev_pool_scale, ev_w_out,
              od_w_in, od_ln_g, od_ln_b, od_ws, od_bs, od_w_out, final_g):
    B, L, D = x.shape
    h_x = x + _grid_pos_embed(L, D).astype(x.dtype)[None]
    h_c = ctx
    last_even = 2 * ((DEPTH - 1) // 2)
    for i in range(DEPTH):
        j = i // 2
        mx = _ada(c, ada_w[i], ada_b[i])[:, None]
        mc = _ada(c_ctx, ada_w[i], ada_b[i])
        ctx_full = i < last_even
        hx = _modulate(h_x, norm1_g[i], mx[..., 0, :], mx[..., 1, :])
        if i % 2 == 0:
            ev = (ev_w_in[j], ev_conv_w[j], ev_a_log[j], ev_dt_bias[j], ev_onorm_g[j],
                  ev_pool_w[j], ev_pool_scale[j], ev_w_out[j])
            hc = _modulate(h_c, norm1_g[i], mc[0], mc[1])
            if ctx_full:
                z0 = _zero_state(B)
                yc, sf, sb = _even_mixer(hc, *ev, z0, z0)
            else:
                sf, sb = _context_states(hc, ev_w_in[j], ev_conv_w[j], ev_a_log[j], ev_dt_bias[j])
            yx, _, _ = _even_mixer(hx, *ev, sf, sb)
        else:
            od = (od_w_in[j], od_ln_g[j], od_ln_b[j], od_ws[j], od_bs[j], od_w_out[j])
            yx = _odd_mixer(hx, *od)
            if ctx_full:
                yc = _odd_mixer(_modulate(h_c, norm1_g[i], mc[0], mc[1]), *od)
        h_x = h_x + mx[..., 2, :] * yx
        h_x = h_x + mx[..., 5, :] * _mlp(_modulate(h_x, norm2_g[i], mx[..., 3, :], mx[..., 4, :]),
                                         mlp_w1[i], mlp_w2[i])
        if ctx_full:
            h_c = h_c + mc[2] * yc
            h_c = h_c + mc[5] * _mlp(_modulate(h_c, norm2_g[i], mc[3], mc[4]), mlp_w1[i], mlp_w2[i])
    return _rmsnorm(h_x, final_g)


_drawn_inputs = setup_inputs


def setup_inputs(seed=0):
    import zlib

    import numpy as np

    out = dict(_drawn_inputs(seed))
    spreads = {}
    factors = {'ctx': 3.488,
     'c_ctx': 6.278,
     'ada_b': 2.783,
     'norm1_g': 2.888,
     'ev_a_log': 3.357,
     'ev_onorm_g': 8.0,
     'ev_pool_scale': 7.782,
     'od_ln_g': 6.936,
     'od_ln_b': 8.0,
     'od_bs': 8.0}
    for name, (base, spread) in spreads.items():
        noise = np.random.default_rng([zlib.crc32(name.encode()), seed]).standard_normal(out[name].shape)
        drawn = base * np.exp(spread * noise) if base else spread * noise
        out[name] = __import__('jax').numpy.asarray(drawn.astype(out[name].dtype))
    for name, factor in factors.items():
        out[name] = (out[name] * factor).astype(out[name].dtype)
    return out
```

```python
import concourse.bass as bass
from concourse import mybir
from contextlib import ExitStack

F32 = mybir.dt.float32
F32R = mybir.dt.float32r
ALU = mybir.AluOpType
ACT = mybir.ActivationFunctionType
AX = mybir.AxisListType
ds = bass.ds

P = 128
D = 2048
KC = D // P
L = 256
NT = L // P
CB = 512
H = 8
QKV = 3 * H * P
EV_IN = QKV + 4 * H + 2 * H * P
ZP0 = QKV + 4 * H
FF = 4 * D
SLAB = 1024
SK = SLAB // P
SLABS = FF // SLAB
EPS = 1e-6
LEVELS = 7
UNIT = 2
UPB = KC // UNIT
RAW = 8
SPLIT = 4

U_KV, U_Q, U_ZP, U_OUT, U_MLP0 = 0, 32, 48, 80, 112
U_OIN, U_OOUT, U_MLP1 = 368, 432, 464
N_ZP, N_OUT, N_MLP0, N_OIN, N_OOUT, N_MLP1 = 0, 4, 8, 56, 64, 68
A0_UNITS = 64

TILE = [[2, 3, 0, 1], [3, 2, 1, 0]]


class Units:

    def __init__(self, base, step=0, i=None):
        self.base, self.step, self.i = base, step, i

    def u(self, j, off=0):
        c = self.base + j + off
        return c if self.i is None else self.i * self.step + c

    def r(self, j, off=0):
        c = (self.base + j) // RAW + off
        return c if self.i is None else self.i * (self.step // RAW) + c

    def r16(self, j, off=0):
        c = 16 * ((self.base + j) // RAW + off)
        return c if self.i is None else self.i * (16 * self.step // RAW) + c


class Chain:

    def __init__(self, eng, sem):
        self.eng, self.sem, self.n, self.base = eng, sem, 0, 0

    def __call__(self, ins):
        self.n += 1
        ins.then_inc(self.sem, 1)
        self.eng.wait_ge(self.sem, self.base + self.n)

    def enter(self, i, per):
        self.n0, self.per = self.n, per
        self.base, self.n = i * per + self.n0, 0

    def leave(self, turns):
        assert self.n == self.per, f"{self.n} steps in a turn, not {self.per}"
        self.n, self.base = self.n0 + turns * self.per, 0

class Turn:

    def __init__(self, n0, layer, i=None):
        self.n0, self.layer, self.i = n0, layer, i

    def add(self, c, per):
        return c if self.i is None else self.i * per + c

    def n(self, n, off):
        return self.add(self.n0 + n + off, 12)

    __call__ = n

    def free(self, n):
        return self.add(2 * ((self.n0 + n) // 2), 12)

    def tau(self, tau, off):
        return self.add(32 * self.layer + 2 * tau + off, 8)

    def e(self, e, off):
        return self.add(8 + 72 * self.layer + 2 * e + off, 16)


def build(nc, A, out):
    stack = ExitStack()
    with stack:
        def sem(name):
            return stack.enter_context(nc.semaphore(name))

        def dram(name, shape):
            return nc.dram_tensor(name, shape, F32, kind="Internal").ap()

        def sbuf(where, name, shape, dt=F32):
            return where.enter_context(nc.sbuf_tensor(name, [P] + shape, dt))

        raw = sbuf(stack, "raw", [RAW, UNIT * CB])
        wh = sbuf(stack, "wh", [SPLIT, UNIT * CB], F32R)
        wl = sbuf(stack, "wl", [SPLIT, UNIT * CB], F32R)
        ada_raw = sbuf(stack, "ada_raw", [2, D])
        ada_acc = sbuf(stack, "ada_acc", [D])
        gate = sbuf(stack, "gate", [2, D])
        ident = sbuf(stack, "ident", [P])
        ones = sbuf(stack, "ones", [P])
        ccol = sbuf(stack, "ccol", [KC, 2])
        csil = sbuf(stack, "csil", [KC, 2])
        mod0 = sbuf(stack, "mod0", [2 * KC, 2])
        adab = sbuf(stack, "adab", [12, KC])
        gcol = sbuf(stack, "gcol", [4, KC])
        shc = sbuf(stack, "shc", [5, KC])
        gsc = sbuf(stack, "gsc", [5, KC])
        eps = sbuf(stack, "eps", [1])
        ss = sbuf(stack, "ss", [16])
        rs = sbuf(stack, "rs", [16])
        bscol = sbuf(stack, "bscol", [4])
        colbuf = sbuf(stack, "colbuf", [3 * KC])
        spl = sbuf(stack, "spl", [512])
        PS = stack.enter_context(nc.psum_tensor("PS", [P, 8, 512], F32))

        e1 = ExitStack()
        x1h = sbuf(e1, "x1h", [KC, 2 * L], F32R)
        x1l = sbuf(e1, "x1l", [KC, 2 * L], F32R)
        nrm1 = sbuf(e1, "nrm1", [2, D])
        stage = nrm1[:, :, :].rearrange("p a (b n) -> p (a b) n", n=CB)
        abw = sbuf(e1, "abw", [KC, 4 * H])
        abh = sbuf(e1, "abh", [KC, 4 * H], F32R)
        abl = sbuf(e1, "abl", [KC, 4 * H], F32R)
        abs_ = sbuf(e1, "abs_", [4, 4 * H])
        e1.close()

        late = ExitStack()
        otok = sbuf(late, "otok", [NT, H, P])
        e2 = ExitStack()
        abr = sbuf(e2, "abr", [4, 4 * H])
        dtb = sbuf(e2, "dtb", [2 * H]); alog = sbuf(e2, "alog", [2 * H])
        gt = sbuf(e2, "gt", [6, 4, 2 * H])
        Q = sbuf(e2, "Q", [6, 4, 2, H])
        Qs = sbuf(e2, "Qs", [48, 2])
        gamT = sbuf(e2, "gamT", [4 * P])
        sel = sbuf(e2, "sel", [4, P])
        incl = sbuf(e2, "incl", [2, P])
        edge = sbuf(e2, "edge", [2, P])
        lmask = sbuf(e2, "lmask", [LEVELS, 2, P])
        convw = sbuf(e2, "convw", [3, H * 5])
        cws = sbuf(e2, "cws", [3, 10])
        cbuf = sbuf(e2, "cbuf", [2560])
        ck = cbuf[:, 0:1024].rearrange("p (a n) -> p a n", a=2)
        cv = cbuf[:, 1024:2048].rearrange("p (a n) -> p a n", a=2)
        cq = cbuf[:, 2048:2560].rearrange("p (a n) -> p a n", a=2)
        B = cbuf[:, 0:2048].rearrange("p (s q n) -> p s q n", s=4, q=4)
        qT = sbuf(e2, "qT", [2, L]); kT = sbuf(e2, "kT", [2, 2 * L]); vT = sbuf(e2, "vT", [2, 2 * L])
        ktok = sbuf(e2, "ktok", [2, 4, P]); vtok = sbuf(e2, "vtok", [2, 4, P])
        X = sbuf(e2, "X", [4, 4, P])
        NM = sbuf(e2, "NM", [4, 4, P])
        XT = sbuf(e2, "XT", [4, 4, P])
        PB = sbuf(e2, "PB", [4, 4, P])
        QK = sbuf(e2, "QK", [2, 4, P]); DI = sbuf(e2, "DI", [2, 4, P])
        S = sbuf(e2, "S", [4, P])
        R, VN, VD, EQ = (PB[:, n] for n in range(4))
        e2.close()

        e3 = ExitStack()
        poolT = sbuf(e3, "poolT", [8, L]); osq = sbuf(e3, "osq", [NT, H, P])
        e3.close()
        late.close()
        tail = ExitStack()
        rbuf = sbuf(tail, "rbuf", [NT, CB])
        tmp = sbuf(tail, "tmp", [NT, CB])
        hx = sbuf(tail, "hx", [NT, D])
        xh = sbuf(tail, "xh", [KC, L], F32R)
        xl = sbuf(tail, "xl", [KC, L], F32R)
        b1 = ExitStack()
        zp = sbuf(b1, "zp", [2, NT, H * P])
        zt, pt = zp[:, 0], zp[:, 1]
        onorm = sbuf(b1, "onorm", [P])
        so = sbuf(b1, "so", [NT * H]); ro = sbuf(b1, "ro", [NT * H])
        poolm = sbuf(b1, "poolm", [4, 2, L])
        poolw = sbuf(b1, "poolw", [4, 2, L])
        pscale = sbuf(b1, "pscale", [8])
        b1.close()
        b2 = ExitStack()
        nrm = sbuf(b2, "nrm", [NT, D])
        b2.close()
        b3 = ExitStack()
        hth = sbuf(b3, "hth", [2, SK, L], F32R)
        htl = sbuf(b3, "htl", [2, SK, L], F32R)
        b3.close()
        b4 = ExitStack()
        ug = sbuf(b4, "ug", [NT, D])
        vg = sbuf(b4, "vg", [NT, D])
        lnp = sbuf(b4, "lnp", [2, 2, CB])
        wsT = sbuf(b4, "wsT", [4, P])
        bst = sbuf(b4, "bst", [NT, 4, 6])
        mv = sbuf(b4, "mv", [NT, 2])
        b4.close()
        b5 = ExitStack()
        fin = sbuf(b5, "fin", [NT, D])
        fg = sbuf(b5, "fg", [D])
        b5.close()
        tail.close()

        s_qT, s_kT, s_vT = dram("s_q", [H, P, L]), dram("s_k", [H, P, 2 * L]), dram("s_v", [H, P, 2 * L])
        s_zp = dram("s_zp", [2, NT, P, H * P])

        consts = sem("consts")
        gate_bias = [sem("gate_bias0"), sem("gate_bias1")]
        w_loaded = [sem(f"w_loaded{r}") for r in range(RAW)]
        w_high, w_split, w_used = sem("w_high"), sem("w_split"), sem("w_used")
        a0_used, a0_done, a0_read = sem("a0_used"), sem("a0_done"), sem("a0_read")
        ada_loaded = [sem("ada_loaded0"), sem("ada_loaded1")]
        ada_used, ada_summed = sem("ada_used"), sem("ada_summed")
        sum_done, sum_read = sem("sum_done"), sem("sum_read")
        eps_ready, um_done, umh_ready, uml_ready = sem("eps_ready"), sem("um_done"), sem("umh_ready"), sem("uml_ready")
        ln_loaded2 = [sem("ln_loaded0"), sem("ln_loaded1")]
        csil_ready, cols_ready = sem("csil_ready"), sem("cols_ready")
        h_loaded = [sem("h_loaded0"), sem("h_loaded1")]
        pos_loaded, h_ready = sem("pos_loaded"), sem("h_ready")
        sq_done, rt_done, nrm_ready = sem("sq_done"), sem("rt_done"), sem("nrm_ready")
        xp_done, xh_ready, xt_ready = sem("xp_done"), sem("xh_ready"), sem("xt_ready")
        fm_done, fm_read = sem("fm_done"), sem("fm_read")
        fm_stored = [sem("fm_stored0"), sem("fm_stored1")]
        lin_done = sem("lin_done")
        acc_free = [sem("acc_free0"), sem("acc_free1")]
        zp_stored = [sem("zp_stored0"), sem("zp_stored1")]
        ab_loaded, ab_high, ab_split, ab_done = sem("ab_loaded"), sem("ab_high"), sem("ab_split"), sem("ab_done")
        c2_loaded = sem("c2_loaded")
        act_step, dve_step, pool_step = sem("act_step"), sem("dve_step"), sem("pool_step")
        ab_ready, ex_ready, lx_ready, g_ready = sem("ab_ready"), sem("ex_ready"), sem("lx_ready"), sem("g_ready")
        gam_done, gam_ready, tot_done, q_dve, q_ready = (sem(n) for n in ("gam_done", "gam_ready", "tot_done", "q_dve", "q_ready"))
        gamT_ready = sem("gamT_ready")
        pair_in, pair_free = sem("pair_in"), sem("pair_free")
        conv_done, silu_done, sq_ready2, nsum_done, nroot = (sem(n) for n in ("conv_done", "silu_done", "sq2_ready", "nsum_done", "nroot"))
        kqn, tok_done, tok_read, sel_ready = (sem(n) for n in ("kqn", "tok_done", "tok_read", "sel_ready"))
        kk_done, row_done, dif_ready, dec_ready, di_ready, nm_ready = (
            sem(n) for n in ("kk_done", "row_done", "dif_ready", "dec_ready", "di_ready", "nm_ready"))
        qk_ready = sem("qk_ready")
        b_ready, mm1_done, p_ready, mm2_done, xT_ready, tr_done, x_ready = (
            sem(n) for n in ("b_ready", "mm1_done", "p_ready", "mm2_done", "xT_ready", "tr_done", "x_ready"))
        ks_done, r_ready, y_done, vn_ready, vd_ready, ds_done, s_ready = (
            sem(n) for n in ("ks_done", "r_ready", "y_done", "vn_ready", "vd_ready", "ds_done", "s_ready"))
        qs_done, eq_ready, ov_done, o_ready = (sem(n) for n in ("qs_done", "eq_ready", "ov_done", "o_ready"))
        dn_done = sem("dn_done")
        zp_loaded, e3_loaded, pool_done, poolT_ready, yb_done = (
            sem(n) for n in ("zp_loaded", "e3_loaded", "pool_done", "poolT_ready", "yb_done"))
        osum_ready, oroot, zs_ready, ya_ready, ya_done = (sem(n) for n in ("osum_ready", "oroot", "zs_ready", "ya_ready", "ya_done"))
        yh_ready, y_ready = sem("yh_ready"), sem("y_ready")
        hx_loaded, hx_ready = sem("hx_loaded"), sem("hx_ready")
        tmp_ready, hx_added = sem("tmp_ready"), sem("hx_added")
        relu_ready, sqr_ready, mt_done, hth_ready, ht_ready = (
            sem(n) for n in ("relu_ready", "sqr_ready", "mt_done", "hth_ready", "ht_ready"))
        u_ready, v_ready, mv_ready, lroot, vn_norm, ln_loaded, ws_loaded = (
            sem(n) for n in ("u_ready", "v_ready", "mv_ready", "lroot", "vn_norm", "ln_loaded", "ws_loaded"))
        ln_free, mix_done, um_ready = sem("ln_free"), sem("mix_done"), sem("um_ready")
        fg_loaded, fin_ready, stored = sem("fg_loaded"), sem("fin_ready"), sem("stored")

        block = stack.enter_context(nc.Block())

        AT16 = [7, 7, 8, 8, 9, 9, 10, 10, 11, 11, 12, 13, 13, 14, 15, 15]
        AT32 = [8 + 3 * k // 2 for k in range(16)]
        AT64 = [8 + 3 * k for k in range(16)]
        ADA = [(0, 2), (0, 3), (0, 4), (0, 5), (1, 0), (1, 1), (1, 2), (1, 3), (1, 4), (1, 5)]
        HX = {2: 8, 3: 72, 4: 80, 5: 144}
        COLS = {1: (2, 0), 2: (2, 1), 4: (3, 0), 5: (3, 1), 7: (4, 0), 8: (4, 1)}
        GATES = {0: 0, 3: 1, 6: 0, 9: 1}
        ROUND = [0, 2, 3, 4, 6, 7, 9, 11, 12, 13]

        def load_unit(sp, U, j, src):
            sp.dma_start(raw[:, j % RAW, :].rearrange("p (k n) -> p k n", k=UNIT),
                         src.rearrange("(k p) n -> p k n", p=P)).then_inc(w_loaded[j % RAW], 16)

        def load_ada(sp, a16, k, src, first=False):
            if not (first and k < 2):
                sp.wait_ge(ada_used, a16 + k - 1)
            sp.dma_start(ada_raw[:, k % 2, :], src).then_inc(ada_loaded[k % 2], 16)

        @block.sync
        def _(sp):
            for dst, name in ((ident[:], "ident"), (ones[:], "ones"), (ccol[:, :, :], "ccol"), (adab[:, :, :], "adab"),
                              (gcol[:, :, :], "gcol"), (bscol[:], "bscol")):
                sp.dma_start(dst, A[name]).then_inc(consts, 16)

            def a0(g, k, wait):
                r = k % RAW
                if wait is not None:
                    sp.wait_ge(a0_used, wait)
                sp.dma_start(raw[:, r, :], A["ada_w"][0, k * P:(k + 1) * P, ds(g * 1024, 1024)])\
                  .then_inc(w_loaded[r], 16)

            for k in range(KC):
                a0(0, k, k - 7 if k >= RAW else None)
            with sp.Fori(1, 4) as g:
                for k in range(KC):
                    a0(g, k, g * KC + k - 7)
            for g in range(2):
                layer, part = ADA[3 * g]
                sp.dma_start(gate[:, g, :], A["ada_b"][layer, part * D:(part + 1) * D].partition_broadcast(P))\
                  .then_inc(gate_bias[g], 16)

            U = Units(U_KV)
            w_in = A["ev_w_in"][0]
            for j in range(UPB):
                sp.wait_ge(a0_used, A0_UNITS - 7 + j)
                load_unit(sp, U, j, w_in[j * UNIT * P:(j + 1) * UNIT * P, H * P:H * P + CB])
            with sp.Fori(1, 4) as b:
                U = Units(U_KV, UPB, b)
                for j in range(UPB):
                    sp.wait_ge(w_split, U.u(j, -7))
                    load_unit(sp, U, j, w_in[j * UNIT * P:(j + 1) * UNIT * P, ds(b * CB + H * P, CB)])

            def phase(base, blocks, src, at, M, units=UPB):
                U = Units(base)
                j = 0
                for b in range(blocks):
                    for c in range(units):
                        sp.wait_ge(w_split, U.u(j, -7))
                        load_unit(sp, U, j, src(b, c))
                        for n, a in enumerate(at):
                            for k in range(KC):
                                if a[k] + n * (max(a) // 16 * 16 + 16) == j:
                                    layer, part = ADA[M + n]
                                    load_ada(sp, 16 * (M + n), k,
                                             A["ada_w"][layer, k * P:(k + 1) * P, part * D:(part + 1) * D], M + n == 0)
                        j += 1

            def rows(w, c):
                return w[c * UNIT * P:(c + 1) * UNIT * P]

            sp.wait_ge(h_ready, 2)
            phase(U_Q, 2, lambda b, c: rows(w_in, c)[:, b * CB:(b + 1) * CB], [AT16], 0)
            phase(U_ZP, 4, lambda b, c: rows(w_in, c)[:, ZP0 + b * CB:ZP0 + (b + 1) * CB], [AT16, AT16], 1)
            phase(U_OUT, 4, lambda b, c: rows(A["ev_w_out"][0], c)[:, b * CB:(b + 1) * CB], [AT32], 3)

            def mlp(layer, base, ada):
                w1, w2 = A["mlp_w1"][layer], A["mlp_w2"][layer]

                def up(U, j0, slab, b):
                    for c in range(UPB):
                        j = j0 + 8 * b + c
                        sp.wait_ge(w_split, U.u(j, -7))
                        load_unit(sp, U, j, w1[c * UNIT * P:(c + 1) * UNIT * P, ds(slab * SLAB + b * CB, CB)])
                        yield j

                def down(U, j0, slab, b):
                    for c in range(SK // UNIT):
                        j = j0 + 4 * b + c
                        sp.wait_ge(w_split, U.u(j, -7))
                        load_unit(sp, U, j, w2[ds(slab * SLAB + c * UNIT * P, UNIT * P), b * CB:(b + 1) * CB])
                        yield j

                def turn(U, slab, i, two):
                    for h in range(2):
                        for b in range(2 if (two or h == 0) else 0):
                            yield from up(U, 32 * h, slab + h + 1, b)
                        for b in range(4):
                            yield from down(U, 32 * h + (16 if (two or h == 0) else 0), slab + h, b)

                U = Units(base)
                for b in range(2):
                    for _ in up(U, 0, 0, b):
                        pass
                with sp.Fori(0, 3) as i:
                    for j in turn(Units(base + 16, 64, i), i * 2, i, True):
                        if ada and j in AT64:
                            k = AT64.index(j)
                            load_ada(sp, i * 16 + 64, k,
                                     A["ada_w"][1, k * P:(k + 1) * P, ds(i * D, D)])
                if ada:
                    sp.wait_ge(hx_added, 2 * 4)
                    sp.dma_start(gate[:, 0, :], A["ada_b"][1, 2 * D:3 * D].partition_broadcast(P)).then_inc(gate_bias[0], 16)
                for _ in turn(Units(base + 16 + 192), 6, None, False):
                    pass

            mlp(0, U_MLP0, True)
            phase(U_OIN, 8, lambda b, c: rows(A["od_w_in"][0], c)[:, b * CB:(b + 1) * CB], [AT32, AT32], 7)
            sp.wait_ge(hx_added, 2 * 36)
            sp.dma_start(gate[:, 1, :], A["ada_b"][1, 5 * D:6 * D].partition_broadcast(P)).then_inc(gate_bias[1], 16)
            phase(U_OOUT, 4, lambda b, c: rows(A["od_w_out"][0], c)[:, b * CB:(b + 1) * CB], [AT32], 9)
            mlp(1, U_MLP1, False)
            for t in range(NT):
                sp.wait_ge(fin_ready, t + 1)
                sp.dma_start(out[0, t * P:(t + 1) * P, :], fin[:, t, :]).then_inc(stored, 16)
            sp.wait_ge(stored, 16 * NT)

        @block.scalar
        def _(act):
            step = Chain(act, act_step)
            act.sem_inc(fm_read, 2)

            def high(U, j):
                act.wait_ge(w_loaded[j % RAW], U.r16(j, A0_UNITS // RAW + 1))
                act.wait_ge(w_used, U.u(j, 1))
                act.copy(wh[:, j % SPLIT, :], raw[:, j % RAW, :]).then_inc(w_high, 1)

            def highs(U, *js):
                for j in range(*js):
                    high(U, j)

            for t in range(NT):
                act.dma_start(nrm1[:, t, :], A["x"][0, t * P:(t + 1) * P, :]).then_inc(h_loaded[t], 16)
                act.dma_start(ada_raw[:, t, :], A["pos"][t * P:(t + 1) * P, :]).then_inc(pos_loaded, 16)
            act.dma_start(abw[:, :, :], A["ev_w_in"][0][:, QKV:QKV + 4 * H].rearrange("(k p) n -> p k n", p=P))\
               .then_inc(ab_loaded, 16)
            act.wait_ge(consts, 16 * 6)
            act.activation(csil[:, :, :], ccol[:, :, :], ACT.Silu).then_inc(csil_ready, 1)

            def root(c, t, src):
                col = 2 * c + t
                if c < 2:
                    act.wait_ge(h_loaded[t], 16 * (c + 1))
                    if c == 0:
                        act.wait_ge(h_ready, t + 1)
                act.activation(PS[:, 0:4, :].rearrange("p b n -> p (b n)"), src, ACT.Square,
                               accum_out=ss[:, col:col + 1]).then_inc(sq_done, 1)
                act.wait_ge(sq_done, col + 1)
                act.activation(ss[:, col:col + 1], ss[:, col:col + 1], ACT.Sqrt, bias=eps[:, 0:1], scale=1.0 / D)\
                   .then_inc(rt_done, 1)

            def split_high(c, dst, cols):
                for kp in range(KC // 2):
                    act.wait_ge(xp_done, 8 * c + kp + 1)
                    for h in range(2):
                        k = 2 * kp + h
                        ins = act.activation(dst[:, k, cols], PS[:, 4 + kp % 4, h * L:(h + 1) * L], ACT.Identity,
                                             bias=shc[:, c, k:k + 1], scale=gsc[:, c, k:k + 1])
                    ins.then_inc(xh_ready, 1)

            act.wait_ge(eps_ready, 1)
            for c in range(2):
                for t in range(NT):
                    if c == 1:
                        act.wait_ge(nrm_ready, 2)
                        act.wait_ge(xp_done, 8)
                        act.dma_start(nrm1[:, t, :], A["ctx"][0, t * P:(t + 1) * P, :]).then_inc(h_loaded[t], 16)
                for t in range(NT):
                    root(c, t, nrm1[:, t, :])
                act.wait_ge(cols_ready, 1)
                split_high(c, x1h, slice(c * L, (c + 1) * L))

            def fm_store(f, F, width, dst, hs):
                p = f % 2
                act.wait_ge(fm_done, F(1))
                if not isinstance(F(0), int) or F(0) >= 2:
                    act.wait_ge(fm_stored[p], F(None))
                act.copy(stage[:, 4 * p:4 * p + 4, 0:width], PS[:, 4 * p:4 * p + 4, 0:width]).then_inc(fm_read, 1)
                act.wait_ge(fm_read, F(3))
                act.dma_start(dst[hs, :, :].rearrange("h p n -> p h n"), stage[:, 4 * p:4 * p + 4, 0:width])\
                   .then_inc(fm_stored[p], 16)

            def fm_block(f):
                return lambda off: 16 * (f // 2) if off is None else f + off

            stores = [(2 * L, s_kT, 0), (2 * L, s_kT, 4), (2 * L, s_vT, 0), (2 * L, s_vT, 4), (L, s_qT, 0), (L, s_qT, 4)]
            U = Units(U_KV)
            highs(U, 4)
            for f in range(6):
                width, dst, h0 = stores[f]
                highs(U, 8 * f + 4, 8 * f + 12)
                fm_store(f, fm_block(f), width, dst, slice(h0, h0 + 4))

            act.wait_ge(ab_loaded, 16)
            act.copy(abh[:, :, :], abw[:, :, :]).then_inc(ab_high, 1)
            U = Units(U_ZP)
            act.wait_ge(fm_stored[0], 48)
            act.wait_ge(fm_stored[1], 48)
            for n in range(4):
                highs(U, 8 * n + 4, min(8 * n + 12, 32))
                act.wait_ge(lin_done, n + 1)
                if n >= 2:
                    act.wait_ge(zp_stored[n % 2], 16)
                q = 4 * (n % 2)
                for t in range(NT):
                    act.copy(stage[:, q + t, :], PS[:, 2 * (n % 2) + t, :]).then_inc(acc_free[n % 2], 1)
                act.wait_ge(acc_free[n % 2], 2 * (n // 2) + 2)
                act.dma_start(s_zp[n // 2, :, :, (n % 2) * CB:(n % 2 + 1) * CB].rearrange("t p n -> p t n"),
                              stage[:, q:q + NT, :]).then_inc(zp_stored[n % 2], 16)

            act.wait_ge(ab_done, 1)
            act.wait_ge(zp_stored[0], 32)
            act.wait_ge(zp_stored[1], 32)
            for dst, name in ((incl[:, :, :], "incl"), (edge[:, :, :], "edge"), (lmask[:, :, :, :], "lmask"), (convw[:, :, :], "convw")):
                act.dma_start(dst, A[name]).then_inc(c2_loaded, 16)
            for dst, name in ((dtb[:], "ev_dt_bias"), (alog[:], "ev_a_log")):
                act.dma_start(dst, A[name].rearrange("o d h -> (o d h)").partition_broadcast(P)).then_inc(c2_loaded, 16)
            act.copy(abr[:, :, :], PS[:, 4, 0:4 * 4 * H].rearrange("p (t n) -> p t n", t=4)).then_inc(ab_ready, 1)
            act.wait_ge(ab_ready, 1)
            act.wait_ge(c2_loaded, 16 * 6)
            act.activation(Q[:, 1, :, :, :].rearrange("p t d h -> p t (d h)"), abr[:, :, 2 * H:4 * H], ACT.Sigmoid)
            step(act.activation(alog[:], alog[:], ACT.Exp))
            act.wait_ge(ex_ready, 1)
            act.activation(gt[:, 1], gt[:, 1], ACT.Exp).then_inc(lx_ready, 1)
            act.wait_ge(q_dve, 1)
            act.activation(Q[:, 5, :, :, :].rearrange("p t d h -> p (t d h)"), Q[:, 0, :, :, :].rearrange("p t d h -> p (t d h)"), ACT.Exp)
            act.activation(gt[:, 2], gt[:, 2], ACT.Exp)
            act.activation(Q[:, 4, :, :, :].rearrange("p t d h -> p (t d h)"), gt[:, 3].rearrange("p t n -> p (t n)"), ACT.Exp)\
               .then_inc(q_ready, 1)
            act.wait_ge(gam_done, 3)
            act.copy(gamT[0:16, :], PS[0:16, 6, :]).then_inc(gamT_ready, 1)

            with act.Fori(0, H // 2) as i:
                act.wait_ge(pair_free, i * 4 + 4)
                for dst, src in ((kT, s_kT), (vT, s_vT), (qT, s_qT)):
                    act.dma_start(dst[:, :, :], src[ds(i * 2, 2), :, :].rearrange("h p n -> p h n")).then_inc(pair_in, 16)
                for n, (dst, src) in enumerate(((kT, ck), (qT, cq), (vT, cv))):
                    act.wait_ge(conv_done, i * 3 + n + 1)
                    act.activation(dst[:, :, :], src, ACT.Silu).then_inc(silu_done, 1)
                for n, (dst, src) in enumerate(((ck, PS[:, 0:2, :]), (cq, PS[:, 2, :].rearrange("p (a n) -> p a n", a=2)))):
                    act.wait_ge(nsum_done, i * 2 + n + 1)
                    act.activation(dst, src, ACT.Sqrt, bias=eps[:, 0:1]).then_inc(nroot, 1)
                act.wait_ge(tok_done, i * 2 + 1)
                act.copy(vtok[:, :, :, :].rearrange("p a t n -> p a (t n)"), PS[:, 6:8, :]).then_inc(tok_read, 1)
                act.wait_ge(tok_done, i * 2 + 2)
                act.copy(ktok[:, :, :, :].rearrange("p a t n -> p a (t n)"), PS[:, 4:6, :]).then_inc(tok_read, 1)
                act.wait_ge(dif_ready, i + 1)
                act.activation(X[:, :, :, :].rearrange("p s q n -> p (s q n)"), X[:, :, :, :].rearrange("p s q n -> p (s q n)"), ACT.Exp)\
                   .then_inc(dec_ready, 1)

                def take_x(lv, s):
                    act.wait_ge(tr_done, i * 24 + 4 * lv + s + 1)
                    act.copy(X[:, s], PS[:, s, :].rearrange("p (q n) -> p q n", q=4)).then_inc(x_ready, 1)

                for s in range(4):
                    take_x(0, s)
                for lv in range(1, LEVELS):
                    for s in range(4):
                        act.wait_ge(mm1_done, i * 24 + 4 * (lv - 1) + s + 1)
                        act.copy(PB[:, s], PS[:, s, :].rearrange("p (q n) -> p q n", q=4)).then_inc(p_ready, 1)
                    if lv < LEVELS - 1:
                        for s in range(4):
                            take_x(lv, s)
                for s in range(4):
                    act.wait_ge(vd_ready, i * 4 + s + 1)
                    for q in range(4):
                        t = TILE[q // 2][s]
                        ins = act.activation(VN[:, q], PS[:, 2, q * P:(q + 1) * P], ACT.Copy, scale=Qs[:, 8 + 2 * t + q // 2, q % 2:q % 2 + 1])
                    ins.then_inc(vn_ready, 1)
                    if s >= 2:
                        act.wait_ge(qs_done, i * 2 + s - 1)
                        if s == 3:
                            act.wait_ge(o_ready, i * 2 + 1)
                        for q in range(4):
                            t = TILE[q // 2][s]
                            ins = act.activation(EQ[:, q], PS[:, 1, q * P:(q + 1) * P], ACT.Copy,
                                                 scale=Qs[:, 40 + 2 * t + q // 2, q % 2:q % 2 + 1])
                        ins.then_inc(eq_ready, 1)
                act.wait_ge(vn_ready, i * 4 + 4)
                act.wait_ge(eq_ready, i * 2 + 2)
                act.sem_inc(pair_free, 1)

            act.wait_ge(dn_done, 1)
            act.dma_start(zp[:, :, :, :].rearrange("p s t n -> p (s t) n"), s_zp.rearrange("s t p n -> p (s t) n")).then_inc(e3_loaded, 16)
            for dst, name in ((poolm[:, :, :, :], "poolm"), (poolw[:, :, :, :], "poolw"), (pscale[:], "pscale")):
                act.dma_start(dst, A[name]).then_inc(e3_loaded, 16)
            act.dma_start(onorm[:], A["ev_onorm_g"].rearrange("o n -> (o n)").partition_broadcast(P)).then_inc(e3_loaded, 16)
            act.wait_ge(osum_ready, 1)
            act.activation(ro[:], so[:], ACT.Sqrt, bias=eps[:, 0:1], scale=1.0 / P).then_inc(oroot, 1)
            act.wait_ge(e3_loaded, 16 * 5)
            act.activation(zt, zt, ACT.Silu).then_inc(zs_ready, 1)
            act.wait_ge(pool_done, 1)
            act.copy(poolT[:, :, :].rearrange("p c n -> p (c n)"), PS[:, 0:4, :].rearrange("p b n -> p (b n)")).then_inc(poolT_ready, 1)
            act.wait_ge(yb_done, 1)
            for c in range(8):
                act.activation(xh[:, 8 + c, :], PS[:, 4 + c // 2, (c % 2) * L:(c % 2 + 1) * L], ACT.Copy,
                               scale=pscale[:, c:c + 1]).then_inc(yh_ready, 1)
            act.wait_ge(ya_done, 1)
            for c in range(8):
                act.copy(xh[:, c, :], PS[:, c // 2, (c % 2) * L:(c % 2 + 1) * L]).then_inc(yh_ready, 1)
            act.wait_ge(y_ready, 16)
            for t in range(NT):
                act.dma_start(hx[:, t, :], A["x"][0, t * P:(t + 1) * P, :]).then_inc(hx_loaded, 16)
                act.dma_start(zp[:, t, :, :].rearrange("p a n -> p (a n)"), A["pos"][t * P:(t + 1) * P, :]).then_inc(hx_loaded, 16)

            highs(Units(U_OUT), 0, 32)

            def normalise(c):
                act.wait_ge(hx_added, HX[c])
                for t in range(NT):
                    root(c, t, hx[:, t, :])
                act.wait_ge(cols_ready, c)
                split_high(c, xh, slice(0, L))

            def relus(T, layer, tau, n):
                act.wait_ge(lin_done, T(n, 1))
                first = tau == 0 and T.i is None and layer == 0
                if not first:
                    act.wait_ge(mt_done, T.tau(tau, 0))
                for t in range(NT):
                    act.activation(rbuf[:, t, :], PS[:, 2 * (n % 2) + t, :], ACT.Relu).then_inc(relu_ready, 1)

            def mids(T, tau, buf):
                for t in range(NT):
                    act.wait_ge(mt_done, T.tau(tau, 1 + t))
                    act.copy(hth[:, buf, 4 * (tau % 2):4 * (tau % 2) + 4, t * P:(t + 1) * P],
                             PS[:, 4 + t, :].rearrange("p (c n) -> p c n", c=4)).then_inc(hth_ready, 1)

            def mlp(layer, base, n0):
                U, T = Units(base), Turn(n0, layer)
                highs(U, 0, 12)
                relus(T, layer, 0, 0)
                highs(U, 12, 16)
                U = Units(base + 16)
                highs(U, 0, 2)
                mids(T, 0, 0)
                highs(U, 2, 4)
                relus(T, layer, 1, 1)
                highs(U, 4, 8)
                mids(T, 1, 0)

                def pair(U, T, j0, tau, n, buf):
                    highs(U, j0, j0 + 12)
                    relus(T, layer, tau, n)
                    highs(U, j0 + 12, j0 + 18)
                    mids(T, tau, buf)
                    highs(U, j0 + 18, j0 + 20)
                    relus(T, layer, tau + 1, n + 1)
                    highs(U, j0 + 20, j0 + 26)
                    mids(T, tau + 1, buf)
                    highs(U, j0 + 26, j0 + 32)

                with act.Fori(0, 3) as i:
                    U, T = Units(base + 16, 64, i), Turn(n0 + 2, layer, i)
                    highs(U, 8, 12)
                    relus(T, layer, 2, 0)
                    highs(U, 12, 18)
                    mids(T, 2, 1)
                    highs(U, 18, 20)
                    relus(T, layer, 3, 1)
                    highs(U, 20, 26)
                    mids(T, 3, 1)
                    highs(U, 26, 32)
                    pair(U, T, 32, 4, 6, 0)
                    highs(U, 64, 72)
                U, T = Units(base + 16 + 192), Turn(n0 + 2, layer, 3)
                highs(U, 8, 12)
                relus(T, layer, 2, 0)
                highs(U, 12, 18)
                mids(T, 2, 1)
                highs(U, 18, 20)
                relus(T, layer, 3, 1)
                highs(U, 20, 26)
                mids(T, 3, 1)
                highs(U, 26, 48)

            normalise(2)
            mlp(0, U_MLP0, N_MLP0)
            normalise(3)

            U = Units(U_OIN)
            act.dma_start(wsT[:, :, :], A["wsT"]).then_inc(ws_loaded, 16)
            highs(U, 0, 4)
            for n in range(8):
                highs(U, 8 * n + 4, min(8 * n + 12, 64))
                act.wait_ge(lin_done, N_OIN + n + 1)
                if n == 0:
                    act.wait_ge(xp_done, 32)
                dst = (ug, vg)[n // 4]
                for t in range(NT):
                    act.activation(dst[:, t, (n % 4) * CB:(n % 4 + 1) * CB], PS[:, 2 * (n % 2) + t, :], ACT.Gelu)\
                       .then_inc(acc_free[n % 2], 1)
                act.wait_ge(acc_free[n % 2], 2 * ((N_OIN + n) // 2) + 2)
                if n >= 4:
                    act.sem_inc(v_ready, 1)
            act.wait_ge(mv_ready, 1)
            act.activation(mv[:, :, 1:2].rearrange("p t o -> p (t o)"), mv[:, :, 1:2].rearrange("p t o -> p (t o)"), ACT.Sqrt,
                           bias=eps[:, 0:1]).then_inc(lroot, 1)
            for g in range(4):
                if g >= 2:
                    act.wait_ge(vn_norm, g - 1)
                for n, name in enumerate(("od_ln_g", "od_ln_b")):
                    act.dma_start(lnp[:, g % 2, n, :], A[name][0, g * CB:(g + 1) * CB].partition_broadcast(P)).then_inc(ln_loaded2[g % 2], 16)
            for kp in range(8):
                act.wait_ge(um_done, kp + 1)
                act.copy(xh[:, 2 * kp:2 * kp + 2, :].rearrange("p k n -> p (k n)"), PS[:, 4 + kp % 4, :]).then_inc(umh_ready, 1)
            highs(Units(U_OOUT), 0, 32)
            normalise(4)
            mlp(1, U_MLP1, N_MLP1)
            act.wait_ge(hx_added, HX[5])
            act.dma_start(fg[:], A["final_g"].partition_broadcast(P)).then_inc(fg_loaded, 16)
            for t in range(NT):
                root(5, t, hx[:, t, :])

        def flat(ap):
            return ap.rearrange("p a b -> p (a b)")

        @block.gpsimd
        def _(pool):
            step = Chain(pool, pool_step)
            pool.memset(eps[:], EPS).then_inc(eps_ready, 1)
            pool.sem_inc(pair_free, 4)

            with pool.Fori(0, H // 2) as i:
                for n, (dst, src) in enumerate(((ck, kT), (cq, qT))):
                    pool.wait_ge(silu_done, i * 3 + n + 1)
                    pool.tensor_tensor(dst, src[:, :, :], src[:, :, :], ALU.mult).then_inc(sq_ready2, 1)
                pool.wait_ge(dec_ready, i + 1)
                for s in range(2):
                    ins = pool.tensor_tensor(DI[:, s].rearrange("p (d a) n -> p d a n", d=2),
                                             X[:, 2 + s].rearrange("p (d a) n -> p d a n", d=2),
                                             incl[:, :, :].unsqueeze(2).broadcast_to([P, 2, 2, P]), ALU.mult)
                ins.then_inc(di_ready, 1)
                for lv in range(1, LEVELS):
                    for s in range(4):
                        pool.wait_ge(nm_ready, i * 4 + s + 1)
                        if lv > 1:
                            pool.wait_ge(mm1_done, i * 24 + 4 * (lv - 2) + s + 1)
                        pool.tensor_tensor(B[:, s].rearrange("p (d a) n -> p d a n", d=2),
                                           NM[:, s].rearrange("p (d a) n -> p d a n", d=2),
                                           lmask[:, lv].unsqueeze(2).broadcast_to([P, 2, 2, P]), ALU.mult).then_inc(b_ready, 1)
                pool.wait_ge(b_ready, i * 24 + 24)
                pool.sem_inc(pair_free, 1)

            for t in range(NT):
                pool.wait_ge(hx_loaded, 64)
                pool.tensor_tensor(hx[:, t, :], hx[:, t, :], zp[:, t].rearrange("p a n -> p (a n)"), ALU.add).then_inc(hx_ready, 1)
            pool.wait_ge(hx_ready, 2)

            def add(e_count, cols, n):
                for t in range(NT):
                    pool.wait_ge(tmp_ready, e_count(1 + t))
                    pool.sem_inc(acc_free[n % 2], 1)
                    pool.tensor_tensor(hx[:, t, cols], hx[:, t, cols], tmp[:, t, :], ALU.add).then_inc(hx_added, 1)

            def square(T, tau, n):
                for t in range(NT):
                    pool.wait_ge(relu_ready, T.tau(tau, 1 + t))
                    pool.sem_inc(acc_free[n % 2], 1)
                    pool.tensor_tensor(rbuf[:, t, :], rbuf[:, t, :], rbuf[:, t, :], ALU.mult).then_inc(sqr_ready, 1)

            for b in range(4):
                add(lambda off: 2 * b + off, slice(b * CB, (b + 1) * CB), N_OUT + b)

            def mlp(layer):
                def downs(T, e, which):
                    for b in which:
                        add(lambda off: T.e(e + b, off), slice(b * CB, (b + 1) * CB), b)

                T = Turn(0, layer)
                square(T, 0, 0)
                square(T, 1, 1)
                with pool.Fori(0, 3) as i:
                    T = Turn(0, layer, i)
                    for h in range(2):
                        square(T, 2 + 2 * h, 0)
                        square(T, 3 + 2 * h, 1)
                        downs(T, 4 * h, range(4))
                T = Turn(0, layer, 3)
                square(T, 2, 0)
                square(T, 3, 1)
                downs(T, 0, range(4))
                downs(T, 4, range(4))

            mlp(0)
            for b in range(4):
                add(lambda off: 72 + 2 * b + off, slice(b * CB, (b + 1) * CB), N_OOUT + b)
            mlp(1)

        @block.vector
        def _(dve):
            step = Chain(dve, dve_step)

            def split(U, *js):
                for j in range(*js):
                    dve.wait_ge(w_high, U.u(j, 1))
                    dve.tensor_tensor(wl[:, j % SPLIT, :], raw[:, j % RAW, :], wh[:, j % SPLIT, :].bitcast(F32), ALU.subtract)\
                       .then_inc(w_split, 1)

            def ada(M, k, first=False):
                dve.wait_ge(ada_loaded[k % 2], M * 128 + 16 * (k // 2 + 1))
                if k == 0:
                    if not first:
                        dve.wait_ge(ada_summed, M)
                        dve.wait_ge(ada_used, M * KC)
                    dve.tensor_scalar(ada_acc[:], ada_raw[:, 0, :], csil[:, 0, 0:1], None, ALU.mult).then_inc(ada_used, 1)
                else:
                    dve.wait_ge(ada_used, M * KC + k)
                    dve.scalar_tensor_tensor(ada_acc[:], ada_raw[:, k % 2, :], csil[:, k, 0:1], ada_acc[:], ALU.mult, ALU.add)\
                       .then_inc(ada_used, 1)

            def sum_gate(M, half):
                dve.wait_ge(sum_done, ROUND[M] + half + 1)
                if half == 0:
                    dve.wait_ge(gate_bias[GATES[M]], 16 if M < 6 else 32)
                g = gate[:, GATES[M], half * 1024:(half + 1) * 1024]
                step(dve.tensor_tensor(g, flat(PS[:, 6:8, :]), g, ALU.add))
                dve.sem_inc(sum_read, 1)

            def cols(c, scale, src):
                dst = gsc if scale else shc
                part = (0 if c < 2 or c == 3 else 3) + scale
                layer = 0 if c < 3 else 1
                step(dve.tensor_tensor(dst[:, c, :], src, adab[:, 6 * layer + part, :], ALU.add))
                if scale:
                    step(dve.scalar_tensor_tensor(dst[:, c, :], dst[:, c, :], 1.0, gcol[:, max(c - 1, 0), :], ALU.add, ALU.mult))

            def sum_cols(M):
                c, scale = COLS[M]
                dve.wait_ge(sum_done, ROUND[M] + 1)
                cols(c, scale, PS[:, 6, 0:KC])
                dve.sem_inc(sum_read, 1)
                if scale:
                    dve.sem_inc(cols_ready, 1)

            def sums(M, U, j0):
                split(U, j0, j0 + 5)
                sum_gate(M, 0) if M in GATES else sum_cols(M)
                split(U, j0 + 5, j0 + 7)
                if M in GATES:
                    sum_gate(M, 1)

            for t in range(NT):
                dve.wait_ge(h_loaded[t], 16)
                dve.wait_ge(pos_loaded, 32)
                dve.tensor_tensor(nrm1[:, t, :], nrm1[:, t, :], ada_raw[:, t, :], ALU.add).then_inc(h_ready, 1)

            def normalise(c, src, dst):
                for t in range(NT):
                    col = 2 * c + t
                    dve.wait_ge(rt_done, col + 1)
                    step(dve.reciprocal(rs[:, col:col + 1], ss[:, col:col + 1]))
                    dve.tensor_scalar(dst[:, t, :], src[:, t, :], rs[:, col:col + 1], None, ALU.mult).then_inc(nrm_ready, 1)

            def split_low(c, high, dst, cols):
                for kp in range(KC // 2):
                    dve.wait_ge(xh_ready, 8 * c + kp + 1)
                    for h in range(2):
                        k = 2 * kp + h
                        ins = dve.tensor_scalar(spl[:, h * L:(h + 1) * L], PS[:, 4 + kp % 4, h * L:(h + 1) * L],
                                                gsc[:, c, k:k + 1], shc[:, c, k:k + 1], ALU.mult, ALU.add)
                    step(ins)
                    dve.tensor_tensor(dst[:, 2 * kp:2 * kp + 2, cols], spl[:].rearrange("p (k n) -> p k n", k=2),
                                      high[:, 2 * kp:2 * kp + 2, cols].bitcast(F32), ALU.subtract).then_inc(xt_ready, 1)
                    dve.wait_ge(xt_ready, 8 * c + kp + 1)

            dve.wait_ge(consts, 16 * 6)
            dve.wait_ge(csil_ready, 1)
            normalise(0, nrm1, nrm1)
            for g in range(4):
                dve.wait_ge(a0_done, g + 1)
                step(dve.tensor_copy(mod0[:, 8 * g:8 * g + 8, :], PS[:, 6 + g % 2, 0:16].rearrange("p (j c) -> p j c", c=2)))
                dve.sem_inc(a0_read, 1)
            for c in range(2):
                cols(c, 0, mod0[:, 0:KC, c])
                cols(c, 1, mod0[:, KC:2 * KC, c])
            dve.sem_inc(cols_ready, 1)
            split_low(0, x1h, x1l, slice(0, L))
            normalise(1, nrm1, nrm1)
            split_low(1, x1h, x1l, slice(L, 2 * L))

            split(Units(U_KV), 0, 32)

            def adas(at, j, M):
                for k in range(KC):
                    if at[k] == j:
                        ada(M, k, M == 0)

            def group(U, length, at, M, before=None, first=0):
                if before is None:
                    split(U, first, first + 7)
                else:
                    sums(before, U, first)
                for j in range(7, length):
                    split(U, first + j, first + j + 1)
                    adas(at, j, M)

            dve.wait_ge(h_ready, 2)
            group(Units(U_Q), 16, AT16, 0)
            dve.wait_ge(ab_high, 1)
            dve.tensor_tensor(abl[:, :, :], abw[:, :, :], abh[:, :, :].bitcast(F32), ALU.subtract).then_inc(ab_split, 1)
            group(Units(U_ZP), 16, AT16, 1, 0)
            group(Units(U_ZP), 16, AT16, 2, 1, 16)

            def flat4(ap):
                return ap.rearrange("p t n -> p (t n)")
            dve.wait_ge(ab_ready, 1)
            dve.wait_ge(c2_loaded, 16 * 6)
            step(dve.tensor_tensor(gt[:, 0], abr[:, :, 0:2 * H], dtb[:].unsqueeze(1).broadcast_to([P, 4, 2 * H]), ALU.add))
            step(dve.tensor_scalar(gt[:, 1], gt[:, 0], -1.0, None, ALU.mult))
            dve.tensor_tensor(gt[:, 1], gt[:, 1], gt[:, 0], ALU.min).then_inc(ex_ready, 1)
            dve.wait_ge(lx_ready, 1)
            step(dve.tensor_scalar(gt[:, 2], gt[:, 1], 2.0, None, ALU.add))
            step(dve.reciprocal(gt[:, 2], gt[:, 2]))
            step(dve.tensor_tensor(gt[:, 2], gt[:, 2], gt[:, 1], ALU.mult))
            step(dve.tensor_tensor(gt[:, 3], gt[:, 2], gt[:, 2], ALU.mult))
            step(dve.tensor_scalar(gt[:, 4], gt[:, 3], 1.0 / 17, None, ALU.mult))
            for odd in (15, 13, 11, 9, 7, 5, 3):
                step(dve.scalar_tensor_tensor(gt[:, 4], gt[:, 4], 1.0 / odd, gt[:, 3], ALU.add, ALU.mult))
            step(dve.scalar_tensor_tensor(gt[:, 4], gt[:, 4], 1.0, gt[:, 2], ALU.add, ALU.mult))
            step(dve.tensor_scalar(gt[:, 0], gt[:, 0], 0.0, None, ALU.max))
            step(dve.scalar_tensor_tensor(gt[:, 4], gt[:, 4], 2.0, gt[:, 0], ALU.mult, ALU.add))
            dve.scalar_tensor_tensor(gt[:, 5], gt[:, 4], -1.0, alog[:].unsqueeze(1).broadcast_to([P, 4, 2 * H]), ALU.mult, ALU.mult)\
               .then_inc(g_ready, 1)
            dve.wait_ge(gam_done, 1)
            q0 = Q[:, 0].rearrange("p t d h -> p t (d h)")
            dve.tensor_copy(q0, PS[:, 5, 0:64].rearrange("p (t n) -> p t n", t=4)).then_inc(gam_ready, 1)
            dve.wait_ge(gam_done, 2)
            dve.wait_ge(gam_ready, 1)
            step(dve.tensor_copy(gt[:, 3], PS[:, 7, 0:64].rearrange("p (t n) -> p t n", t=4)))
            step(dve.tensor_tensor(gt[:, 2], gt[:, 3], q0, ALU.subtract))
            dve.tensor_scalar(gt[:, 2], gt[:, 2], 0.0, None, ALU.min).then_inc(q_dve, 1)
            dve.wait_ge(q_ready, 1)
            step(dve.tensor_scalar(Q[:, 2], Q[:, 5], -1.0, None, ALU.mult))
            step(dve.tensor_tensor(Q[:, 3].rearrange("p t d h -> p t (d h)"), Q[:, 1].rearrange("p t d h -> p t (d h)"), gt[:, 2], ALU.mult))

            with dve.Fori(0, H // 2) as i:
                step.enter(i, 21)
                dve.wait_ge(pair_free, i * 4 + 4)
                step(dve.tensor_copy(cws[:, :, :], convw[:, :, ds(i * 10, 10)]))
                step(dve.tensor_copy(Qs[:, :, :], Q[:, :, :, :, :].rearrange("p q t d h -> p (q t d) h")[:, :, ds(i * 2, 2)]))
                for d in range(2):
                    ins = dve.tensor_copy(sel[0:16, 2 * d:2 * d + 2, :],
                                          ident[0:16, ds(i * 2 + 8 * d, 2)].unsqueeze(2).broadcast_to([16, 2, P]))
                ins.then_inc(sel_ready, 1)
                for src, dst, kind, width in ((kT, ck, 1, 2 * L), (qT, cq, 0, L), (vT, cv, 2, 2 * L)):
                    dve.wait_ge(pair_in, i * 48 + 48)
                    for n, tap in enumerate((2, 0, 1, 3, 4)):
                        for a in range(2):
                            w = cws[:, kind, 5 * a + tap:5 * a + tap + 1]
                            s3 = src[:, a, :].rearrange("p (s n) -> p s n", n=L)
                            d3 = dst[:, a, :].rearrange("p (s n) -> p s n", n=L)
                            off = tap - 2
                            lo, hi = max(0, -off), L - max(0, off)
                            if n == 0:
                                ins = dve.tensor_scalar(d3, s3, w, None, ALU.mult)
                            else:
                                ins = dve.scalar_tensor_tensor(d3[:, :, lo:hi], s3[:, :, lo + off:hi + off], w, d3[:, :, lo:hi],
                                                               ALU.mult, ALU.add)
                        if n < 4:
                            step(ins)
                        else:
                            ins.then_inc(conv_done, 1)
                dve.wait_ge(nroot, i * 2 + 1)
                step(dve.reciprocal(ck, ck))
                dve.tensor_tensor(kT[:, :, :], kT[:, :, :], ck, ALU.mult).then_inc(kqn, 1)
                dve.wait_ge(nroot, i * 2 + 2)
                step(dve.reciprocal(cq, cq))
                dve.scalar_tensor_tensor(qT[:, :, :], qT[:, :, :], float(P) ** -0.5, cq, ALU.mult, ALU.mult).then_inc(kqn, 1)
                dve.wait_ge(row_done, i + 1)
                for s in range(4):
                    for q in range(4):
                        t = TILE[q // 2][s]
                        ins = dve.tensor_scalar(X[:, s, q, :], PS[:, 4 + q, t * P:(t + 1) * P],
                                                Qs[:, 2 * t + q // 2, q % 2:q % 2 + 1], 0.0, ALU.subtract, ALU.min)
                ins.then_inc(dif_ready, 1)
                dve.wait_ge(dec_ready, i + 1)
                dve.wait_ge(kk_done, i + 1)
                for s in range(4):
                    for q in range(4):
                        t = TILE[q // 2][s]
                        ins = dve.scalar_tensor_tensor(NM[:, s, q, :], X[:, s, q, :], Qs[:, 8 + 2 * t + q // 2, q % 2:q % 2 + 1],
                                                       PS[:, q % 2, t * P:(t + 1) * P], ALU.mult, ALU.mult)
                    ins.then_inc(nm_ready, 1)
                dve.wait_ge(di_ready, i + 1)
                for s in range(2):
                    for d in range(2):
                        t = TILE[d][2 + s]
                        ins = dve.tensor_tensor(QK[:, s, 2 * d:2 * d + 2, :], DI[:, s, 2 * d:2 * d + 2, :],
                                                PS[:, 2, :].rearrange("p (a t n) -> p a t n", a=2, t=2)[:, :, t, :], ALU.mult)
                ins.then_inc(qk_ready, 1)
                dve.wait_ge(nm_ready, i * 4 + 4)
                for s in range(4):
                    step(dve.tensor_tensor(XT[:, s].rearrange("p (d a) n -> p d a n", d=2),
                                           NM[:, s].rearrange("p (d a) n -> p d a n", d=2),
                                           lmask[:, 0].unsqueeze(2).broadcast_to([P, 2, 2, P]), ALU.mult))
                    dve.scalar_tensor_tensor(XT[:, s], XT[:, s], -1.0, ident[:].unsqueeze(1).broadcast_to([P, 4, P]), ALU.mult, ALU.add)\
                       .then_inc(xT_ready, 1)
                dve.memset(S[:, :, :], 0.0).then_inc(s_ready, 1)
                for lv in range(1, LEVELS):
                    for s in range(4):
                        dve.wait_ge(mm2_done, i * 24 + 4 * (lv - 1) + s + 1)
                        dve.tensor_tensor(XT[:, s], XT[:, s], PS[:, 4 + s, :].rearrange("p (q n) -> p q n", q=4), ALU.subtract)\
                           .then_inc(xT_ready, 1)
                for s in range(4):
                    dve.wait_ge(ks_done, i * 4 + s + 1)
                    for q in range(4):
                        t = TILE[q // 2][s]
                        ins = dve.scalar_tensor_tensor(R[:, q], PS[:, 0, q * P:(q + 1) * P], Qs[:, 16 + 2 * t + q // 2, q % 2:q % 2 + 1],
                                                       vtok[:, q % 2, t, :], ALU.mult, ALU.add)
                    ins.then_inc(r_ready, 1)
                    dve.wait_ge(y_done, i * 4 + s + 1)
                    for q in range(4):
                        t = TILE[q // 2][s]
                        ins = dve.tensor_scalar(VD[:, q], PS[:, 2, q * P:(q + 1) * P], Qs[:, 24 + 2 * t + q // 2, q % 2:q % 2 + 1],
                                                None, ALU.mult)
                    ins.then_inc(vd_ready, 1)
                    dve.wait_ge(ds_done, i * 4 + s + 1)
                    dve.wait_ge(s_ready, i * 5 + s + 1)
                    for q in range(4):
                        t = TILE[q // 2][s]
                        ins = dve.scalar_tensor_tensor(S[:, q], S[:, q], Qs[:, 32 + 2 * t + q // 2, q % 2:q % 2 + 1],
                                                       PS[:, 4, q * P:(q + 1) * P], ALU.mult, ALU.add)
                    ins.then_inc(s_ready, 1)
                    if s >= 2:
                        dve.wait_ge(eq_ready, i * 2 + s - 1)
                        dve.wait_ge(ov_done, i * 2 + s - 1)
                        ov = PS[:, 3, :].rearrange("p (q n) -> p q n", q=4)
                        if s == 2:
                            for d in range(2):
                                ins = dve.tensor_tensor(otok[:, TILE[d][s], ds(i * 2, 2), :], EQ[:, 2 * d:2 * d + 2], ov[:, 2 * d:2 * d + 2], ALU.add)
                            ins.then_inc(o_ready, 1)
                        else:
                            step(dve.tensor_tensor(EQ, EQ, ov, ALU.add))
                            dve.wait_ge(o_ready, i * 2 + 1)
                            for d in range(2):
                                o = otok[:, TILE[d][s], ds(i * 2, 2), :]
                                ins = dve.tensor_tensor(o, o, EQ[:, 2 * d:2 * d + 2], ALU.add)
                            ins.then_inc(o_ready, 1)
                dve.wait_ge(o_ready, i * 2 + 2)
                dve.wait_ge(s_ready, i * 5 + 5)
                dve.sem_inc(pair_free, 1)
                step.leave(H // 2)
            dve.wait_ge(pair_free, 20)
            dve.sem_inc(dn_done, 1)

            o2 = otok[:, :, :, :].rearrange("p t h n -> p (t h) n")
            s2 = osq[:, :, :, :].rearrange("p t h n -> p (t h) n")
            step(dve.tensor_tensor(s2, o2, o2, ALU.mult))
            dve.tensor_reduce(so[:], s2, AX.X, ALU.add).then_inc(osum_ready, 1)
            dve.wait_ge(oroot, 1)
            step(dve.reciprocal(ro[:], ro[:]))
            step(dve.tensor_tensor(o2, o2, ro[:].unsqueeze(2).broadcast_to([P, NT * H, P]), ALU.mult))
            dve.wait_ge(e3_loaded, 16 * 5)
            step(dve.tensor_tensor(o2, o2, onorm[:].unsqueeze(1).broadcast_to([P, NT * H, P]), ALU.mult))
            dve.wait_ge(zs_ready, 1)
            dve.tensor_tensor(o2, o2, zt.rearrange("p t (h n) -> p (t h) n", h=H), ALU.mult).then_inc(ya_ready, 1)

            def y_low(c, n, bank, scale):
                dve.wait_ge(yh_ready, n // 2 * 2 + 2)
                src = PS[:, bank + (c % 8) // 2, (c % 2) * L:(c % 2 + 1) * L]
                if scale:
                    step(dve.tensor_scalar(spl[:, 0:L], src, pscale[:, c - 8:c - 7], None, ALU.mult))
                    src = spl[:, 0:L]
                dve.tensor_tensor(xl[:, c, :], src, xh[:, c, :].bitcast(F32), ALU.subtract).then_inc(y_ready, 1)
                dve.wait_ge(y_ready, n + 1)

            for c in range(8):
                y_low(8 + c, c, 4, True)
            for c in range(8):
                y_low(c, 8 + c, 0, False)

            def gated(e_count, done, n, g, b):
                dve.wait_ge(lin_done, done)
                for t in range(NT):
                    w = e_count(t - 1)
                    if not isinstance(w, int) or w >= 1:
                        dve.wait_ge(hx_added, w)
                    dve.tensor_tensor(tmp[:, t, :], PS[:, 2 * (n % 2) + t, :], gate[:, g, b * CB:(b + 1) * CB], ALU.mult)\
                       .then_inc(tmp_ready, 1)

            U = Units(U_OUT)
            sums(2, U, 0)
            for j in range(7, 32):
                split(U, j, j + 1)
                adas(AT32, j, 3)
                if j % 8 == 3 and j > 8:
                    b = j // 8 - 1
                    gated(lambda off: 2 * b + off, N_OUT + b + 1, N_OUT + b, 0, b)
            gated(lambda off: 6 + off, N_OUT + 4, N_OUT + 3, 0, 3)

            def mid_low(T, tau, buf):
                for t in range(NT):
                    dve.wait_ge(hth_ready, T.tau(tau, 1 + t))
                    hs = (slice(None), buf, slice(4 * (tau % 2), 4 * (tau % 2) + 4), slice(t * P, (t + 1) * P))
                    dve.tensor_tensor(htl[hs], PS[:, 4 + t, :].rearrange("p (c n) -> p c n", c=4), hth[hs].bitcast(F32), ALU.subtract)\
                       .then_inc(ht_ready, 1)

            def mlp(layer, base, n0):
                def down(T, e, n, b):
                    gated(lambda off: T.e(e + b, off), T(n, 1), n, 1, b)

                def units(U, j0, j1, i=None):
                    for j in range(j0, j1):
                        split(U, j, j + 1)
                        if layer == 0 and i is not None and j in AT64:
                            ada(i + 4, AT64.index(j))

                U, T = Units(base), Turn(n0, layer)
                sums(3 if layer == 0 else 9, U, 0)
                split(U, 7, 16)
                U = Units(base + 16)
                split(U, 0, 2)
                mid_low(T, 0, 0)
                split(U, 2, 8)
                mid_low(T, 1, 0)
                with dve.Fori(0, 3) as i:
                    U, T = Units(base + 16, 64, i), Turn(n0 + 2, layer, i)
                    units(U, 8, 18, i)
                    mid_low(T, 2, 1)
                    units(U, 18, 24, i)
                    down(T, 0, 2, 0)
                    units(U, 24, 26, i)
                    mid_low(T, 3, 1)
                    units(U, 26, 28, i)
                    down(T, 0, 3, 1)
                    units(U, 28, 32, i)
                    down(T, 0, 4, 2)
                    units(U, 32, 36, i)
                    down(T, 0, 5, 3)
                    units(U, 36, 50, i)
                    mid_low(T, 4, 0)
                    units(U, 50, 56, i)
                    down(T, 4, 8, 0)
                    units(U, 56, 58, i)
                    mid_low(T, 5, 0)
                    units(U, 58, 60, i)
                    down(T, 4, 9, 1)
                    units(U, 60, 64, i)
                    if layer == 0:
                        dve.wait_ge(sum_done, i + 7)
                        dve.tensor_copy(colbuf[:, ds(i * KC, KC)], PS[:, 6, 0:KC]).then_inc(sum_read, 1)
                    down(T, 4, 10, 2)
                    units(U, 64, 68, i)
                    down(T, 4, 11, 3)
                    units(U, 68, 72, i)
                U, T = Units(base + 16 + 192), Turn(n0 + 2, layer, 3)
                if layer == 0:
                    sum_gate(6, 0)
                    sum_gate(6, 1)
                    dve.wait_ge(sum_read, 9)
                    cols(3, 0, colbuf[:, 0:KC])
                    cols(3, 1, colbuf[:, KC:2 * KC])
                    dve.sem_inc(cols_ready, 1)
                units(U, 8, 18)
                mid_low(T, 2, 1)
                units(U, 18, 24)
                down(T, 0, 2, 0)
                units(U, 24, 26)
                mid_low(T, 3, 1)
                units(U, 26, 28)
                down(T, 0, 3, 1)
                units(U, 28, 32)
                down(T, 0, 4, 2)
                units(U, 32, 36)
                down(T, 0, 5, 3)
                units(U, 36, 40)
                down(T, 4, 6, 0)
                units(U, 40, 44)
                down(T, 4, 7, 1)
                units(U, 44, 48)
                down(T, 4, 8, 2)
                down(T, 4, 9, 3)

            def norm_hx(c):
                normalise(c, hx, nrm)
                dve.wait_ge(cols_ready, c)
                split_low(c, xh, xl, slice(0, L))

            norm_hx(2)
            mlp(0, U_MLP0, N_MLP0)
            norm_hx(3)

            def stats(n):
                dve.wait_ge(v_ready, n - 3)
                for t in range(NT):
                    ins = dve.bn_stats(bst[:, t, n - 4, :], vg[:, t, (n - 4) * CB:(n - 3) * CB])
                return ins

            U = Units(U_OIN)
            for j in range(64):
                if j == 32:
                    split(U, 32, 37)
                    sum_cols(7)
                elif not 32 < j < 37:
                    split(U, j, j + 1)
                adas(AT32, j, 7)
                adas([a + 32 for a in AT32], j, 8)
                if j % 8 == 3 and j >= 43:
                    stats(j // 8 - 1)
            step(stats(7))
            for t in range(NT):
                ins = dve.bn_aggr(mv[:, t, :], bst[:, t, :, :].rearrange("p a b -> p (a b)"))
            ins.then_inc(mv_ready, 1)
            dve.wait_ge(lroot, 1)
            step(dve.reciprocal(mv[:, :, 1:2].rearrange("p t o -> p (t o)"), mv[:, :, 1:2].rearrange("p t o -> p (t o)")))
            for g in range(4):
                cs = slice(g * CB, (g + 1) * CB)
                for t in range(NT):
                    ins = dve.tensor_scalar(vg[:, t, cs], vg[:, t, cs], mv[:, t, 0:1], mv[:, t, 1:2], ALU.subtract, ALU.mult)
                step(ins)
                dve.wait_ge(ln_loaded2[g % 2], 32 * (g // 2 + 1))
                for n, op in ((0, ALU.mult), (1, ALU.add)):
                    ins = dve.tensor_tensor(vg[:, :, cs], vg[:, :, cs], lnp[:, g % 2, n, :].unsqueeze(1).broadcast_to([P, NT, CB]), op)
                    if n == 0:
                        step(ins)
                    else:
                        ins.then_inc(vn_norm, 1)
            for g in range(4):
                for t in range(NT):
                    dve.wait_ge(mix_done, 2 * g + t + 1)
                    cs = slice(g * CB, (g + 1) * CB)
                    dve.scalar_tensor_tensor(ug[:, t, cs], PS[:, (2 * g + t) % 4, :], bscol[:, g:g + 1], ug[:, t, cs], ALU.add, ALU.mult)\
                       .then_inc(um_ready, 1)
            for kp in range(8):
                dve.wait_ge(umh_ready, kp + 1)
                dve.tensor_tensor(xl[:, 2 * kp:2 * kp + 2, :].rearrange("p k n -> p (k n)"), PS[:, 4 + kp % 4, :],
                                  xh[:, 2 * kp:2 * kp + 2, :].rearrange("p k n -> p (k n)").bitcast(F32), ALU.subtract).then_inc(uml_ready, 1)
            U = Units(U_OOUT)
            sums(8, U, 0)
            for j in range(7, 32):
                split(U, j, j + 1)
                adas(AT32, j, 9)
                if j % 8 == 3 and j > 8:
                    b = j // 8 - 1
                    gated(lambda off: 72 + 2 * b + off, N_OOUT + b + 1, N_OOUT + b, 0, b)
            gated(lambda off: 78 + off, N_OOUT + 4, N_OOUT + 3, 0, 3)
            norm_hx(4)
            mlp(1, U_MLP1, N_MLP1)

            for t in range(NT):
                dve.wait_ge(rt_done, 11 + t)
                step(dve.reciprocal(rs[:, 10 + t:11 + t], ss[:, 10 + t:11 + t]))
                dve.wait_ge(fg_loaded, 16)
                dve.scalar_tensor_tensor(fin[:, t, :], hx[:, t, :], rs[:, 10 + t:11 + t], fg[:], ALU.mult, ALU.mult).then_inc(fin_ready, 1)


        @block.tensor
        def _(pe):
            pe.sem_inc(w_used, SPLIT)

            def mm(dst, lhsT, rhs, start=True, stop=True, **kw):
                return pe.matmul(dst, lhsT, rhs, start=start, stop=stop, **kw)

            def tok(U, j0, n, x, last=UPB, part=lambda j, h: 2 * j + h, ready=None, after=None, done=True):
                xa, xb = x
                for j in range(last):
                    pe.wait_ge(w_split, U.u(j0 + j, 1))
                    if ready is not None:
                        pe.wait_ge(ready[0], ready[1] + j + 1)
                    r = (j0 + j) % SPLIT
                    for h in range(UNIT):
                        k = part(j, h)
                        hi, lo = wh[:, r, h * CB:(h + 1) * CB], wl[:, r, h * CB:(h + 1) * CB]
                        for t in range(NT):
                            dst = PS[:, 2 * (n % 2) + t, :]
                            a, b = xa(k, t), xb(k, t)
                            mm(dst, a, hi, start=(j == 0 and h == 0), stop=False)
                            mm(dst, a, lo, start=False, stop=False)
                            ins = mm(dst, b, hi, start=False, stop=(j == last - 1 and h == 1))
                    ins.then_inc(w_used, 1)
                    if after and j in after:
                        after[j]()
                if done:
                    pe.wait_ge(w_used, U.u(j0 + last, SPLIT))
                    pe.sem_inc(lin_done, 1)

            def ada_sum(M, part):
                def go():
                    r = ROUND[M] + part
                    pe.wait_ge(ada_used, KC * (M + 1))
                    if r:
                        pe.wait_ge(sum_read, r)
                    if M in GATES:
                        for b in range(2):
                            c = (2 * part + b) * CB
                            ins = mm(PS[:, 6 + b, :], ones[:], ada_acc[:, c:c + CB])
                    else:
                        for k in range(KC):
                            ins = mm(PS[:, 6, k:k + 1], ada_acc[:, k * P:(k + 1) * P], ones[:, 0:1])
                    ins.then_inc(sum_done, 1)
                    if M != 6 and (part == 1 or M not in GATES):
                        pe.wait_ge(sum_done, r + 1)
                        pe.sem_inc(ada_summed, 1)
                return go

            def sum_at(M):
                return {0: ada_sum(M, 0), 2: ada_sum(M, 1)} if M in GATES else {0: ada_sum(M, 0)}

            pe.wait_ge(consts, 16 * 6)
            pe.wait_ge(csil_ready, 1)
            with pe.Fori(0, 2) as i:
                for g in range(2):
                    for k in range(KC):
                        r = k % RAW
                        pe.wait_ge(w_loaded[r], i * 64 + 32 * g + 16 * (k // RAW + 1))
                        for j in range(8):
                            ins = mm(PS[:, 6 + g, 2 * j:2 * j + 2], raw[:, r, j * P:(j + 1) * P], csil[:, k, :],
                                     start=(k == 0 and j == 0), stop=(k == KC - 1), skip_group_check=True)
                        ins.then_inc(a0_used, 1)
                    pe.wait_ge(a0_used, i * 32 + 16 * g + 16)
                    pe.sem_inc(a0_done, 1)
                    pe.wait_ge(a0_read, i * 2 + g + 1)

            def transposes(c, src, ready=None):
                pe.wait_ge(nrm_ready, 2 * c + 2)
                for kp in range(KC // 2):
                    w = 8 * c + kp - 3
                    if w >= 1:
                        pe.wait_ge(xt_ready, w)
                    for h in range(2):
                        for t in range(NT):
                            k = 2 * kp + h
                            ins = pe.transpose(PS[:, 4 + kp % 4, h * L + t * P:h * L + (t + 1) * P], src[:, t, k * P:(k + 1) * P], ident[:])
                    ins.then_inc(xp_done, 1)

            transposes(0, nrm1)
            transposes(1, nrm1)

            def fm(U, f, width):
                p = 4 * (f % 2)
                for j in range(UPB):
                    pe.wait_ge(w_split, U.u(8 * (f % 2) + j, 1))
                    for h in range(UNIT):
                        k = UNIT * j + h
                        for s in range(4):
                            dst = PS[:, p + s, 0:width]
                            c = h * CB + s * P
                            hi, lo = wh[:, j % SPLIT, c:c + P], wl[:, j % SPLIT, c:c + P]
                            mm(dst, hi, x1h[:, k, 0:width], start=(k == 0), stop=False)
                            mm(dst, hi, x1l[:, k, 0:width], start=False, stop=False)
                            ins = mm(dst, lo, x1h[:, k, 0:width], start=False, stop=(k == KC - 1))
                    ins.then_inc(w_used, 1)
                pe.wait_ge(w_used, U.u(8 * (f % 2) + 8, SPLIT))
                pe.sem_inc(fm_done, 1)

            pe.wait_ge(xt_ready, 16)
            with pe.Fori(0, 2) as i:
                for f in range(2):
                    pe.wait_ge(fm_read, i * 2 + f + 1)
                    fm(Units(U_KV, 16, i), f, 2 * L)
            for f in range(2):
                pe.wait_ge(fm_read, 5 + f)
                fm(Units(U_Q), f, L)
            pe.wait_ge(fm_read, 8)

            def x1(t):
                return slice(t * P, (t + 1) * P)
            xx = (lambda k, t: x1h[:, k, x1(t)], lambda k, t: x1l[:, k, x1(t)])
            for n in range(4):
                if n >= 2:
                    pe.wait_ge(acc_free[n % 2], 2 * (n // 2))
                tok(Units(U_ZP), 8 * n, n, xx, after=sum_at(n // 2) if n % 2 == 0 else None)
            pe.wait_ge(ab_split, 1)
            for t in range(4):
                dst = PS[:, 4, t * 4 * H:(t + 1) * 4 * H]
                for k in range(KC):
                    mm(dst, x1h[:, k, x1(t)], abh[:, k, :], start=(k == 0), stop=False)
                    mm(dst, x1h[:, k, x1(t)], abl[:, k, :], start=False, stop=False)
                    ins = mm(dst, x1l[:, k, x1(t)], abh[:, k, :], start=False, stop=(k == KC - 1))
            ins.then_inc(ab_done, 1)

            pe.wait_ge(g_ready, 1)
            for t in range(4):
                for d in range(2):
                    c = t * 2 * H + d * H
                    ins = mm(PS[:, 5, c:c + H], incl[:, d, :], gt[:, 5, t, d * H:(d + 1) * H])
            ins.then_inc(gam_done, 1)
            pe.wait_ge(gam_ready, 1)
            for t in range(4):
                for d in range(2):
                    c = t * 2 * H + d * H
                    ins = mm(PS[:, 7, c:c + H], edge[:, d, :], Q[:, 0, t, d, :])
            ins.then_inc(gam_done, 1)
            for t in range(4):
                ins = pe.transpose(PS[0:16, 6, t * P:(t + 1) * P], Q[:, 0, t, :, :].rearrange("p d h -> p (d h)"), ident[:])
            ins.then_inc(gam_done, 1)
            pe.wait_ge(gamT_ready, 1)

            with pe.Fori(0, H // 2) as i:
                pe.wait_ge(pair_free, i * 4 + 4)
                for n, (src, bank) in enumerate(((ck, 0), (cq, 2))):
                    pe.wait_ge(sq_ready2, i * 2 + n + 1)
                    for a in range(2):
                        dst = PS[:, a, :] if n == 0 else PS[:, 2, a * L:(a + 1) * L]
                        ins = mm(dst, ones[:], src[:, a, :])
                    ins.then_inc(nsum_done, 1)
                pe.wait_ge(silu_done, i * 3 + 3)
                for a in range(2):
                    for t in range(4):
                        ins = pe.transpose(PS[:, 6 + a, t * P:(t + 1) * P], vT[:, a, t * P:(t + 1) * P], ident[:])
                ins.then_inc(tok_done, 1)
                pe.wait_ge(kqn, i * 2 + 1)
                for a in range(2):
                    for t in range(4):
                        ins = pe.transpose(PS[:, 4 + a, t * P:(t + 1) * P], kT[:, a, t * P:(t + 1) * P], ident[:])
                ins.then_inc(tok_done, 1)
                for a in range(2):
                    for t in range(4):
                        k = kT[:, a, t * P:(t + 1) * P]
                        mm(PS[:, a, t * P:(t + 1) * P], k, k)
                pe.wait_ge(kqn, i * 2 + 2)
                for a in range(2):
                    for t in range(2):
                        ins = mm(PS[:, 2, a * L + t * P:a * L + (t + 1) * P], kT[:, a, t * P:(t + 1) * P], qT[:, a, t * P:(t + 1) * P])
                ins.then_inc(kk_done, 1)
                pe.wait_ge(sel_ready, i + 1)
                pe.wait_ge(tok_read, i * 2 + 2)
                for q in range(4):
                    ins = mm(PS[:, 4 + q, :], sel[0:16, q, :], gamT[0:16, :])
                ins.then_inc(row_done, 1)

                def flip(lv, s):
                    pe.wait_ge(xT_ready, i * 28 + 4 * lv + s + 1)
                    if lv == 0 and s == 0:
                        pe.wait_ge(qk_ready, i + 1)
                    for q in range(4):
                        ins = pe.transpose(PS[:, s, q * P:(q + 1) * P], XT[:, s, q, :], ident[:])
                    ins.then_inc(tr_done, 1)

                for s in range(4):
                    flip(0, s)
                for lv in range(1, LEVELS):
                    for s in range(4):
                        pe.wait_ge(b_ready, i * 24 + 4 * (lv - 1) + s + 1)
                        pe.wait_ge(x_ready, i * 24 + 4 * (lv - 1) + s + 1)
                        for q in range(4):
                            ins = mm(PS[:, s, q * P:(q + 1) * P], B[:, s, q, :], X[:, s, q, :])
                        ins.then_inc(mm1_done, 1)
                    for s in range(4):
                        pe.wait_ge(p_ready, i * 24 + 4 * (lv - 1) + s + 1)
                        pe.wait_ge(xT_ready, i * 28 + 4 * (lv - 1) + s + 1)
                        for q in range(4):
                            ins = mm(PS[:, 4 + s, q * P:(q + 1) * P], PB[:, s, q, :], XT[:, s, q, :])
                        ins.then_inc(mm2_done, 1)
                    if lv < LEVELS - 1:
                        for s in range(4):
                            flip(lv, s)

                pe.wait_ge(xT_ready, i * 28 + 28)
                for s in range(4):
                    pe.wait_ge(s_ready, i * 5 + s + 1)
                    for q in range(4):
                        t = TILE[q // 2][s]
                        ins = mm(PS[:, 0, q * P:(q + 1) * P], kT[:, q % 2, t * P:(t + 1) * P], S[:, q])
                    ins.then_inc(ks_done, 1)
                    if s >= 2:
                        if s == 3:
                            pe.wait_ge(eq_ready, i * 2 + 1)
                        for q in range(4):
                            t = TILE[q // 2][s]
                            ins = mm(PS[:, 1, q * P:(q + 1) * P], qT[:, q % 2, t * P:(t + 1) * P], S[:, q])
                        ins.then_inc(qs_done, 1)
                    pe.wait_ge(r_ready, i * 4 + s + 1)
                    for q in range(4):
                        ins = mm(PS[:, 2, q * P:(q + 1) * P], XT[:, s, q, :], R[:, q])
                    ins.then_inc(y_done, 1)
                    pe.wait_ge(vd_ready, i * 4 + s + 1)
                    for q in range(4):
                        t = TILE[q // 2][s]
                        ins = mm(PS[:, 4, q * P:(q + 1) * P], ktok[:, q % 2, t, :], VD[:, q])
                    ins.then_inc(ds_done, 1)
                    pe.wait_ge(vn_ready, i * 4 + s + 1)
                    if s >= 2:
                        if s == 3:
                            pe.wait_ge(o_ready, i * 2 + 1)
                        for q in range(4):
                            ins = mm(PS[:, 3, q * P:(q + 1) * P], QK[:, s - 2, q], VN[:, q])
                        ins.then_inc(ov_done, 1)
                pe.wait_ge(s_ready, i * 5 + 5)
                pe.wait_ge(o_ready, i * 2 + 2)
                pe.sem_inc(pair_free, 1)

            pe.wait_ge(dn_done, 1)
            pe.wait_ge(e3_loaded, 16 * 5)
            for c in range(8):
                for t in range(NT):
                    ins = mm(PS[:, c // 2, (c % 2) * L:(c % 2 + 1) * L], pt[:, t, c * P:(c + 1) * P], poolm[:, c // 2, t, :],
                             start=(t == 0), stop=(t == 1))
            ins.then_inc(pool_done, 1)
            pe.wait_ge(poolT_ready, 1)
            for c in range(8):
                g = c // 2
                for h in range(2):
                    ins = mm(PS[:, 4 + g, (c % 2) * L:(c % 2 + 1) * L], poolw[:, g, h, (c % 2) * P:(c % 2 + 1) * P], poolT[:, 2 * g + h, :],
                             start=(h == 0), stop=(h == 1))
            ins.then_inc(yb_done, 1)
            pe.wait_ge(ya_ready, 1)
            for h in range(H):
                for t in range(NT):
                    ins = pe.transpose(PS[:, h // 2, (h % 2) * L + t * P:(h % 2) * L + (t + 1) * P], otok[:, t, h, :], ident[:])
            ins.then_inc(ya_done, 1)

            xx = (lambda k, t: xh[:, k, x1(t)], lambda k, t: xl[:, k, x1(t)])
            pe.wait_ge(y_ready, 16)
            for n in range(N_OUT, N_OUT + 4):
                pe.wait_ge(acc_free[n % 2], 2 * (n // 2))
                tok(Units(U_OUT), 8 * (n - N_OUT), n, xx, after=sum_at(2) if n == N_OUT else None)

            def mlp(layer, base, n0):
                hl = [(lambda k, t, b=b: hth[:, b, k, x1(t)], lambda k, t, b=b: htl[:, b, k, x1(t)]) for b in range(2)]

                def turnover(T, tau):
                    def go():
                        pe.wait_ge(sqr_ready, T.tau(tau, 2))
                        if not (layer == 0 and tau == 0):
                            pe.wait_ge(ht_ready, T.tau(tau, 0))
                        for t in range(NT):
                            for c in range(4):
                                ins = pe.transpose(PS[:, 4 + t, c * P:(c + 1) * P], rbuf[:, t, c * P:(c + 1) * P], ident[:])
                            ins.then_inc(mt_done, 1)
                    return go

                def up(U, T, j, n, **kw):
                    pe.wait_ge(acc_free[n % 2], T.free(n))
                    tok(U, j, n, xx, **kw)

                def down(U, T, j, n, buf, after=None):
                    pe.wait_ge(acc_free[n % 2], T.free(n))
                    tok(U, j, n, hl[buf], last=SK // UNIT, after=after)

                def pair(U, T, j0, n, tau, buf, after=None):
                    up(U, T, j0, n, after=after)
                    up(U, T, j0 + 8, n + 1, after={4: turnover(T, tau)})
                    pe.wait_ge(ht_ready, T.tau(tau, 0))
                    down(U, T, j0 + 16, n + 2, 1 - buf)
                    down(U, T, j0 + 20, n + 3, 1 - buf, after={0: turnover(T, tau + 1)})
                    if layer == 0 and T.i is not None and not isinstance(T.i, int) and tau == 4:
                        def loop_sum():
                            pe.wait_ge(ada_used, T.i * KC + 5 * KC)
                            pe.wait_ge(sum_read, T.i + 6)
                            for k in range(KC):
                                ins = mm(PS[:, 6, k:k + 1], ada_acc[:, k * P:(k + 1) * P], ones[:, 0:1])
                            ins.then_inc(sum_done, 1)
                            pe.wait_ge(sum_done, T.i + 7)
                            pe.sem_inc(ada_summed, 1)
                        down(U, T, j0 + 24, n + 4, 1 - buf, after={1: loop_sum})
                    else:
                        down(U, T, j0 + 24, n + 4, 1 - buf)
                    down(U, T, j0 + 28, n + 5, 1 - buf)

                U, T = Units(base), Turn(n0, layer)
                up(U, T, 0, 0, ready=(xt_ready, 16 if layer == 0 else 32), after=sum_at(3 if layer == 0 else 9))
                up(U, T, 8, 1, after={4: turnover(T, 0)})
                U, T = Units(base + 16), Turn(n0 + 2, layer)
                pe.wait_ge(sqr_ready, T.tau(1, 2))
                turnover(T, 1)()
                with pe.Fori(0, 3) as i:
                    U, T = Units(base + 16, 64, i), Turn(n0 + 2, layer, i)
                    pair(U, T, 0, 0, 2, 1)
                    pair(U, T, 32, 6, 4, 0)
                U, T = Units(base + 16 + 192), Turn(n0 + 2, layer, 3)
                pair(U, T, 0, 0, 2, 1, after={3: ada_sum(6, 0), 4: ada_sum(6, 1)} if layer == 0 else None)
                pe.wait_ge(ht_ready, T.tau(4, 0))
                for b in range(4):
                    down(U, T, 32 + 4 * b, 6 + b, 1)

            transposes(2, nrm)
            mlp(0, U_MLP0, N_MLP0)
            transposes(3, nrm)

            for n in range(N_OIN, N_OIN + 8):
                b = n - N_OIN
                pe.wait_ge(acc_free[n % 2], 2 * (n // 2))
                tok(Units(U_OIN), 8 * b, n, xx, ready=(xt_ready, 24) if b == 0 else None, after=sum_at(7) if b == 4 else None)
            pe.wait_ge(ws_loaded, 16)
            pe.wait_ge(acc_free[0], 2 * 32)
            pe.wait_ge(acc_free[1], 2 * 32)
            for g in range(4):
                pe.wait_ge(vn_norm, g + 1)
                for t in range(NT):
                    m = 2 * g + t
                    if m >= 4:
                        pe.wait_ge(um_ready, m - 3)
                    mm(PS[:, m % 4, :], wsT[:, g, :], vg[:, t, g * CB:(g + 1) * CB]).then_inc(mix_done, 1)
            for kp in range(8):
                pe.wait_ge(um_ready, 2 * (kp // 2) + 2)
                if kp >= 4:
                    pe.wait_ge(uml_ready, kp - 3)
                for h in range(2):
                    for t in range(NT):
                        k = 2 * kp + h
                        ins = pe.transpose(PS[:, 4 + kp % 4, h * L + t * P:h * L + (t + 1) * P], ug[:, t, k * P:(k + 1) * P], ident[:])
                ins.then_inc(um_done, 1)
            for n in range(N_OOUT, N_OOUT + 4):
                b = n - N_OOUT
                if b == 0:
                    pe.wait_ge(um_ready, 8)
                pe.wait_ge(acc_free[n % 2], 2 * (n // 2))
                tok(Units(U_OOUT), 8 * b, n, xx, ready=(uml_ready, 0) if b == 0 else None, after=sum_at(8) if b == 0 else None)
            transposes(4, nrm)
            mlp(1, U_MLP1, N_MLP1)


def kernel(**inputs):
    import numpy as np
    import concourse.bacc as bacc
    from concourse.bass_utils import run_bass_kernel_spmd as run

    f = {k: np.ascontiguousarray(v) for k, v in inputs.items()}

    def cols(a, n):
        a = np.asarray(a)
        return np.ascontiguousarray(np.moveaxis(a.reshape(a.shape[:-1] + (n, P)), -1, 0))

    arrays = {name: f[name] for name in ("x", "ctx", "ada_w", "ada_b", "mlp_w1", "mlp_w2", "ev_w_in", "ev_dt_bias", "ev_a_log",
                                         "ev_onorm_g", "ev_w_out", "od_w_in", "od_ln_g", "od_ln_b", "od_w_out", "final_g")}
    arrays["ccol"] = np.ascontiguousarray(np.stack([cols(f["c"][0], KC), cols(f["c_ctx"], KC)], -1))
    arrays["adab"] = cols(f["ada_b"].reshape(12, D), KC)
    arrays["gcol"] = cols(np.stack([f["norm1_g"], f["norm2_g"]], 1).reshape(4, D), KC)
    arrays["bscol"] = np.ascontiguousarray(f["od_bs"][0].T)
    arrays["convw"] = np.ascontiguousarray(f["ev_conv_w"][0].reshape(5, 3, H, P).transpose(3, 1, 2, 0).reshape(P, 3, H * 5))
    arrays["poolw"] = np.ascontiguousarray(f["ev_pool_w"][0].reshape(4, 2, P, 2 * P).transpose(2, 0, 1, 3))
    arrays["pscale"] = cols(f["ev_pool_scale"][0], 8)
    arrays["wsT"] = np.ascontiguousarray(f["od_ws"][0].transpose(2, 0, 1))
    j, i = np.meshgrid(np.arange(P), np.arange(P), indexing="ij")
    arrays["ident"] = np.eye(P, dtype=np.float32)
    arrays["ones"] = np.ones((P, P), np.float32)
    arrays["incl"] = np.stack([i >= j, i <= j], 1).astype(np.float32)
    arrays["edge"] = np.stack([j == P - 1, j == 0], 1).astype(np.float32)
    lv = [((i > j) & (i >> (v + 1) == j >> (v + 1)) & (i >> v != j >> v)).astype(np.float32) for v in range(LEVELS)]
    arrays["lmask"] = np.ascontiguousarray(np.stack([np.stack([m, m.T], 1) for m in lv], 1))
    t = np.arange(L)
    pm = []
    for r in (1, 2, 4, 8):
        hi, lo = np.minimum(t + r + 1, L), np.maximum(t - r, 0)
        m = ((t[None] >= lo[:, None]) & (t[None] < hi[:, None])) / (hi - lo)[:, None].astype(np.float32) - np.eye(L)
        pm.append(m.T.reshape(2, P, L))
    arrays["poolm"] = np.ascontiguousarray(np.stack(pm).transpose(2, 0, 1, 3).astype(np.float32))
    nf = D // 4
    omega = (1.0 / (10000.0 ** (np.arange(nf, dtype=np.float32) / np.float32(nf)))).astype(np.float32)
    ar = (t // 64).astype(np.float32)[:, None] * omega
    ac = (t % 64).astype(np.float32)[:, None] * omega
    arrays["pos"] = np.concatenate([np.sin(ar), np.cos(ar), np.sin(ac), np.cos(ac)], -1).astype(np.float32)

    nc = bacc.Bacc("TRN2", target_bir_lowering=False, num_devices=1)
    A = {n: nc.dram_tensor("in_" + n, a.shape, F32, kind="ExternalInput").ap() for n, a in arrays.items()}
    out = nc.dram_tensor("out", (1, L, D), F32, kind="ExternalOutput").ap()
    build(nc, A, out)
    r = run(nc, [{"in_" + n: a for n, a in arrays.items()}], core_ids=[0])
    return r.results[0]["out"]
```

```python
import concourse.bass as bass
from concourse import mybir
from contextlib import ExitStack

F32 = mybir.dt.float32
F32R = mybir.dt.float32r
ALU = mybir.AluOpType
ACT = mybir.ActivationFunctionType
AX = mybir.AxisListType
ds = bass.ds

P = 128
D = 2048
KC = D // P
L = 256
NT = L // P
CB = 512
H = 8
QKV = 3 * H * P
EV_IN = QKV + 4 * H + 2 * H * P
ZP0 = QKV + 4 * H
FF = 4 * D
SLAB = 1024
SK = SLAB // P
SLABS = FF // SLAB
EPS = 1e-6
LEVELS = 7
UNIT = 2
UPB = KC // UNIT
RAW = 8
SPLIT = 4

U_A0, U_KV, U_Q, U_ZP, U_OUT, U_MLP0 = 0, 64, 96, 112, 144, 176
U_OIN, U_OOUT, U_MLP1 = 432, 496, 528
N_ZP, N_OUT, N_MLP0, N_OIN, N_OOUT, N_MLP1 = 0, 4, 8, 56, 64, 68

TILE = [[2, 3, 0, 1], [3, 2, 1, 0]]


class Units:

    def __init__(self, base, step=0, i=None):
        self.base, self.step, self.i = base, step, i

    def u(self, j, off=0):
        c = self.base + j + off
        return c if self.i is None else self.i * self.step + c

    def r(self, j, off=0):
        c = (self.base + j) // RAW + off
        return c if self.i is None else self.i * (self.step // RAW) + c

    def r16(self, j, off=0):
        c = 16 * ((self.base + j) // RAW + off)
        return c if self.i is None else self.i * (16 * self.step // RAW) + c


class Chain:

    def __init__(self, eng, sem):
        self.eng, self.sem, self.n, self.base = eng, sem, 0, 0

    def __call__(self, ins):
        self.n += 1
        ins.then_inc(self.sem, 1)
        self.eng.wait_ge(self.sem, self.base + self.n)

    def enter(self, i, per):
        self.n0, self.per = self.n, per
        self.base, self.n = i * per + self.n0, 0

    def leave(self, turns):
        assert self.n == self.per, f"{self.n} steps in a turn, not {self.per}"
        self.n, self.base = self.n0 + turns * self.per, 0

class Turn:

    def __init__(self, n0, layer, i=None):
        self.n0, self.layer, self.i = n0, layer, i

    def add(self, c, per):
        return c if self.i is None else self.i * per + c

    def n(self, n, off):
        return self.add(self.n0 + n + off, 12)

    __call__ = n

    def free(self, n):
        return self.add(2 * ((self.n0 + n) // 2), 12)

    def tau(self, tau, off):
        return self.add(32 * self.layer + 2 * tau + off, 8)

    def e(self, e, off):
        return self.add(8 + 72 * self.layer + 2 * e + off, 16)


def build(nc, A, out):
    stack = ExitStack()
    with stack:
        def sem(name):
            return stack.enter_context(nc.semaphore(name))

        def dram(name, shape):
            return nc.dram_tensor(name, shape, F32, kind="Internal").ap()

        def sbuf(where, name, shape, dt=F32):
            return where.enter_context(nc.sbuf_tensor(name, [P] + shape, dt))

        raw = sbuf(stack, "raw", [RAW, UNIT * CB])
        wh = sbuf(stack, "wh", [SPLIT, UNIT * CB], F32R)
        wl = sbuf(stack, "wl", [SPLIT, UNIT * CB], F32R)
        ada_raw = sbuf(stack, "ada_raw", [2, D])
        ada_acc = sbuf(stack, "ada_acc", [D])
        gate = sbuf(stack, "gate", [2, D])
        ident = sbuf(stack, "ident", [P])
        ones = sbuf(stack, "ones", [P])
        ccol = sbuf(stack, "ccol", [KC, 2])
        csil = sbuf(stack, "csil", [KC, 2])
        chl = sbuf(stack, "chl", [KC, 4], F32R)
        mod0 = sbuf(stack, "mod0", [2 * KC, 2])
        adab = sbuf(stack, "adab", [12, KC])
        gcol = sbuf(stack, "gcol", [4, KC])
        shc = sbuf(stack, "shc", [5, KC])
        gsc = sbuf(stack, "gsc", [5, KC])
        eps = sbuf(stack, "eps", [1])
        ss = sbuf(stack, "ss", [16])
        rs = sbuf(stack, "rs", [16])
        bscol = sbuf(stack, "bscol", [4])
        colbuf = sbuf(stack, "colbuf", [10, KC])
        spl = sbuf(stack, "spl", [512])
        PS = stack.enter_context(nc.psum_tensor("PS", [P, 8, 512], F32))

        e1 = ExitStack()
        x1h = sbuf(e1, "x1h", [KC, 2 * L], F32R)
        e0 = ExitStack()
        xtok = sbuf(e0, "xtok", [KC, 2 * L])
        e0.close()
        x1l = sbuf(e1, "x1l", [KC, 2 * L], F32R)
        nrm1 = sbuf(e1, "nrm1", [2, D])
        stage = nrm1[:, :, :].rearrange("p a (b n) -> p (a b) n", n=CB)
        arow = sbuf(e1, "arow", [2, 1024])
        abw = sbuf(e1, "abw", [KC, 4 * H])
        abh = sbuf(e1, "abh", [KC, 4 * H], F32R)
        abl = sbuf(e1, "abl", [KC, 4 * H], F32R)
        e1.close()

        late = ExitStack()
        otok = sbuf(late, "otok", [NT, H, P])
        e2 = ExitStack()
        abr = sbuf(e2, "abr", [4, 4 * H])
        dtb = sbuf(e2, "dtb", [2 * H]); alog = sbuf(e2, "alog", [2 * H])
        gt = sbuf(e2, "gt", [6, 4, 2 * H])
        Q = sbuf(e2, "Q", [6, 4, 2, H])
        Qs = sbuf(e2, "Qs", [48, 2])
        gamT = sbuf(e2, "gamT", [4 * P])
        sel = sbuf(e2, "sel", [4, P])
        incl = sbuf(e2, "incl", [2, P])
        edge = sbuf(e2, "edge", [2, P])
        lmask = sbuf(e2, "lmask", [LEVELS, 2, P])
        convw = sbuf(e2, "convw", [3, H * 5])
        cws = sbuf(e2, "cws", [3, 10])
        cbuf = sbuf(e2, "cbuf", [2560])
        ck = cbuf[:, 0:1024].rearrange("p (a n) -> p a n", a=2)
        cv = cbuf[:, 1024:2048].rearrange("p (a n) -> p a n", a=2)
        cq = cbuf[:, 2048:2560].rearrange("p (a n) -> p a n", a=2)
        B = cbuf[:, 0:2048].rearrange("p (s q n) -> p s q n", s=4, q=4)
        qT = sbuf(e2, "qT", [2, L]); kT = sbuf(e2, "kT", [2, 2 * L]); vT = sbuf(e2, "vT", [2, 2 * L])
        ktok = sbuf(e2, "ktok", [2, 4, P]); vtok = sbuf(e2, "vtok", [2, 4, P])
        X = sbuf(e2, "X", [4, 4, P])
        NM = sbuf(e2, "NM", [4, 4, P])
        XT = sbuf(e2, "XT", [4, 4, P])
        PB = sbuf(e2, "PB", [4, 4, P])
        QK = sbuf(e2, "QK", [2, 4, P]); DI = sbuf(e2, "DI", [2, 4, P])
        S = sbuf(e2, "S", [4, P])
        R, VN, VD, EQ = (PB[:, n] for n in range(4))
        e2.close()

        e3 = ExitStack()
        poolT = sbuf(e3, "poolT", [8, L]); osq = sbuf(e3, "osq", [NT, H, P])
        e3.close()
        late.close()
        tail = ExitStack()
        rbuf = sbuf(tail, "rbuf", [NT, CB])
        tmp = sbuf(tail, "tmp", [NT, CB])
        hx = sbuf(tail, "hx", [NT, D])
        xh = sbuf(tail, "xh", [KC, L], F32R)
        xl = sbuf(tail, "xl", [KC, L], F32R)
        b1 = ExitStack()
        zp = sbuf(b1, "zp", [2, NT, H * P])
        zt, pt = zp[:, 0], zp[:, 1]
        onorm = sbuf(b1, "onorm", [P])
        so = sbuf(b1, "so", [NT * H]); ro = sbuf(b1, "ro", [NT * H])
        poolm = sbuf(b1, "poolm", [4, 2, L])
        poolw = sbuf(b1, "poolw", [4, 2, L])
        pscale = sbuf(b1, "pscale", [8])
        b1.close()
        b2 = ExitStack()
        nrm = sbuf(b2, "nrm", [NT, D])
        b2.close()
        b3 = ExitStack()
        hth = sbuf(b3, "hth", [2, SK, L], F32R)
        htl = sbuf(b3, "htl", [2, SK, L], F32R)
        b3.close()
        b4 = ExitStack()
        ug = sbuf(b4, "ug", [NT, D])
        vg = sbuf(b4, "vg", [NT, D])
        wsT = sbuf(b4, "wsT", [4, P])
        bst = sbuf(b4, "bst", [NT, 4, 6])
        mv = sbuf(b4, "mv", [NT, 2])
        b4.close()
        b5 = ExitStack()
        fin = sbuf(b5, "fin", [NT, D])
        fg = sbuf(b5, "fg", [D])
        b5.close()
        tail.close()
        lnp = (rbuf, tmp)

        s_qT, s_kT, s_vT = dram("s_q", [H, P, L]), dram("s_k", [H, P, 2 * L]), dram("s_v", [H, P, 2 * L])
        s_zp = dram("s_zp", [2, NT, P, H * P])

        consts = sem("consts")
        cs_high, cs_split, arow_ready = sem("cs_high"), sem("cs_split"), sem("arow_ready")
        diag_ready, bc_done, gate_ready = sem("diag_ready"), sem("bc_done"), sem("gate_ready")
        xs_ready, spl_ready = sem("xs_ready"), sem("spl_ready")
        w_loaded = [sem(f"w_loaded{r}") for r in range(RAW)]
        w_high, w_split, w_used = sem("w_high"), sem("w_split"), sem("w_used")
        a0_half, a0_done = sem("a0_half"), sem("a0_done")
        ada_loaded = [sem("ada_loaded0"), sem("ada_loaded1")]
        ada_used, ada_summed = sem("ada_used"), sem("ada_summed")
        sum_done, sum_read = sem("sum_done"), sem("sum_read")
        eps_ready, um_done, umh_ready, uml_ready = sem("eps_ready"), sem("um_done"), sem("umh_ready"), sem("uml_ready")
        ln_loaded2 = [sem("ln_loaded0"), sem("ln_loaded1")]
        csil_ready, cols_ready = sem("csil_ready"), sem("cols_ready")
        h_loaded = [sem("h_loaded0"), sem("h_loaded1")]
        pos_loaded, h_ready = sem("pos_loaded"), sem("h_ready")
        sq_done, rt_done, nrm_ready = sem("sq_done"), sem("rt_done"), sem("nrm_ready")
        xp_done, xh_ready, xt_ready = sem("xp_done"), sem("xh_ready"), sem("xt_ready")
        fm_done, fm_read = sem("fm_done"), sem("fm_read")
        fm_stored = [sem("fm_stored0"), sem("fm_stored1")]
        lin_done = sem("lin_done")
        acc_free = [sem("acc_free0"), sem("acc_free1")]
        zp_stored = [sem("zp_stored0"), sem("zp_stored1")]
        ab_loaded, ab_high, ab_split, ab_done = sem("ab_loaded"), sem("ab_high"), sem("ab_split"), sem("ab_done")
        c2_loaded = sem("c2_loaded")
        act_step, dve_step, pool_step = sem("act_step"), sem("dve_step"), sem("pool_step")
        ab_ready, ex_ready, lx_ready, g_ready = sem("ab_ready"), sem("ex_ready"), sem("lx_ready"), sem("g_ready")
        gam_done, gam_ready, tot_done, q_dve, q_ready = (sem(n) for n in ("gam_done", "gam_ready", "tot_done", "q_dve", "q_ready"))
        gamT_ready = sem("gamT_ready")
        pair_in, pair_free = sem("pair_in"), sem("pair_free")
        conv_done, silu_done, sq_ready2, nsum_done, nroot, nlog = (sem(n) for n in ("conv_done", "silu_done", "sq2_ready", "nsum_done", "nroot", "nlog"))
        kqn, tok_done, tok_read, sel_ready = (sem(n) for n in ("kqn", "tok_done", "tok_read", "sel_ready"))
        kk_done, row_done, dif_ready, dec_ready, di_ready, nm_ready = (
            sem(n) for n in ("kk_done", "row_done", "dif_ready", "dec_ready", "di_ready", "nm_ready"))
        qk_ready = sem("qk_ready")
        b_ready, mm1_done, p_ready, mm2_done, xT_ready, tr_done, x_ready = (
            sem(n) for n in ("b_ready", "mm1_done", "p_ready", "mm2_done", "xT_ready", "tr_done", "x_ready"))
        ks_done, r_ready, y_done, vn_ready, vd_ready, ds_done, s_ready = (
            sem(n) for n in ("ks_done", "r_ready", "y_done", "vn_ready", "vd_ready", "ds_done", "s_ready"))
        qs_done, eq_ready, ov_done, o_ready = (sem(n) for n in ("qs_done", "eq_ready", "ov_done", "o_ready"))
        dn_done = sem("dn_done")
        zp_loaded, e3_loaded, pool_done, poolT_ready, yb_done = (
            sem(n) for n in ("zp_loaded", "e3_loaded", "pool_done", "poolT_ready", "yb_done"))
        osum_ready, oroot, zs_ready, ya_ready, ya_done = (sem(n) for n in ("osum_ready", "oroot", "zs_ready", "ya_ready", "ya_done"))
        yh_ready, y_ready = sem("yh_ready"), sem("y_ready")
        hx_loaded, hx_ready = sem("hx_loaded"), sem("hx_ready")
        tmp_ready, hx_added = sem("tmp_ready"), sem("hx_added")
        relu_ready, sqr_ready, mt_done, hth_ready, ht_ready = (
            sem(n) for n in ("relu_ready", "sqr_ready", "mt_done", "hth_ready", "ht_ready"))
        u_ready, v_ready, mv_ready, lroot, vn_norm, ln_loaded, ws_loaded = (
            sem(n) for n in ("u_ready", "v_ready", "mv_ready", "lroot", "vn_norm", "ln_loaded", "ws_loaded"))
        ln_free, mix_done, um_ready = sem("ln_free"), sem("mix_done"), sem("um_ready")
        fg_loaded, fin_ready, stored = sem("fg_loaded"), sem("fin_ready"), sem("stored")

        block = stack.enter_context(nc.Block())

        AT32 = [8 + 3 * k // 2 for k in range(16)]
        AT64 = [8 + 3 * k for k in range(16)]
        AT_OIN = {8: [9 + 3 * k // 2 for k in range(16)], 9: [38 + 3 * k // 2 for k in range(16)]}
        ADA = [(0, 2), (0, 3), (0, 4), (0, 5), (1, 3), (1, 0), (1, 1), (1, 2), (1, 4), (1, 5)]
        HX = {2: 8, 3: 72, 4: 80, 5: 144}

        def load_unit(sp, U, j, src):
            sp.dma_start(raw[:, j % RAW, :].rearrange("p (k n) -> p k n", k=UNIT),
                         src.rearrange("(k p) n -> p k n", p=P)).then_inc(w_loaded[j % RAW], 16)

        def ada_rows(M, k):
            layer, part = ADA[M]
            return A["ada_w"][layer, k * P:(k + 1) * P, part * D:(part + 1) * D]

        @block.sync
        def _(sp):
            for dst, name in ((ident[:], "ident"), (ones[:], "ones"), (ccol[:, :, :], "ccol"), (adab[:, :, :], "adab"),
                              (gcol[:, :, :], "gcol"), (bscol[:], "bscol")):
                sp.dma_start(dst, A[name]).then_inc(consts, 16)

            def load_ada(used, k, src):
                if used is not None:
                    sp.wait_ge(ada_used, used)
                sp.dma_start(ada_raw[:, k % 2, :], src).then_inc(ada_loaded[k % 2], 16)

            def a0(g, k, wait):
                if wait is not None:
                    sp.wait_ge(w_split, wait)
                sp.dma_start(raw[:, k % RAW, :], A["ada_w"][0, k * P:(k + 1) * P, ds(g * 1024, 1024)])\
                  .then_inc(w_loaded[k % RAW], 16)

            for k in range(KC):
                a0(0, k, k - 7 if k >= RAW else None)
            with sp.Fori(1, 4) as g:
                for k in range(KC):
                    a0(g, k, g * KC + k - 7)

            w_in = A["ev_w_in"][0]
            with sp.Fori(0, 4) as b:
                U = Units(U_KV, UPB, b)
                for j in range(UPB):
                    sp.wait_ge(w_split, U.u(j, -7))
                    load_unit(sp, U, j, w_in[j * UNIT * P:(j + 1) * UNIT * P, ds(b * CB + H * P, CB)])

            def phase(base, blocks, src, at=None, units=UPB):
                U = Units(base)
                for b in range(blocks):
                    for c in range(units):
                        j = b * units + c
                        sp.wait_ge(w_split, U.u(j, -7))
                        load_unit(sp, U, j, src(b, c))
                        for M in at or ():
                            for k in range(KC):
                                if at[M][k] == j:
                                    load_ada(16 * M + k - 1, k, ada_rows(M, k))

            def rows(w, c):
                return w[c * UNIT * P:(c + 1) * UNIT * P]

            phase(U_Q, 2, lambda b, c: rows(w_in, c)[:, b * CB:(b + 1) * CB])
            phase(U_ZP, 4, lambda b, c: rows(w_in, c)[:, ZP0 + b * CB:ZP0 + (b + 1) * CB])

            def heads(a):
                for dst, src in ((ck, s_kT), (cq, s_qT), (cv, s_vT)):
                    sp.dma_start(dst, src[a, :, :].rearrange("h p n -> p h n")).then_inc(pair_in, 16)

            sp.wait_ge(h_ready, 2)
            for k in range(2):
                load_ada(None, k, ada_rows(0, k))
            for p in range(2):
                sp.wait_ge(fm_stored[p], 16 * 3)
                sp.wait_ge(zp_stored[p], 16 * 2)
            sp.wait_ge(ab_done, 1)
            heads(slice(0, 2))
            for k in range(2, KC):
                load_ada(k - 1, k, ada_rows(0, k))
            with sp.Fori(1, 4) as i:
                for k in range(2):
                    load_ada(i * KC + k - 1, k, A["ada_w"][0, k * P:(k + 1) * P, ds(i * D + 2 * D, D)])
                sp.wait_ge(mm1_done, i * 24)
                heads(ds(i * 2, 2))
                for k in range(2, KC):
                    load_ada(i * KC + k - 1, k, A["ada_w"][0, k * P:(k + 1) * P, ds(i * D + 2 * D, D)])
            phase(U_OUT, 4, lambda b, c: rows(A["ev_w_out"][0], c)[:, b * CB:(b + 1) * CB], {4: AT32})

            def mlp(layer, base, ada):
                w1, w2 = A["mlp_w1"][layer], A["mlp_w2"][layer]

                def up(U, j0, slab, b):
                    for c in range(UPB):
                        j = j0 + 8 * b + c
                        sp.wait_ge(w_split, U.u(j, -7))
                        load_unit(sp, U, j, w1[c * UNIT * P:(c + 1) * UNIT * P, ds(slab * SLAB + b * CB, CB)])
                        yield j

                def down(U, j0, slab, b):
                    for c in range(SK // UNIT):
                        j = j0 + 4 * b + c
                        sp.wait_ge(w_split, U.u(j, -7))
                        load_unit(sp, U, j, w2[ds(slab * SLAB + c * UNIT * P, UNIT * P), b * CB:(b + 1) * CB])
                        yield j

                def turn(U, slab, i, two):
                    for h in range(2):
                        for b in range(2 if (two or h == 0) else 0):
                            yield from up(U, 32 * h, slab + h + 1, b)
                        for b in range(4):
                            yield from down(U, 32 * h + (16 if (two or h == 0) else 0), slab + h, b)

                U = Units(base)
                for b in range(2):
                    for _ in up(U, 0, 0, b):
                        pass
                with sp.Fori(0, 3) as i:
                    for j in turn(Units(base + 16, 64, i), i * 2, i, True):
                        if ada and j in AT64:
                            k = AT64.index(j)
                            load_ada(i * KC + 5 * KC + k - 1, k,
                                     A["ada_w"][1, k * P:(k + 1) * P, ds(i * D, D)])
                for _ in turn(Units(base + 16 + 192), 6, None, False):
                    pass

            mlp(0, U_MLP0, True)
            phase(U_OIN, 8, lambda b, c: rows(A["od_w_in"][0], c)[:, b * CB:(b + 1) * CB], AT_OIN)
            phase(U_OOUT, 4, lambda b, c: rows(A["od_w_out"][0], c)[:, b * CB:(b + 1) * CB])
            mlp(1, U_MLP1, False)
            for t in range(NT):
                sp.wait_ge(fin_ready, t + 1)
                sp.dma_start(out[0, t * P:(t + 1) * P, :], fin[:, t, :]).then_inc(stored, 16)
            sp.wait_ge(stored, 16 * NT)

        @block.scalar
        def _(act):
            step = Chain(act, act_step)
            act.sem_inc(fm_read, 2)

            def high(U, j):
                act.wait_ge(w_loaded[j % RAW], U.r16(j, 1))
                act.wait_ge(w_used, U.u(j, 1))
                act.copy(wh[:, j % SPLIT, :], raw[:, j % RAW, :]).then_inc(w_high, 1)

            def highs(U, *js):
                for j in range(*js):
                    high(U, j)

            for t in range(NT):
                act.dma_start(nrm1[:, t, :], A["x"][0, t * P:(t + 1) * P, :]).then_inc(h_loaded[t], 16)
                act.dma_start(ada_raw[:, t, :], A["pos"][t * P:(t + 1) * P, :]).then_inc(pos_loaded, 16)
            act.dma_start(abw[:, :, :], A["ev_w_in"][0][:, QKV:QKV + 4 * H].rearrange("(k p) n -> p k n", p=P))\
               .then_inc(ab_loaded, 16)
            act.wait_ge(consts, 16 * 6)
            act.activation(csil[:, :, :], ccol[:, :, :], ACT.Silu).then_inc(csil_ready, 1)
            act.wait_ge(csil_ready, 1)
            act.copy(chl[:, :, 0:2], csil[:, :, :]).then_inc(cs_high, 1)
            act.sem_inc(xs_ready, 2)

            def root(c, t, src, junk):
                col = 2 * c + t
                act.activation(junk, src, ACT.Square, accum_out=ss[:, col:col + 1]).then_inc(sq_done, 1)
                act.wait_ge(sq_done, col + 1)
                act.activation(ss[:, col:col + 1], ss[:, col:col + 1], ACT.Sqrt, bias=eps[:, 0:1], scale=1.0 / D)\
                   .then_inc(rt_done, 1)

            def roots1(c):
                for t in range(NT):
                    if c == 0:
                        act.wait_ge(h_ready, t + 1)
                    else:
                        act.wait_ge(h_loaded[t], 32)
                    root(c, t, nrm1[:, t, :].rearrange("p (a n) -> p a n", n=L), xtok[:, 0:8, c * L:(c + 1) * L])

            def take_tokens(c):
                for kp in range(KC // 2):
                    act.wait_ge(xp_done, 8 * c + kp + 1)
                    act.copy(xtok[:, 2 * kp:2 * kp + 2, c * L:(c + 1) * L],
                             PS[:, 6 + kp % 2, :].rearrange("p (k n) -> p k n", k=2)).then_inc(xs_ready, 1)

            U = Units(U_A0)
            act.wait_ge(eps_ready, 1)
            highs(U, 0, 6)
            roots1(0)
            highs(U, 6, 20)
            take_tokens(0)
            for t in range(NT):
                act.dma_start(nrm1[:, t, :], A["ctx"][0, t * P:(t + 1) * P, :]).then_inc(h_loaded[t], 16)
            highs(U, 20, 36)
            roots1(1)
            highs(U, 36, 52)
            take_tokens(1)
            highs(U, 52, 64)

            def split_high(c, dst, cols):
                for kp in range(KC // 2):
                    act.wait_ge(xp_done, 8 * c + kp + 1)
                    for h in range(2):
                        k = 2 * kp + h
                        ins = act.activation(dst[:, k, cols], PS[:, 4 + kp % 4, h * L:(h + 1) * L], ACT.Identity,
                                             bias=shc[:, c, k:k + 1], scale=gsc[:, c, k:k + 1])
                    ins.then_inc(xh_ready, 1)

            act.wait_ge(cols_ready, 1)
            act.wait_ge(xs_ready, 18)
            U = Units(U_KV)
            for j in range(4):
                for k in range(4 * j, 4 * j + 4):
                    for c in range(2):
                        ins = act.activation(x1h[:, k, c * L:(c + 1) * L], xtok[:, k, c * L:(c + 1) * L], ACT.Identity,
                                             bias=shc[:, c, k:k + 1], scale=gsc[:, c, k:k + 1])
                    ins.then_inc(xh_ready, 1)
                high(U, j)

            def fm_store(f, F, width, dst, hs):
                p = f % 2
                act.wait_ge(fm_done, F(1))
                if not isinstance(F(0), int) or F(0) >= 2:
                    act.wait_ge(fm_stored[p], F(None))
                act.copy(stage[:, 4 * p:4 * p + 4, 0:width], PS[:, 4 * p:4 * p + 4, 0:width]).then_inc(fm_read, 1)
                act.wait_ge(fm_read, F(3))
                act.dma_start(dst[hs, :, :].rearrange("h p n -> p h n"), stage[:, 4 * p:4 * p + 4, 0:width])\
                   .then_inc(fm_stored[p], 16)

            def fm_block(f):
                return lambda off: 16 * (f // 2) if off is None else f + off

            stores = [(2 * L, s_kT, 0), (2 * L, s_kT, 4), (2 * L, s_vT, 0), (2 * L, s_vT, 4), (L, s_qT, 0), (L, s_qT, 4)]
            for f in range(6):
                width, dst, h0 = stores[f]
                highs(U, 8 * f + 4, 8 * f + 12)
                fm_store(f, fm_block(f), width, dst, slice(h0, h0 + 4))

            act.wait_ge(ab_loaded, 16)
            act.copy(abh[:, :, :], abw[:, :, :]).then_inc(ab_high, 1)
            U = Units(U_ZP)
            act.wait_ge(fm_stored[0], 48)
            act.wait_ge(fm_stored[1], 48)
            for n in range(4):
                highs(U, 8 * n + 4, min(8 * n + 12, 32))
                act.wait_ge(lin_done, n + 1)
                if n >= 2:
                    act.wait_ge(zp_stored[n % 2], 16)
                q = 4 * (n % 2)
                for t in range(NT):
                    act.copy(stage[:, q + t, :], PS[:, 2 * (n % 2) + t, :]).then_inc(acc_free[n % 2], 1)
                act.wait_ge(acc_free[n % 2], 2 * (n // 2) + 2)
                act.dma_start(s_zp[n // 2, :, :, (n % 2) * CB:(n % 2 + 1) * CB].rearrange("t p n -> p t n"),
                              stage[:, q:q + NT, :]).then_inc(zp_stored[n % 2], 16)

            act.wait_ge(ab_done, 1)
            act.wait_ge(zp_stored[0], 32)
            act.wait_ge(zp_stored[1], 32)
            for dst, name in ((incl[:, :, :], "incl"), (edge[:, :, :], "edge"), (lmask[:, :, :, :], "lmask"), (convw[:, :, :], "convw")):
                act.dma_start(dst, A[name]).then_inc(c2_loaded, 16)
            for dst, name in ((dtb[:], "ev_dt_bias"), (alog[:], "ev_a_log")):
                act.dma_start(dst, A[name].rearrange("o d h -> (o d h)").partition_broadcast(P)).then_inc(c2_loaded, 16)
            act.copy(abr[:, :, :], PS[:, 4, 0:4 * 4 * H].rearrange("p (t n) -> p t n", t=4)).then_inc(ab_ready, 1)
            act.wait_ge(ab_ready, 1)
            act.wait_ge(c2_loaded, 16 * 6)
            act.activation(Q[:, 1, :, :, :].rearrange("p t d h -> p t (d h)"), abr[:, :, 2 * H:4 * H], ACT.Sigmoid)
            step(act.activation(alog[:], alog[:], ACT.Exp))
            act.wait_ge(ex_ready, 1)
            act.activation(gt[:, 1], gt[:, 1], ACT.Exp).then_inc(lx_ready, 1)
            act.wait_ge(q_dve, 1)
            act.activation(Q[:, 5, :, :, :].rearrange("p t d h -> p (t d h)"), Q[:, 0, :, :, :].rearrange("p t d h -> p (t d h)"), ACT.Exp)
            act.activation(gt[:, 2], gt[:, 2], ACT.Exp)
            act.activation(Q[:, 4, :, :, :].rearrange("p t d h -> p (t d h)"), gt[:, 3].rearrange("p t n -> p (t n)"), ACT.Exp)\
               .then_inc(q_ready, 1)
            act.wait_ge(gam_done, 3)
            act.copy(gamT[0:16, :], PS[0:16, 6, :]).then_inc(gamT_ready, 1)

            with act.Fori(0, H // 2) as i:
                act.wait_ge(pair_free, i * 4 + 4)
                for n, dst in enumerate((kT, qT, vT)):
                    act.wait_ge(conv_done, i * 3 + n + 1)
                    act.activation(dst[:, :, :], dst[:, :, :], ACT.Silu).then_inc(silu_done, 1)
                for n, (dst, src) in enumerate(((ck, PS[:, 0:2, :]), (cq, PS[:, 2, :].rearrange("p (a n) -> p a n", a=2)))):
                    act.wait_ge(nsum_done, i * 2 + n + 1)
                    act.activation(dst, src, ACT.Ln, bias=eps[:, 0:1]).then_inc(nlog, 1)
                for n, dst in enumerate((ck, cq)):
                    act.wait_ge(nlog, i * 2 + n + 1)
                    act.activation(dst, dst, ACT.Exp, scale=-0.5).then_inc(nroot, 1)
                act.wait_ge(tok_done, i * 2 + 1)
                act.copy(vtok[:, :, :, :].rearrange("p a t n -> p a (t n)"), PS[:, 6:8, :]).then_inc(tok_read, 1)
                act.wait_ge(tok_done, i * 2 + 2)
                act.copy(ktok[:, :, :, :].rearrange("p a t n -> p a (t n)"), PS[:, 4:6, :]).then_inc(tok_read, 1)
                act.wait_ge(dif_ready, i + 1)
                act.activation(X[:, :, :, :].rearrange("p s q n -> p (s q n)"), X[:, :, :, :].rearrange("p s q n -> p (s q n)"), ACT.Exp)\
                   .then_inc(dec_ready, 1)

                def take_x(lv, s):
                    act.wait_ge(tr_done, i * 24 + 4 * lv + s + 1)
                    act.copy(X[:, s], PS[:, s, :].rearrange("p (q n) -> p q n", q=4)).then_inc(x_ready, 1)

                for s in range(4):
                    take_x(0, s)
                for lv in range(1, LEVELS):
                    for s in range(4):
                        act.wait_ge(mm1_done, i * 24 + 4 * (lv - 1) + s + 1)
                        act.copy(PB[:, s], PS[:, s, :].rearrange("p (q n) -> p q n", q=4)).then_inc(p_ready, 1)
                    if lv < LEVELS - 1:
                        for s in range(4):
                            take_x(lv, s)
                for s in range(4):
                    act.wait_ge(vd_ready, i * 4 + s + 1)
                    for q in range(4):
                        t = TILE[q // 2][s]
                        ins = act.activation(VN[:, q], PS[:, 2, q * P:(q + 1) * P], ACT.Copy, scale=Qs[:, 8 + 2 * t + q // 2, q % 2:q % 2 + 1])
                    ins.then_inc(vn_ready, 1)
                    if s >= 2:
                        act.wait_ge(qs_done, i * 2 + s - 1)
                        if s == 3:
                            act.wait_ge(o_ready, i * 2 + 1)
                        for q in range(4):
                            t = TILE[q // 2][s]
                            ins = act.activation(EQ[:, q], PS[:, 1, q * P:(q + 1) * P], ACT.Copy,
                                                 scale=Qs[:, 40 + 2 * t + q // 2, q % 2:q % 2 + 1])
                        ins.then_inc(eq_ready, 1)
                act.wait_ge(vn_ready, i * 4 + 4)
                act.wait_ge(eq_ready, i * 2 + 2)
                act.sem_inc(pair_free, 1)

            act.wait_ge(dn_done, 1)
            act.dma_start(zp[:, :, :, :].rearrange("p s t n -> p (s t) n"), s_zp.rearrange("s t p n -> p (s t) n")).then_inc(e3_loaded, 16)
            for dst, name in ((poolm[:, :, :, :], "poolm"), (poolw[:, :, :, :], "poolw"), (pscale[:], "pscale")):
                act.dma_start(dst, A[name]).then_inc(e3_loaded, 16)
            act.dma_start(onorm[:], A["ev_onorm_g"].rearrange("o n -> (o n)").partition_broadcast(P)).then_inc(e3_loaded, 16)
            act.wait_ge(bc_done, 1)
            act.copy(gate[:, 0, :], PS[:, 4:8, :].rearrange("p b n -> p (b n)")).then_inc(gate_ready, 1)
            act.wait_ge(osum_ready, 1)
            act.activation(ro[:], so[:], ACT.Sqrt, bias=eps[:, 0:1], scale=1.0 / P).then_inc(oroot, 1)
            act.wait_ge(e3_loaded, 16 * 5)
            act.activation(zt, zt, ACT.Silu).then_inc(zs_ready, 1)
            act.wait_ge(pool_done, 1)
            act.copy(poolT[:, :, :].rearrange("p c n -> p (c n)"), PS[:, 0:4, :].rearrange("p b n -> p (b n)")).then_inc(poolT_ready, 1)
            act.wait_ge(yb_done, 1)
            for c in range(8):
                act.activation(xh[:, 8 + c, :], PS[:, 4 + c // 2, (c % 2) * L:(c % 2 + 1) * L], ACT.Copy,
                               scale=pscale[:, c:c + 1]).then_inc(yh_ready, 1)
            act.wait_ge(ya_done, 1)
            for c in range(8):
                act.copy(xh[:, c, :], PS[:, c // 2, (c % 2) * L:(c % 2 + 1) * L]).then_inc(yh_ready, 1)
            act.wait_ge(y_ready, 16)
            for t in range(NT):
                act.dma_start(hx[:, t, :], A["x"][0, t * P:(t + 1) * P, :]).then_inc(hx_loaded, 16)
                act.dma_start(zp[:, t, :, :].rearrange("p a n -> p (a n)"), A["pos"][t * P:(t + 1) * P, :]).then_inc(hx_loaded, 16)

            def take_gate(n, g):
                act.wait_ge(bc_done, n + 1)
                act.copy(gate[:, g, :], PS[:, 4:8, :].rearrange("p b n -> p (b n)")).then_inc(gate_ready, 1)

            highs(Units(U_OUT), 0, 8)
            take_gate(1, 1)
            highs(Units(U_OUT), 8, 32)

            def normalise(c):
                act.wait_ge(hx_added, HX[c])
                for t in range(NT):
                    root(c, t, hx[:, t, :], PS[:, 0:4, :].rearrange("p b n -> p (b n)"))
                act.wait_ge(cols_ready, c)
                split_high(c, xh, slice(0, L))

            def relus(T, layer, tau, n):
                act.wait_ge(lin_done, T(n, 1))
                first = tau == 0 and T.i is None and layer == 0
                if not first:
                    act.wait_ge(mt_done, T.tau(tau, 0))
                for t in range(NT):
                    act.activation(rbuf[:, t, :], PS[:, 2 * (n % 2) + t, :], ACT.Relu).then_inc(relu_ready, 1)

            def mids(T, tau, buf):
                for t in range(NT):
                    act.wait_ge(mt_done, T.tau(tau, 1 + t))
                    act.copy(hth[:, buf, 4 * (tau % 2):4 * (tau % 2) + 4, t * P:(t + 1) * P],
                             PS[:, 4 + t, :].rearrange("p (c n) -> p c n", c=4)).then_inc(hth_ready, 1)

            def mlp(layer, base, n0):
                U, T = Units(base), Turn(n0, layer)
                highs(U, 0, 12)
                relus(T, layer, 0, 0)
                highs(U, 12, 16)
                U = Units(base + 16)
                highs(U, 0, 2)
                mids(T, 0, 0)
                highs(U, 2, 4)
                relus(T, layer, 1, 1)
                highs(U, 4, 8)
                mids(T, 1, 0)

                def pair(U, T, j0, tau, n, buf):
                    highs(U, j0, j0 + 12)
                    relus(T, layer, tau, n)
                    highs(U, j0 + 12, j0 + 18)
                    mids(T, tau, buf)
                    highs(U, j0 + 18, j0 + 20)
                    relus(T, layer, tau + 1, n + 1)
                    highs(U, j0 + 20, j0 + 26)
                    mids(T, tau + 1, buf)
                    highs(U, j0 + 26, j0 + 32)

                with act.Fori(0, 3) as i:
                    U, T = Units(base + 16, 64, i), Turn(n0 + 2, layer, i)
                    highs(U, 8, 12)
                    relus(T, layer, 2, 0)
                    highs(U, 12, 18)
                    mids(T, 2, 1)
                    highs(U, 18, 20)
                    relus(T, layer, 3, 1)
                    highs(U, 20, 26)
                    mids(T, 3, 1)
                    highs(U, 26, 32)
                    pair(U, T, 32, 4, 6, 0)
                    highs(U, 64, 72)
                U, T = Units(base + 16 + 192), Turn(n0 + 2, layer, 3)
                highs(U, 8, 12)
                relus(T, layer, 2, 0)
                highs(U, 12, 18)
                mids(T, 2, 1)
                highs(U, 18, 20)
                relus(T, layer, 3, 1)
                highs(U, 20, 26)
                mids(T, 3, 1)
                highs(U, 26, 48)

            normalise(2)
            mlp(0, U_MLP0, N_MLP0)
            normalise(3)

            U = Units(U_OIN)
            act.dma_start(wsT[:, :, :], A["wsT"]).then_inc(ws_loaded, 16)
            highs(U, 0, 4)
            for n in range(8):
                highs(U, 8 * n + 4, min(8 * n + 12, 64))
                act.wait_ge(lin_done, N_OIN + n + 1)
                if n == 0:
                    act.wait_ge(xp_done, 32)
                dst = (ug, vg)[n // 4]
                for t in range(NT):
                    act.activation(dst[:, t, (n % 4) * CB:(n % 4 + 1) * CB], PS[:, 2 * (n % 2) + t, :], ACT.Gelu)\
                       .then_inc(acc_free[n % 2], 1)
                act.wait_ge(acc_free[n % 2], 2 * ((N_OIN + n) // 2) + 2)
                if n >= 4:
                    act.sem_inc(v_ready, 1)
                if n == 0:
                    take_gate(2, 0)
            act.wait_ge(mv_ready, 1)
            act.activation(mv[:, :, 1:2].rearrange("p t o -> p (t o)"), mv[:, :, 1:2].rearrange("p t o -> p (t o)"), ACT.Sqrt,
                           bias=eps[:, 0:1]).then_inc(lroot, 1)
            for g in range(4):
                if g >= 2:
                    act.wait_ge(vn_norm, g - 1)
                for n, name in enumerate(("od_ln_g", "od_ln_b")):
                    act.dma_start(lnp[g % 2][:, n, :], A[name][0, g * CB:(g + 1) * CB].partition_broadcast(P)).then_inc(ln_loaded2[g % 2], 16)
            for kp in range(8):
                act.wait_ge(um_done, kp + 1)
                act.copy(xh[:, 2 * kp:2 * kp + 2, :].rearrange("p k n -> p (k n)"), PS[:, 4 + kp % 4, :]).then_inc(umh_ready, 1)
            highs(Units(U_OOUT), 0, 8)
            take_gate(3, 1)
            highs(Units(U_OOUT), 8, 32)
            normalise(4)
            mlp(1, U_MLP1, N_MLP1)
            act.wait_ge(hx_added, HX[5])
            act.dma_start(fg[:], A["final_g"].partition_broadcast(P)).then_inc(fg_loaded, 16)
            for t in range(NT):
                root(5, t, hx[:, t, :], PS[:, 0:4, :].rearrange("p b n -> p (b n)"))

        def flat(ap):
            return ap.rearrange("p a b -> p (a b)")

        @block.gpsimd
        def _(pool):
            step = Chain(pool, pool_step)
            pool.memset(eps[:], EPS).then_inc(eps_ready, 1)
            pool.sem_inc(pair_free, 4)

            with pool.Fori(0, H // 2) as i:
                for n, (dst, src) in enumerate(((ck, kT), (cq, qT))):
                    pool.wait_ge(silu_done, i * 3 + n + 1)
                    pool.tensor_tensor(dst, src[:, :, :], src[:, :, :], ALU.mult).then_inc(sq_ready2, 1)
                pool.wait_ge(dec_ready, i + 1)
                for s in range(2):
                    ins = pool.tensor_tensor(DI[:, s].rearrange("p (d a) n -> p d a n", d=2),
                                             X[:, 2 + s].rearrange("p (d a) n -> p d a n", d=2),
                                             incl[:, :, :].unsqueeze(2).broadcast_to([P, 2, 2, P]), ALU.mult)
                ins.then_inc(di_ready, 1)
                for lv in range(1, LEVELS):
                    for s in range(4):
                        pool.wait_ge(nm_ready, i * 4 + s + 1)
                        if lv > 1:
                            pool.wait_ge(mm1_done, i * 24 + 4 * (lv - 2) + s + 1)
                        pool.tensor_tensor(B[:, s].rearrange("p (d a) n -> p d a n", d=2),
                                           NM[:, s].rearrange("p (d a) n -> p d a n", d=2),
                                           lmask[:, lv].unsqueeze(2).broadcast_to([P, 2, 2, P]), ALU.mult).then_inc(b_ready, 1)
                pool.wait_ge(b_ready, i * 24 + 24)
                pool.sem_inc(pair_free, 1)

            for t in range(NT):
                pool.wait_ge(hx_loaded, 64)
                pool.tensor_tensor(hx[:, t, :], hx[:, t, :], zp[:, t].rearrange("p a n -> p (a n)"), ALU.add).then_inc(hx_ready, 1)
            pool.wait_ge(hx_ready, 2)

            def add(e_count, cols, n):
                for t in range(NT):
                    pool.wait_ge(tmp_ready, e_count(1 + t))
                    pool.sem_inc(acc_free[n % 2], 1)
                    pool.tensor_tensor(hx[:, t, cols], hx[:, t, cols], tmp[:, t, :], ALU.add).then_inc(hx_added, 1)

            def square(T, tau, n):
                for t in range(NT):
                    pool.wait_ge(relu_ready, T.tau(tau, 1 + t))
                    pool.sem_inc(acc_free[n % 2], 1)
                    pool.tensor_tensor(rbuf[:, t, :], rbuf[:, t, :], rbuf[:, t, :], ALU.mult).then_inc(sqr_ready, 1)

            for b in range(4):
                add(lambda off: 2 * b + off, slice(b * CB, (b + 1) * CB), N_OUT + b)

            def mlp(layer):
                def downs(T, e, which):
                    for b in which:
                        add(lambda off: T.e(e + b, off), slice(b * CB, (b + 1) * CB), b)

                T = Turn(0, layer)
                square(T, 0, 0)
                square(T, 1, 1)
                with pool.Fori(0, 3) as i:
                    T = Turn(0, layer, i)
                    for h in range(2):
                        square(T, 2 + 2 * h, 0)
                        square(T, 3 + 2 * h, 1)
                        downs(T, 4 * h, range(4))
                T = Turn(0, layer, 3)
                square(T, 2, 0)
                square(T, 3, 1)
                downs(T, 0, range(4))
                downs(T, 4, range(4))

            mlp(0)
            for b in range(4):
                add(lambda off: 72 + 2 * b + off, slice(b * CB, (b + 1) * CB), N_OOUT + b)
            mlp(1)

        @block.vector
        def _(dve):
            step = Chain(dve, dve_step)

            def split(U, *js):
                for j in range(*js):
                    dve.wait_ge(w_high, U.u(j, 1))
                    dve.tensor_tensor(wl[:, j % SPLIT, :], raw[:, j % RAW, :], wh[:, j % SPLIT, :].bitcast(F32), ALU.subtract)\
                       .then_inc(w_split, 1)

            dve.sem_inc(sum_read, 1)

            def ada(M, k, i=None):
                def count(per, off):
                    return M * per + off if i is None else i * per + M * per + off
                dve.wait_ge(ada_loaded[k % 2], count(128, 16 * (k // 2 + 1)))
                if k == 0:
                    dve.wait_ge(ada_summed, count(1, 1))
                    dve.tensor_scalar(ada_acc[:], ada_raw[:, 0, :], csil[:, 0, 0:1], None, ALU.mult).then_inc(ada_used, 1)
                else:
                    dve.wait_ge(ada_used, count(KC, k))
                    dve.scalar_tensor_tensor(ada_acc[:], ada_raw[:, k % 2, :], csil[:, k, 0:1], ada_acc[:], ALU.mult, ALU.add)\
                       .then_inc(ada_used, 1)

            def adas(at, j, M):
                for k in range(KC):
                    if at[k] == j:
                        ada(M, k)

            def take_sum(M):
                dve.wait_ge(sum_done, M + 1)
                step(dve.tensor_copy(colbuf[:, M, :], PS[:, 6, 0:KC]))
                dve.sem_inc(sum_read, 1)

            def diagonals(M, layer, part):
                step(dve.tensor_tensor(colbuf[:, M, :], colbuf[:, M, :], adab[:, 6 * layer + part, :], ALU.add))
                dve.tensor_tensor(ada_acc[:].rearrange("p (k n) -> p k n", k=KC), ident[:].unsqueeze(1).broadcast_to([P, KC, P]),
                                  colbuf[:, M, :].unsqueeze(2).broadcast_to([P, KC, P]), ALU.mult).then_inc(diag_ready, 1)

            def cols(c, scale, src):
                dst = gsc if scale else shc
                part = (0 if c < 2 or c == 3 else 3) + scale
                layer = 0 if c < 3 else 1
                step(dve.tensor_tensor(dst[:, c, :], src, adab[:, 6 * layer + part, :], ALU.add))
                if scale:
                    step(dve.scalar_tensor_tensor(dst[:, c, :], dst[:, c, :], 1.0, gcol[:, max(c - 1, 0), :], ALU.add, ALU.mult))

            for t in range(NT):
                dve.wait_ge(h_loaded[t], 16)
                dve.wait_ge(pos_loaded, 32)
                dve.tensor_tensor(nrm1[:, t, :], nrm1[:, t, :], ada_raw[:, t, :], ALU.add).then_inc(h_ready, 1)
            dve.wait_ge(consts, 16 * 6)
            dve.wait_ge(csil_ready, 1)
            dve.wait_ge(cs_high, 1)
            dve.tensor_tensor(chl[:, :, 2:4], csil[:, :, :], chl[:, :, 0:2].bitcast(F32), ALU.subtract).then_inc(cs_split, 1)

            def normalise(c, src, dst):
                for t in range(NT):
                    col = 2 * c + t
                    dve.wait_ge(rt_done, col + 1)
                    step(dve.reciprocal(rs[:, col:col + 1], ss[:, col:col + 1]))
                    dve.tensor_scalar(dst[:, t, :], src[:, t, :], rs[:, col:col + 1], None, ALU.mult).then_inc(nrm_ready, 1)

            def split_low(c, high, dst, cols):
                for kp in range(KC // 2):
                    dve.wait_ge(xh_ready, 8 * c + kp + 1)
                    for h in range(2):
                        k = 2 * kp + h
                        ins = dve.tensor_scalar(spl[:, h * L:(h + 1) * L], PS[:, 4 + kp % 4, h * L:(h + 1) * L],
                                                gsc[:, c, k:k + 1], shc[:, c, k:k + 1], ALU.mult, ALU.add)
                    step(ins)
                    dve.tensor_tensor(dst[:, 2 * kp:2 * kp + 2, cols], spl[:].rearrange("p (k n) -> p k n", k=2),
                                      high[:, 2 * kp:2 * kp + 2, cols].bitcast(F32), ALU.subtract).then_inc(xt_ready, 1)
                    dve.wait_ge(xt_ready, 8 * c + kp + 1)

            dve.wait_ge(consts, 16 * 6)
            dve.wait_ge(csil_ready, 1)
            def take_row(g):
                dve.wait_ge(w_used, SPLIT + KC * (g + 1))
                dve.tensor_copy(arow[0:4, g % 2, :].rearrange("p (b n) -> p b n", b=2), PS[0:4, 2 * (g % 2):2 * (g % 2) + 2, :])\
                   .then_inc(arow_ready, 1)

            U = Units(U_A0)
            split(U, 0, 8)
            dve.wait_ge(h_ready, 2)
            normalise(0, nrm1, nrm1)
            split(U, 8, 16)
            take_row(0)
            split(U, 16, 32)
            take_row(1)
            split(U, 32, 40)
            normalise(1, nrm1, nrm1)
            split(U, 40, 48)
            take_row(2)
            split(U, 48, 64)
            take_row(3)
            dve.wait_ge(a0_done, 1)
            step(dve.tensor_copy(mod0[:, :, :], PS[:, 4, 0:4 * KC].rearrange("p (j c) -> p j c", c=2)))
            for c in range(2):
                cols(c, 0, mod0[:, 0:KC, c])
                cols(c, 1, mod0[:, KC:2 * KC, c])
            dve.sem_inc(cols_ready, 1)

            dve.wait_ge(xs_ready, 18)
            scratch = nrm1[:, :, :].rearrange("p a (b c n) -> p (a b) c n", b=4, c=2)

            def scaled(k):
                for c in range(2):
                    ins = dve.tensor_scalar(scratch[:, k % 8, c, :], xtok[:, k, c * L:(c + 1) * L],
                                            gsc[:, c, k:k + 1], shc[:, c, k:k + 1], ALU.mult, ALU.add)
                ins.then_inc(spl_ready, 1)

            scaled(0)
            for k in range(KC):
                if k < KC - 1:
                    if k >= 7:
                        dve.wait_ge(xt_ready, k - 6)
                    scaled(k + 1)
                dve.wait_ge(spl_ready, k + 1)
                dve.wait_ge(xh_ready, k + 1)
                dve.tensor_tensor(x1l[:, k, :], scratch[:, k % 8].rearrange("p c n -> p (c n)"), x1h[:, k, :].bitcast(F32), ALU.subtract)\
                   .then_inc(xt_ready, 1)
                if k % 4 == 3:
                    split(Units(U_KV), k // 4, k // 4 + 1)
            split(Units(U_KV), 4, 32)
            split(Units(U_Q), 0, 16)
            dve.wait_ge(ab_high, 1)
            dve.tensor_tensor(abl[:, :, :], abw[:, :, :], abh[:, :, :].bitcast(F32), ALU.subtract).then_inc(ab_split, 1)
            split(Units(U_ZP), 0, 32)

            def flat4(ap):
                return ap.rearrange("p t n -> p (t n)")
            dve.wait_ge(ab_ready, 1)
            dve.wait_ge(c2_loaded, 16 * 6)
            step(dve.tensor_tensor(gt[:, 0], abr[:, :, 0:2 * H], dtb[:].unsqueeze(1).broadcast_to([P, 4, 2 * H]), ALU.add))
            step(dve.tensor_scalar(gt[:, 1], gt[:, 0], -1.0, None, ALU.mult))
            dve.tensor_tensor(gt[:, 1], gt[:, 1], gt[:, 0], ALU.min).then_inc(ex_ready, 1)
            dve.wait_ge(lx_ready, 1)
            step(dve.tensor_scalar(gt[:, 2], gt[:, 1], 2.0, None, ALU.add))
            step(dve.reciprocal(gt[:, 2], gt[:, 2]))
            step(dve.tensor_tensor(gt[:, 2], gt[:, 2], gt[:, 1], ALU.mult))
            step(dve.tensor_tensor(gt[:, 3], gt[:, 2], gt[:, 2], ALU.mult))
            step(dve.tensor_scalar(gt[:, 4], gt[:, 3], 1.0 / 17, None, ALU.mult))
            for odd in (15, 13, 11, 9, 7, 5, 3):
                step(dve.scalar_tensor_tensor(gt[:, 4], gt[:, 4], 1.0 / odd, gt[:, 3], ALU.add, ALU.mult))
            step(dve.scalar_tensor_tensor(gt[:, 4], gt[:, 4], 1.0, gt[:, 2], ALU.add, ALU.mult))
            step(dve.tensor_scalar(gt[:, 0], gt[:, 0], 0.0, None, ALU.max))
            step(dve.scalar_tensor_tensor(gt[:, 4], gt[:, 4], 2.0, gt[:, 0], ALU.mult, ALU.add))
            dve.scalar_tensor_tensor(gt[:, 5], gt[:, 4], -1.0, alog[:].unsqueeze(1).broadcast_to([P, 4, 2 * H]), ALU.mult, ALU.mult)\
               .then_inc(g_ready, 1)
            dve.wait_ge(gam_done, 1)
            q0 = Q[:, 0].rearrange("p t d h -> p t (d h)")
            dve.tensor_copy(q0, PS[:, 5, 0:64].rearrange("p (t n) -> p t n", t=4)).then_inc(gam_ready, 1)
            dve.wait_ge(gam_done, 2)
            dve.wait_ge(gam_ready, 1)
            step(dve.tensor_copy(gt[:, 3], PS[:, 7, 0:64].rearrange("p (t n) -> p t n", t=4)))
            step(dve.tensor_tensor(gt[:, 2], gt[:, 3], q0, ALU.subtract))
            dve.tensor_scalar(gt[:, 2], gt[:, 2], 0.0, None, ALU.min).then_inc(q_dve, 1)
            dve.wait_ge(q_ready, 1)
            step(dve.tensor_scalar(Q[:, 2], Q[:, 5], -1.0, None, ALU.mult))
            step(dve.tensor_tensor(Q[:, 3].rearrange("p t d h -> p t (d h)"), Q[:, 1].rearrange("p t d h -> p t (d h)"), gt[:, 2], ALU.mult))

            with dve.Fori(0, H // 2) as i:
                step.enter(i, 20)
                dve.wait_ge(pair_free, i * 4 + 4)
                step(dve.tensor_copy(cws[:, :, :], convw[:, :, ds(i * 10, 10)]))
                step(dve.tensor_copy(Qs[:, :, :], Q[:, :, :, :, :].rearrange("p q t d h -> p (q t d) h")[:, :, ds(i * 2, 2)]))
                for d in range(2):
                    ins = dve.tensor_copy(sel[0:16, 2 * d:2 * d + 2, :],
                                          ident[0:16, ds(i * 2 + 8 * d, 2)].unsqueeze(2).broadcast_to([16, 2, P]))
                ins.then_inc(sel_ready, 1)
                dve.wait_ge(pair_in, i * 48 + 48)
                for src, dst, kind in ((ck, kT, 1), (cq, qT, 0), (cv, vT, 2)):
                    for n, tap in enumerate((2, 0, 1, 3, 4)):
                        for a in range(2):
                            w = cws[:, kind, 5 * a + tap:5 * a + tap + 1]
                            s3 = src[:, a, :].rearrange("p (s n) -> p s n", n=L)
                            d3 = dst[:, a, :].rearrange("p (s n) -> p s n", n=L)
                            off = tap - 2
                            lo, hi = max(0, -off), L - max(0, off)
                            if n == 0:
                                ins = dve.tensor_scalar(d3, s3, w, None, ALU.mult)
                            else:
                                ins = dve.scalar_tensor_tensor(d3[:, :, lo:hi], s3[:, :, lo + off:hi + off], w, d3[:, :, lo:hi],
                                                               ALU.mult, ALU.add)
                        if n < 4:
                            step(ins)
                        else:
                            ins.then_inc(conv_done, 1)
                ada(0, 0, i)
                dve.wait_ge(nroot, i * 2 + 1)
                dve.tensor_tensor(kT[:, :, :], kT[:, :, :], ck, ALU.mult).then_inc(kqn, 1)
                dve.wait_ge(nroot, i * 2 + 2)
                dve.scalar_tensor_tensor(qT[:, :, :], qT[:, :, :], float(P) ** -0.5, cq, ALU.mult, ALU.mult).then_inc(kqn, 1)
                ada(0, 1, i)
                ada(0, 2, i)
                dve.wait_ge(row_done, i + 1)
                for s in range(4):
                    for q in range(4):
                        t = TILE[q // 2][s]
                        ins = dve.tensor_scalar(X[:, s, q, :], PS[:, 4 + q, t * P:(t + 1) * P],
                                                Qs[:, 2 * t + q // 2, q % 2:q % 2 + 1], 0.0, ALU.subtract, ALU.min)
                ins.then_inc(dif_ready, 1)
                ada(0, 3, i)
                dve.wait_ge(dec_ready, i + 1)
                dve.wait_ge(kk_done, i + 1)
                for s in range(4):
                    for q in range(4):
                        t = TILE[q // 2][s]
                        ins = dve.scalar_tensor_tensor(NM[:, s, q, :], X[:, s, q, :], Qs[:, 8 + 2 * t + q // 2, q % 2:q % 2 + 1],
                                                       PS[:, q % 2, t * P:(t + 1) * P], ALU.mult, ALU.mult)
                    ins.then_inc(nm_ready, 1)
                dve.wait_ge(di_ready, i + 1)
                for s in range(2):
                    for d in range(2):
                        t = TILE[d][2 + s]
                        ins = dve.tensor_tensor(QK[:, s, 2 * d:2 * d + 2, :], DI[:, s, 2 * d:2 * d + 2, :],
                                                PS[:, 2, :].rearrange("p (a t n) -> p a t n", a=2, t=2)[:, :, t, :], ALU.mult)
                ins.then_inc(qk_ready, 1)
                dve.wait_ge(nm_ready, i * 4 + 4)
                for s in range(4):
                    step(dve.tensor_tensor(XT[:, s].rearrange("p (d a) n -> p d a n", d=2),
                                           NM[:, s].rearrange("p (d a) n -> p d a n", d=2),
                                           lmask[:, 0].unsqueeze(2).broadcast_to([P, 2, 2, P]), ALU.mult))
                    dve.scalar_tensor_tensor(XT[:, s], XT[:, s], -1.0, ident[:].unsqueeze(1).broadcast_to([P, 4, P]), ALU.mult, ALU.add)\
                       .then_inc(xT_ready, 1)
                dve.memset(S[:, :, :], 0.0).then_inc(s_ready, 1)
                for lv in range(1, LEVELS):
                    for s in range(4):
                        dve.wait_ge(mm2_done, i * 24 + 4 * (lv - 1) + s + 1)
                        dve.tensor_tensor(XT[:, s], XT[:, s], PS[:, 4 + s, :].rearrange("p (q n) -> p q n", q=4), ALU.subtract)\
                           .then_inc(xT_ready, 1)
                    for k in range(2 * lv + 2, 2 * lv + 4):
                        ada(0, k, i)
                for s in range(4):
                    dve.wait_ge(ks_done, i * 4 + s + 1)
                    for q in range(4):
                        t = TILE[q // 2][s]
                        ins = dve.scalar_tensor_tensor(R[:, q], PS[:, 0, q * P:(q + 1) * P], Qs[:, 16 + 2 * t + q // 2, q % 2:q % 2 + 1],
                                                       vtok[:, q % 2, t, :], ALU.mult, ALU.add)
                    ins.then_inc(r_ready, 1)
                    dve.wait_ge(y_done, i * 4 + s + 1)
                    for q in range(4):
                        t = TILE[q // 2][s]
                        ins = dve.tensor_scalar(VD[:, q], PS[:, 2, q * P:(q + 1) * P], Qs[:, 24 + 2 * t + q // 2, q % 2:q % 2 + 1],
                                                None, ALU.mult)
                    ins.then_inc(vd_ready, 1)
                    dve.wait_ge(ds_done, i * 4 + s + 1)
                    dve.wait_ge(s_ready, i * 5 + s + 1)
                    for q in range(4):
                        t = TILE[q // 2][s]
                        ins = dve.scalar_tensor_tensor(S[:, q], S[:, q], Qs[:, 32 + 2 * t + q // 2, q % 2:q % 2 + 1],
                                                       PS[:, 4, q * P:(q + 1) * P], ALU.mult, ALU.add)
                    ins.then_inc(s_ready, 1)
                    if s == 1:
                        dve.wait_ge(sum_done, i + 1)
                        step(dve.tensor_copy(colbuf[:, ds(i, 1), :], PS[:, 6, 0:KC].unsqueeze(1)))
                        dve.sem_inc(sum_read, 1)
                    if s >= 2:
                        dve.wait_ge(eq_ready, i * 2 + s - 1)
                        dve.wait_ge(ov_done, i * 2 + s - 1)
                        ov = PS[:, 3, :].rearrange("p (q n) -> p q n", q=4)
                        if s == 2:
                            for d in range(2):
                                ins = dve.tensor_tensor(otok[:, TILE[d][s], ds(i * 2, 2), :], EQ[:, 2 * d:2 * d + 2], ov[:, 2 * d:2 * d + 2], ALU.add)
                            ins.then_inc(o_ready, 1)
                        else:
                            step(dve.tensor_tensor(EQ, EQ, ov, ALU.add))
                            dve.wait_ge(o_ready, i * 2 + 1)
                            for d in range(2):
                                o = otok[:, TILE[d][s], ds(i * 2, 2), :]
                                ins = dve.tensor_tensor(o, o, EQ[:, 2 * d:2 * d + 2], ALU.add)
                            ins.then_inc(o_ready, 1)
                dve.wait_ge(o_ready, i * 2 + 2)
                dve.wait_ge(s_ready, i * 5 + 5)
                dve.sem_inc(pair_free, 1)
                step.leave(H // 2)
            dve.wait_ge(pair_free, 20)
            dve.sem_inc(dn_done, 1)

            cols(2, 0, colbuf[:, 1, :])
            cols(2, 1, colbuf[:, 2, :])
            dve.sem_inc(cols_ready, 1)
            dve.wait_ge(ada_summed, 5)
            diagonals(0, 0, 2)

            o2 = otok[:, :, :, :].rearrange("p t h n -> p (t h) n")
            s2 = osq[:, :, :, :].rearrange("p t h n -> p (t h) n")
            step(dve.tensor_tensor(s2, o2, o2, ALU.mult))
            dve.tensor_reduce(so[:], s2, AX.X, ALU.add).then_inc(osum_ready, 1)
            dve.wait_ge(oroot, 1)
            step(dve.reciprocal(ro[:], ro[:]))
            step(dve.tensor_tensor(o2, o2, ro[:].unsqueeze(2).broadcast_to([P, NT * H, P]), ALU.mult))
            dve.wait_ge(e3_loaded, 16 * 5)
            step(dve.tensor_tensor(o2, o2, onorm[:].unsqueeze(1).broadcast_to([P, NT * H, P]), ALU.mult))
            dve.wait_ge(zs_ready, 1)
            dve.tensor_tensor(o2, o2, zt.rearrange("p t (h n) -> p (t h) n", h=H), ALU.mult).then_inc(ya_ready, 1)

            def y_low(c, n, bank, scale):
                dve.wait_ge(yh_ready, n // 2 * 2 + 2)
                src = PS[:, bank + (c % 8) // 2, (c % 2) * L:(c % 2 + 1) * L]
                if scale:
                    step(dve.tensor_scalar(spl[:, 0:L], src, pscale[:, c - 8:c - 7], None, ALU.mult))
                    src = spl[:, 0:L]
                dve.tensor_tensor(xl[:, c, :], src, xh[:, c, :].bitcast(F32), ALU.subtract).then_inc(y_ready, 1)
                dve.wait_ge(y_ready, n + 1)

            for c in range(8):
                y_low(8 + c, c, 4, True)
            for c in range(8):
                y_low(c, 8 + c, 0, False)

            def gated(e_count, done, n, g, b):
                dve.wait_ge(lin_done, done)
                for t in range(NT):
                    w = e_count(t - 1)
                    if not isinstance(w, int) or w >= 1:
                        dve.wait_ge(hx_added, w)
                    dve.tensor_tensor(tmp[:, t, :], PS[:, 2 * (n % 2) + t, :], gate[:, g, b * CB:(b + 1) * CB], ALU.mult)\
                       .then_inc(tmp_ready, 1)

            U = Units(U_OUT)
            dve.wait_ge(bc_done, 1)
            diagonals(3, 0, 5)
            dve.wait_ge(gate_ready, 1)
            for j in range(32):
                split(U, j, j + 1)
                if j == 8:
                    dve.wait_ge(bc_done, 2)
                adas(AT32, j, 4)
                if j % 8 == 3 and j > 8:
                    b = j // 8 - 1
                    gated(lambda off: 2 * b + off, N_OUT + b + 1, N_OUT + b, 0, b)
            gated(lambda off: 6 + off, N_OUT + 4, N_OUT + 3, 0, 3)

            def mid_low(T, tau, buf):
                for t in range(NT):
                    dve.wait_ge(hth_ready, T.tau(tau, 1 + t))
                    hs = (slice(None), buf, slice(4 * (tau % 2), 4 * (tau % 2) + 4), slice(t * P, (t + 1) * P))
                    dve.tensor_tensor(htl[hs], PS[:, 4 + t, :].rearrange("p (c n) -> p c n", c=4), hth[hs].bitcast(F32), ALU.subtract)\
                       .then_inc(ht_ready, 1)

            def mlp(layer, base, n0):
                def down(T, e, n, b):
                    gated(lambda off: T.e(e + b, off), T(n, 1), n, 1, b)

                def units(U, j0, j1, i=None):
                    for j in range(j0, j1):
                        split(U, j, j + 1)
                        if layer == 0 and i is not None and j in AT64:
                            ada(5, AT64.index(j), i)

                U, T = Units(base), Turn(n0, layer)
                dve.wait_ge(gate_ready, 2 if layer == 0 else 4)
                split(U, 0, 5)
                if layer == 0:
                    take_sum(4)
                    cols(4, 0, colbuf[:, 4, :])
                split(U, 5, 16)
                U = Units(base + 16)
                split(U, 0, 2)
                mid_low(T, 0, 0)
                split(U, 2, 8)
                mid_low(T, 1, 0)
                with dve.Fori(0, 3) as i:
                    U, T = Units(base + 16, 64, i), Turn(n0 + 2, layer, i)
                    units(U, 8, 18, i)
                    mid_low(T, 2, 1)
                    units(U, 18, 24, i)
                    down(T, 0, 2, 0)
                    units(U, 24, 26, i)
                    mid_low(T, 3, 1)
                    units(U, 26, 28, i)
                    down(T, 0, 3, 1)
                    units(U, 28, 32, i)
                    down(T, 0, 4, 2)
                    units(U, 32, 36, i)
                    down(T, 0, 5, 3)
                    units(U, 36, 50, i)
                    mid_low(T, 4, 0)
                    units(U, 50, 56, i)
                    down(T, 4, 8, 0)
                    units(U, 56, 58, i)
                    mid_low(T, 5, 0)
                    units(U, 58, 60, i)
                    down(T, 4, 9, 1)
                    units(U, 60, 64, i)
                    if layer == 0:
                        dve.wait_ge(sum_done, i + 6)
                        dve.tensor_copy(colbuf[:, ds(i + 5, 1), :], PS[:, 6, 0:KC].unsqueeze(1)).then_inc(sum_read, 1)
                    down(T, 4, 10, 2)
                    units(U, 64, 68, i)
                    down(T, 4, 11, 3)
                    units(U, 68, 72, i)
                U, T = Units(base + 16 + 192), Turn(n0 + 2, layer, 3)
                if layer == 0:
                    dve.wait_ge(sum_read, 9)
                    cols(3, 0, colbuf[:, 5, :])
                    cols(3, 1, colbuf[:, 6, :])
                    dve.sem_inc(cols_ready, 1)
                    dve.wait_ge(ada_summed, 9)
                    diagonals(7, 1, 2)
                units(U, 8, 18)
                mid_low(T, 2, 1)
                units(U, 18, 24)
                down(T, 0, 2, 0)
                units(U, 24, 26)
                mid_low(T, 3, 1)
                units(U, 26, 28)
                down(T, 0, 3, 1)
                units(U, 28, 32)
                down(T, 0, 4, 2)
                units(U, 32, 36)
                down(T, 0, 5, 3)
                units(U, 36, 40)
                down(T, 4, 6, 0)
                units(U, 40, 44)
                down(T, 4, 7, 1)
                units(U, 44, 48)
                down(T, 4, 8, 2)
                down(T, 4, 9, 3)

            def norm_hx(c):
                normalise(c, hx, nrm)
                dve.wait_ge(cols_ready, c)
                split_low(c, xh, xl, slice(0, L))

            norm_hx(2)
            mlp(0, U_MLP0, N_MLP0)
            norm_hx(3)

            def stats(n):
                dve.wait_ge(v_ready, n - 3)
                for t in range(NT):
                    ins = dve.bn_stats(bst[:, t, n - 4, :], vg[:, t, (n - 4) * CB:(n - 3) * CB])
                return ins

            U = Units(U_OIN)
            for j in range(64):
                split(U, j, j + 1)
                if j == 8:
                    dve.wait_ge(bc_done, 3)
                if j == 36:
                    take_sum(8)
                    cols(4, 1, colbuf[:, 8, :])
                    dve.sem_inc(cols_ready, 1)
                for M in AT_OIN:
                    adas(AT_OIN[M], j, M)
                if j % 8 == 3 and j >= 43:
                    stats(j // 8 - 1)
            step(stats(7))
            for t in range(NT):
                ins = dve.bn_aggr(mv[:, t, :], bst[:, t, :, :].rearrange("p a b -> p (a b)"))
            ins.then_inc(mv_ready, 1)
            dve.wait_ge(lroot, 1)
            step(dve.reciprocal(mv[:, :, 1:2].rearrange("p t o -> p (t o)"), mv[:, :, 1:2].rearrange("p t o -> p (t o)")))
            for g in range(4):
                cs = slice(g * CB, (g + 1) * CB)
                for t in range(NT):
                    ins = dve.tensor_scalar(vg[:, t, cs], vg[:, t, cs], mv[:, t, 0:1], mv[:, t, 1:2], ALU.subtract, ALU.mult)
                step(ins)
                dve.wait_ge(ln_loaded2[g % 2], 32 * (g // 2 + 1))
                for n, op in ((0, ALU.mult), (1, ALU.add)):
                    ins = dve.tensor_tensor(vg[:, :, cs], vg[:, :, cs], lnp[g % 2][:, n, :].unsqueeze(1).broadcast_to([P, NT, CB]), op)
                    if n == 0:
                        step(ins)
                    else:
                        ins.then_inc(vn_norm, 1)
            for g in range(4):
                for t in range(NT):
                    dve.wait_ge(mix_done, 2 * g + t + 1)
                    cs = slice(g * CB, (g + 1) * CB)
                    dve.scalar_tensor_tensor(ug[:, t, cs], PS[:, (2 * g + t) % 4, :], bscol[:, g:g + 1], ug[:, t, cs], ALU.add, ALU.mult)\
                       .then_inc(um_ready, 1)
            for kp in range(8):
                dve.wait_ge(umh_ready, kp + 1)
                dve.tensor_tensor(xl[:, 2 * kp:2 * kp + 2, :].rearrange("p k n -> p (k n)"), PS[:, 4 + kp % 4, :],
                                  xh[:, 2 * kp:2 * kp + 2, :].rearrange("p k n -> p (k n)").bitcast(F32), ALU.subtract).then_inc(uml_ready, 1)
            U = Units(U_OOUT)
            dve.wait_ge(gate_ready, 3)
            for j in range(32):
                split(U, j, j + 1)
                if j == 4:
                    take_sum(9)
                    dve.wait_ge(ada_summed, 11)
                    diagonals(9, 1, 5)
                if j % 8 == 3 and j > 8:
                    b = j // 8 - 1
                    gated(lambda off: 72 + 2 * b + off, N_OOUT + b + 1, N_OOUT + b, 0, b)
            gated(lambda off: 78 + off, N_OOUT + 4, N_OOUT + 3, 0, 3)
            norm_hx(4)
            mlp(1, U_MLP1, N_MLP1)

            for t in range(NT):
                dve.wait_ge(rt_done, 11 + t)
                step(dve.reciprocal(rs[:, 10 + t:11 + t], ss[:, 10 + t:11 + t]))
                dve.wait_ge(fg_loaded, 16)
                dve.scalar_tensor_tensor(fin[:, t, :], hx[:, t, :], rs[:, 10 + t:11 + t], fg[:], ALU.mult, ALU.mult).then_inc(fin_ready, 1)


        @block.tensor
        def _(pe):
            pe.sem_inc(w_used, SPLIT)

            def mm(dst, lhsT, rhs, start=True, stop=True, **kw):
                return pe.matmul(dst, lhsT, rhs, start=start, stop=stop, **kw)

            def tok(U, j0, n, x, last=UPB, part=lambda j, h: 2 * j + h, ready=None, after=None, done=True):
                xa, xb = x
                for j in range(last):
                    pe.wait_ge(w_split, U.u(j0 + j, 1))
                    if ready is not None:
                        pe.wait_ge(ready[0], ready[1] + j + 1)
                    r = (j0 + j) % SPLIT
                    for h in range(UNIT):
                        k = part(j, h)
                        hi, lo = wh[:, r, h * CB:(h + 1) * CB], wl[:, r, h * CB:(h + 1) * CB]
                        for t in range(NT):
                            dst = PS[:, 2 * (n % 2) + t, :]
                            a, b = xa(k, t), xb(k, t)
                            mm(dst, a, hi, start=(j == 0 and h == 0), stop=False)
                            mm(dst, a, lo, start=False, stop=False)
                            ins = mm(dst, b, hi, start=False, stop=(j == last - 1 and h == 1))
                    ins.then_inc(w_used, 1)
                    if after and j in after:
                        after[j]()
                if done:
                    pe.wait_ge(w_used, U.u(j0 + last, SPLIT))
                    pe.sem_inc(lin_done, 1)

            pe.sem_inc(ada_summed, 1)

            def col_sum(M, i=None):
                def count(per, off):
                    return M * per + off if i is None else i * per + M * per + off

                def go():
                    pe.wait_ge(ada_used, count(KC, KC))
                    pe.wait_ge(sum_read, count(1, 1))
                    for k in range(KC):
                        ins = mm(PS[:, 6, k:k + 1], ada_acc[:, k * P:(k + 1) * P], ones[:, 0:1])
                    ins.then_inc(sum_done, 1)
                    pe.wait_ge(sum_done, count(1, 1))
                    pe.sem_inc(ada_summed, 1)
                return go

            def spread(n):
                def go():
                    pe.wait_ge(diag_ready, n + 1)
                    if n == 3:
                        pe.wait_ge(uml_ready, 8)
                    for b in range(4):
                        ins = mm(PS[:, 4 + b, :], ones[:], ada_acc[:, b * CB:(b + 1) * CB])
                    ins.then_inc(bc_done, 1)
                return go

            pe.wait_ge(consts, 16 * 6)
            pe.wait_ge(cs_split, 1)
            with pe.Fori(0, 2) as i:
                for g in range(2):
                    for k in range(KC):
                        pe.wait_ge(w_split, i * 2 * KC + g * KC + k + 1)
                        for b in range(2):
                            for w in (wh, wl):
                                ins = mm(PS[0:4, 2 * g + b, :], chl[:, k, :], w[:, k % SPLIT, b * CB:(b + 1) * CB],
                                         start=(k == 0 and w is wh), stop=(k == KC - 1 and w is wl))
                        ins.then_inc(w_used, 1)
                    pe.wait_ge(arow_ready, i * 2 + g + 1)
                    for j in range(8):
                        for h in range(2):
                            ins = mm(PS[:, 4, ds(i * 32 + 16 * g + 2 * j, 2)], arow[0:4, g, j * P:(j + 1) * P],
                                     ident[0:4, 2 * h:2 * h + 2], start=(h == 0), stop=(h == 1))
                    if g == 0:
                        pe.wait_ge(nrm_ready, i * 2 + 2)
                        for kp in range(KC // 2):
                            pe.wait_ge(xs_ready, i * 8 + kp + 1)
                            for k in (2 * kp, 2 * kp + 1):
                                for t in range(NT):
                                    at = (k % 2) * L + t * P
                                    tr = pe.transpose(PS[:, 6 + kp % 2, at:at + P], nrm1[:, t, k * P:(k + 1) * P], ident[:])
                            tr.then_inc(xp_done, 1)
                    else:
                        ins.then_inc(a0_half, 1)
            pe.wait_ge(a0_half, 2)
            pe.sem_inc(a0_done, 1)

            def transposes(c, src, ready=None):
                pe.wait_ge(nrm_ready, 2 * c + 2)
                for kp in range(KC // 2):
                    w = 8 * c + kp - 3
                    if w >= 1:
                        pe.wait_ge(xt_ready, w)
                    for h in range(2):
                        for t in range(NT):
                            k = 2 * kp + h
                            ins = pe.transpose(PS[:, 4 + kp % 4, h * L + t * P:h * L + (t + 1) * P], src[:, t, k * P:(k + 1) * P], ident[:])
                    ins.then_inc(xp_done, 1)

            def fm(U, f, width):
                p = 4 * (f % 2)
                for j in range(UPB):
                    pe.wait_ge(w_split, U.u(8 * (f % 2) + j, 1))
                    pe.wait_ge(xt_ready, 2 * j + 2)
                    for h in range(UNIT):
                        k = UNIT * j + h
                        for s in range(4):
                            dst = PS[:, p + s, 0:width]
                            c = h * CB + s * P
                            hi, lo = wh[:, j % SPLIT, c:c + P], wl[:, j % SPLIT, c:c + P]
                            mm(dst, hi, x1h[:, k, 0:width], start=(k == 0), stop=False)
                            mm(dst, hi, x1l[:, k, 0:width], start=False, stop=False)
                            ins = mm(dst, lo, x1h[:, k, 0:width], start=False, stop=(k == KC - 1))
                    ins.then_inc(w_used, 1)
                pe.wait_ge(w_used, U.u(8 * (f % 2) + 8, SPLIT))
                pe.sem_inc(fm_done, 1)

            pe.wait_ge(cols_ready, 1)
            with pe.Fori(0, 2) as i:
                for f in range(2):
                    pe.wait_ge(fm_read, i * 2 + f + 1)
                    fm(Units(U_KV, 16, i), f, 2 * L)
            for f in range(2):
                pe.wait_ge(fm_read, 5 + f)
                fm(Units(U_Q), f, L)
            pe.wait_ge(fm_read, 8)

            def x1(t):
                return slice(t * P, (t + 1) * P)
            xx = (lambda k, t: x1h[:, k, x1(t)], lambda k, t: x1l[:, k, x1(t)])
            for n in range(4):
                if n >= 2:
                    pe.wait_ge(acc_free[n % 2], 2 * (n // 2))
                tok(Units(U_ZP), 8 * n, n, xx)
            pe.wait_ge(ab_split, 1)
            for t in range(4):
                dst = PS[:, 4, t * 4 * H:(t + 1) * 4 * H]
                for k in range(KC):
                    mm(dst, x1h[:, k, x1(t)], abh[:, k, :], start=(k == 0), stop=False)
                    mm(dst, x1h[:, k, x1(t)], abl[:, k, :], start=False, stop=False)
                    ins = mm(dst, x1l[:, k, x1(t)], abh[:, k, :], start=False, stop=(k == KC - 1))
            ins.then_inc(ab_done, 1)

            pe.wait_ge(g_ready, 1)
            for t in range(4):
                for d in range(2):
                    c = t * 2 * H + d * H
                    ins = mm(PS[:, 5, c:c + H], incl[:, d, :], gt[:, 5, t, d * H:(d + 1) * H])
            ins.then_inc(gam_done, 1)
            pe.wait_ge(gam_ready, 1)
            for t in range(4):
                for d in range(2):
                    c = t * 2 * H + d * H
                    ins = mm(PS[:, 7, c:c + H], edge[:, d, :], Q[:, 0, t, d, :])
            ins.then_inc(gam_done, 1)
            for t in range(4):
                ins = pe.transpose(PS[0:16, 6, t * P:(t + 1) * P], Q[:, 0, t, :, :].rearrange("p d h -> p (d h)"), ident[:])
            ins.then_inc(gam_done, 1)
            pe.wait_ge(gamT_ready, 1)

            with pe.Fori(0, H // 2) as i:
                pe.wait_ge(pair_free, i * 4 + 4)
                for n, (src, bank) in enumerate(((ck, 0), (cq, 2))):
                    pe.wait_ge(sq_ready2, i * 2 + n + 1)
                    for a in range(2):
                        dst = PS[:, a, :] if n == 0 else PS[:, 2, a * L:(a + 1) * L]
                        ins = mm(dst, ones[:], src[:, a, :])
                    ins.then_inc(nsum_done, 1)
                pe.wait_ge(silu_done, i * 3 + 3)
                for a in range(2):
                    for t in range(4):
                        ins = pe.transpose(PS[:, 6 + a, t * P:(t + 1) * P], vT[:, a, t * P:(t + 1) * P], ident[:])
                ins.then_inc(tok_done, 1)
                pe.wait_ge(kqn, i * 2 + 1)
                for a in range(2):
                    for t in range(4):
                        ins = pe.transpose(PS[:, 4 + a, t * P:(t + 1) * P], kT[:, a, t * P:(t + 1) * P], ident[:])
                ins.then_inc(tok_done, 1)
                for a in range(2):
                    for t in range(4):
                        k = kT[:, a, t * P:(t + 1) * P]
                        mm(PS[:, a, t * P:(t + 1) * P], k, k)
                pe.wait_ge(kqn, i * 2 + 2)
                for a in range(2):
                    for t in range(2):
                        ins = mm(PS[:, 2, a * L + t * P:a * L + (t + 1) * P], kT[:, a, t * P:(t + 1) * P], qT[:, a, t * P:(t + 1) * P])
                ins.then_inc(kk_done, 1)
                pe.wait_ge(sel_ready, i + 1)
                pe.wait_ge(tok_read, i * 2 + 2)
                for q in range(4):
                    ins = mm(PS[:, 4 + q, :], sel[0:16, q, :], gamT[0:16, :])
                ins.then_inc(row_done, 1)

                def flip(lv, s):
                    pe.wait_ge(xT_ready, i * 28 + 4 * lv + s + 1)
                    if lv == 0 and s == 0:
                        pe.wait_ge(qk_ready, i + 1)
                    for q in range(4):
                        ins = pe.transpose(PS[:, s, q * P:(q + 1) * P], XT[:, s, q, :], ident[:])
                    ins.then_inc(tr_done, 1)

                for s in range(4):
                    flip(0, s)
                for lv in range(1, LEVELS):
                    for s in range(4):
                        pe.wait_ge(b_ready, i * 24 + 4 * (lv - 1) + s + 1)
                        pe.wait_ge(x_ready, i * 24 + 4 * (lv - 1) + s + 1)
                        for q in range(4):
                            ins = mm(PS[:, s, q * P:(q + 1) * P], B[:, s, q, :], X[:, s, q, :])
                        ins.then_inc(mm1_done, 1)
                    for s in range(4):
                        pe.wait_ge(p_ready, i * 24 + 4 * (lv - 1) + s + 1)
                        pe.wait_ge(xT_ready, i * 28 + 4 * (lv - 1) + s + 1)
                        for q in range(4):
                            ins = mm(PS[:, 4 + s, q * P:(q + 1) * P], PB[:, s, q, :], XT[:, s, q, :])
                        ins.then_inc(mm2_done, 1)
                    if lv < LEVELS - 1:
                        for s in range(4):
                            flip(lv, s)

                pe.wait_ge(xT_ready, i * 28 + 28)
                for s in range(4):
                    if s == 1:
                        col_sum(0, i)()
                    pe.wait_ge(s_ready, i * 5 + s + 1)
                    for q in range(4):
                        t = TILE[q // 2][s]
                        ins = mm(PS[:, 0, q * P:(q + 1) * P], kT[:, q % 2, t * P:(t + 1) * P], S[:, q])
                    ins.then_inc(ks_done, 1)
                    if s >= 2:
                        if s == 3:
                            pe.wait_ge(eq_ready, i * 2 + 1)
                        for q in range(4):
                            t = TILE[q // 2][s]
                            ins = mm(PS[:, 1, q * P:(q + 1) * P], qT[:, q % 2, t * P:(t + 1) * P], S[:, q])
                        ins.then_inc(qs_done, 1)
                    pe.wait_ge(r_ready, i * 4 + s + 1)
                    for q in range(4):
                        ins = mm(PS[:, 2, q * P:(q + 1) * P], XT[:, s, q, :], R[:, q])
                    ins.then_inc(y_done, 1)
                    pe.wait_ge(vd_ready, i * 4 + s + 1)
                    for q in range(4):
                        t = TILE[q // 2][s]
                        ins = mm(PS[:, 4, q * P:(q + 1) * P], ktok[:, q % 2, t, :], VD[:, q])
                    ins.then_inc(ds_done, 1)
                    pe.wait_ge(vn_ready, i * 4 + s + 1)
                    if s >= 2:
                        if s == 3:
                            pe.wait_ge(o_ready, i * 2 + 1)
                        for q in range(4):
                            ins = mm(PS[:, 3, q * P:(q + 1) * P], QK[:, s - 2, q], VN[:, q])
                        ins.then_inc(ov_done, 1)
                pe.wait_ge(s_ready, i * 5 + 5)
                pe.wait_ge(o_ready, i * 2 + 2)
                pe.sem_inc(pair_free, 1)

            pe.wait_ge(dn_done, 1)
            spread(0)()
            pe.wait_ge(e3_loaded, 16 * 5)
            for c in range(8):
                for t in range(NT):
                    ins = mm(PS[:, c // 2, (c % 2) * L:(c % 2 + 1) * L], pt[:, t, c * P:(c + 1) * P], poolm[:, c // 2, t, :],
                             start=(t == 0), stop=(t == 1))
            ins.then_inc(pool_done, 1)
            pe.wait_ge(poolT_ready, 1)
            pe.wait_ge(gate_ready, 1)
            for c in range(8):
                g = c // 2
                for h in range(2):
                    ins = mm(PS[:, 4 + g, (c % 2) * L:(c % 2 + 1) * L], poolw[:, g, h, (c % 2) * P:(c % 2 + 1) * P], poolT[:, 2 * g + h, :],
                             start=(h == 0), stop=(h == 1))
            ins.then_inc(yb_done, 1)
            pe.wait_ge(ya_ready, 1)
            for h in range(H):
                for t in range(NT):
                    ins = pe.transpose(PS[:, h // 2, (h % 2) * L + t * P:(h % 2) * L + (t + 1) * P], otok[:, t, h, :], ident[:])
            ins.then_inc(ya_done, 1)

            xx = (lambda k, t: xh[:, k, x1(t)], lambda k, t: xl[:, k, x1(t)])
            pe.wait_ge(y_ready, 16)
            for n in range(N_OUT, N_OUT + 4):
                pe.wait_ge(acc_free[n % 2], 2 * (n // 2))
                tok(Units(U_OUT), 8 * (n - N_OUT), n, xx, after={3: spread(1)} if n == N_OUT else None)

            def mlp(layer, base, n0):
                hl = [(lambda k, t, b=b: hth[:, b, k, x1(t)], lambda k, t, b=b: htl[:, b, k, x1(t)]) for b in range(2)]

                def turnover(T, tau):
                    def go():
                        pe.wait_ge(sqr_ready, T.tau(tau, 2))
                        if not (layer == 0 and tau == 0):
                            pe.wait_ge(ht_ready, T.tau(tau, 0))
                        for t in range(NT):
                            for c in range(4):
                                ins = pe.transpose(PS[:, 4 + t, c * P:(c + 1) * P], rbuf[:, t, c * P:(c + 1) * P], ident[:])
                            ins.then_inc(mt_done, 1)
                    return go

                def up(U, T, j, n, **kw):
                    pe.wait_ge(acc_free[n % 2], T.free(n))
                    tok(U, j, n, xx, **kw)

                def down(U, T, j, n, buf, after=None):
                    pe.wait_ge(acc_free[n % 2], T.free(n))
                    tok(U, j, n, hl[buf], last=SK // UNIT, after=after)

                def pair(U, T, j0, n, tau, buf):
                    up(U, T, j0, n)
                    up(U, T, j0 + 8, n + 1, after={4: turnover(T, tau)})
                    pe.wait_ge(ht_ready, T.tau(tau, 0))
                    down(U, T, j0 + 16, n + 2, 1 - buf)
                    down(U, T, j0 + 20, n + 3, 1 - buf, after={0: turnover(T, tau + 1)})
                    if layer == 0 and T.i is not None and not isinstance(T.i, int) and tau == 4:
                        down(U, T, j0 + 24, n + 4, 1 - buf, after={1: col_sum(5, T.i)})
                    else:
                        down(U, T, j0 + 24, n + 4, 1 - buf)
                    down(U, T, j0 + 28, n + 5, 1 - buf)

                U, T = Units(base), Turn(n0, layer)
                up(U, T, 0, 0, ready=(xt_ready, 16 if layer == 0 else 32), after={0: col_sum(4)} if layer == 0 else None)
                up(U, T, 8, 1, after={4: turnover(T, 0)})
                U, T = Units(base + 16), Turn(n0 + 2, layer)
                pe.wait_ge(sqr_ready, T.tau(1, 2))
                turnover(T, 1)()
                with pe.Fori(0, 3) as i:
                    U, T = Units(base + 16, 64, i), Turn(n0 + 2, layer, i)
                    pair(U, T, 0, 0, 2, 1)
                    pair(U, T, 32, 6, 4, 0)
                U, T = Units(base + 16 + 192), Turn(n0 + 2, layer, 3)
                pair(U, T, 0, 0, 2, 1)
                pe.wait_ge(ht_ready, T.tau(4, 0))
                for b in range(4):
                    down(U, T, 32 + 4 * b, 6 + b, 1)

            transposes(2, nrm)
            mlp(0, U_MLP0, N_MLP0)
            transposes(3, nrm)

            for n in range(N_OIN, N_OIN + 8):
                b = n - N_OIN
                pe.wait_ge(acc_free[n % 2], 2 * (n // 2))
                tok(Units(U_OIN), 8 * b, n, xx, ready=(xt_ready, 24) if b == 0 else None, after={1: {0: spread(2)}, 4: {0: col_sum(8)}}.get(b))
            pe.wait_ge(ws_loaded, 16)
            pe.wait_ge(acc_free[0], 2 * 32)
            pe.wait_ge(acc_free[1], 2 * 32)
            for g in range(4):
                pe.wait_ge(vn_norm, g + 1)
                for t in range(NT):
                    m = 2 * g + t
                    if m >= 4:
                        pe.wait_ge(um_ready, m - 3)
                    mm(PS[:, m % 4, :], wsT[:, g, :], vg[:, t, g * CB:(g + 1) * CB]).then_inc(mix_done, 1)
            for kp in range(8):
                pe.wait_ge(um_ready, 2 * (kp // 2) + 2)
                if kp >= 4:
                    pe.wait_ge(uml_ready, kp - 3)
                for h in range(2):
                    for t in range(NT):
                        k = 2 * kp + h
                        ins = pe.transpose(PS[:, 4 + kp % 4, h * L + t * P:h * L + (t + 1) * P], ug[:, t, k * P:(k + 1) * P], ident[:])
                ins.then_inc(um_done, 1)
            for n in range(N_OOUT, N_OOUT + 4):
                b = n - N_OOUT
                if b == 0:
                    pe.wait_ge(um_ready, 8)
                pe.wait_ge(acc_free[n % 2], 2 * (n // 2))
                tok(Units(U_OOUT), 8 * b, n, xx, ready=(uml_ready, 0) if b == 0 else None, after={0: col_sum(9), 5: spread(3)} if b == 0 else None)
            transposes(4, nrm)
            mlp(1, U_MLP1, N_MLP1)


def kernel(**inputs):
    import numpy as np
    import concourse.bacc as bacc
    from concourse.bass_utils import run_bass_kernel_spmd as run

    f = {k: np.ascontiguousarray(v) for k, v in inputs.items()}

    def cols(a, n):
        a = np.asarray(a)
        return np.ascontiguousarray(np.moveaxis(a.reshape(a.shape[:-1] + (n, P)), -1, 0))

    arrays = {name: f[name] for name in ("x", "ctx", "ada_w", "ada_b", "mlp_w1", "mlp_w2", "ev_w_in", "ev_dt_bias", "ev_a_log",
                                         "ev_onorm_g", "ev_w_out", "od_w_in", "od_ln_g", "od_ln_b", "od_w_out", "final_g")}
    arrays["ccol"] = np.ascontiguousarray(np.stack([cols(f["c"][0], KC), cols(f["c_ctx"], KC)], -1))
    arrays["adab"] = cols(f["ada_b"].reshape(12, D), KC)
    arrays["gcol"] = cols(np.stack([f["norm1_g"], f["norm2_g"]], 1).reshape(4, D), KC)
    arrays["bscol"] = np.ascontiguousarray(f["od_bs"][0].T)
    arrays["convw"] = np.ascontiguousarray(f["ev_conv_w"][0].reshape(5, 3, H, P).transpose(3, 1, 2, 0).reshape(P, 3, H * 5))
    arrays["poolw"] = np.ascontiguousarray(f["ev_pool_w"][0].reshape(4, 2, P, 2 * P).transpose(2, 0, 1, 3))
    arrays["pscale"] = cols(f["ev_pool_scale"][0], 8)
    arrays["wsT"] = np.ascontiguousarray(f["od_ws"][0].transpose(2, 0, 1))
    j, i = np.meshgrid(np.arange(P), np.arange(P), indexing="ij")
    arrays["ident"] = np.eye(P, dtype=np.float32)
    arrays["ones"] = np.ones((P, P), np.float32)
    arrays["incl"] = np.stack([i >= j, i <= j], 1).astype(np.float32)
    arrays["edge"] = np.stack([j == P - 1, j == 0], 1).astype(np.float32)
    lv = [((i > j) & (i >> (v + 1) == j >> (v + 1)) & (i >> v != j >> v)).astype(np.float32) for v in range(LEVELS)]
    arrays["lmask"] = np.ascontiguousarray(np.stack([np.stack([m, m.T], 1) for m in lv], 1))
    t = np.arange(L)
    pm = []
    for r in (1, 2, 4, 8):
        hi, lo = np.minimum(t + r + 1, L), np.maximum(t - r, 0)
        m = ((t[None] >= lo[:, None]) & (t[None] < hi[:, None])) / (hi - lo)[:, None].astype(np.float32) - np.eye(L)
        pm.append(m.T.reshape(2, P, L))
    arrays["poolm"] = np.ascontiguousarray(np.stack(pm).transpose(2, 0, 1, 3).astype(np.float32))
    nf = D // 4
    omega = (1.0 / (10000.0 ** (np.arange(nf, dtype=np.float32) / np.float32(nf)))).astype(np.float32)
    ar = (t // 64).astype(np.float32)[:, None] * omega
    ac = (t % 64).astype(np.float32)[:, None] * omega
    arrays["pos"] = np.concatenate([np.sin(ar), np.cos(ar), np.sin(ac), np.cos(ac)], -1).astype(np.float32)

    nc = bacc.Bacc("TRN2", target_bir_lowering=False, num_devices=1)
    A = {n: nc.dram_tensor("in_" + n, a.shape, F32, kind="ExternalInput").ap() for n, a in arrays.items()}
    out = nc.dram_tensor("out", (1, L, D), F32, kind="ExternalOutput").ap()
    build(nc, A, out)
    r = run(nc, [{"in_" + n: a for n, a in arrays.items()}], core_ids=[0])
    return r.results[0]["out"]
```

```python
import concourse.bass as bass
from concourse import mybir
from contextlib import ExitStack

F32 = mybir.dt.float32
F32R = mybir.dt.float32r
ALU = mybir.AluOpType
ACT = mybir.ActivationFunctionType
AX = mybir.AxisListType
ds = bass.ds

P = 128
D = 2048
KC = D // P
L = 256
NT = L // P
CB = 512
H = 8
QKV = 3 * H * P
EV_IN = QKV + 4 * H + 2 * H * P
ZP0 = QKV + 4 * H
FF = 4 * D
SLAB = 1024
SK = SLAB // P
SLABS = FF // SLAB
EPS = 1e-6
LEVELS = 7
UNIT = 2
UPB = KC // UNIT
RAW = 8
SPLIT = 4

U_A0, U_KV, U_Q, U_ZP, U_OUT, U_MLP0 = 0, 64, 96, 112, 144, 176
U_OIN, U_OOUT, U_MLP1 = 432, 496, 528
N_ZP, N_OUT, N_MLP0, N_OIN, N_OOUT, N_MLP1 = 0, 4, 8, 56, 64, 68

TILE = [[2, 3, 0, 1], [3, 2, 1, 0]]


class Units:

    def __init__(self, base, step=0, i=None):
        self.base, self.step, self.i = base, step, i

    def u(self, j, off=0):
        c = self.base + j + off
        return c if self.i is None else self.i * self.step + c

    def r16(self, j, off=0):
        c = 16 * ((self.base + j) // RAW + off)
        return c if self.i is None else self.i * (16 * self.step // RAW) + c


class Chain:

    def __init__(self, eng, sem):
        self.eng, self.sem, self.n, self.base = eng, sem, 0, 0

    def __call__(self, ins):
        self.n += 1
        ins.then_inc(self.sem, 1)
        self.eng.wait_ge(self.sem, self.base + self.n)

    def enter(self, i, per):
        self.n0, self.per = self.n, per
        self.base, self.n = i * per + self.n0, 0

    def leave(self, turns):
        assert self.n == self.per, f"{self.n} steps in a turn, not {self.per}"
        self.n, self.base = self.n0 + turns * self.per, 0

class Turn:

    def __init__(self, n0, layer, i=None):
        self.n0, self.layer, self.i = n0, layer, i

    def add(self, c, per):
        return c if self.i is None else self.i * per + c

    def n(self, n, off):
        return self.add(self.n0 + n + off, 12)

    __call__ = n

    def free(self, n):
        return self.add(2 * ((self.n0 + n) // 2), 12)

    def tau(self, tau, off):
        return self.add(32 * self.layer + 2 * tau + off, 8)

    def e(self, e, off):
        return self.add(8 + 72 * self.layer + 2 * e + off, 16)


def build(nc, A, out):
    stack = ExitStack()
    with stack:
        def sem(name):
            return stack.enter_context(nc.semaphore(name))

        def dram(name, shape):
            return nc.dram_tensor(name, shape, F32, kind="Internal").ap()

        def sbuf(where, name, shape, dt=F32):
            return where.enter_context(nc.sbuf_tensor(name, [P] + shape, dt))

        raw = sbuf(stack, "raw", [RAW, UNIT * CB])
        wh = sbuf(stack, "wh", [SPLIT, UNIT * CB], F32R)
        wl = sbuf(stack, "wl", [SPLIT, UNIT * CB], F32R)
        eab = ExitStack()
        abh = sbuf(eab, "abh", [KC, 4 * H], F32R)
        abl = sbuf(eab, "abl", [KC, 4 * H], F32R)
        eab.close()
        ada_raw = sbuf(stack, "ada_raw", [2, D])
        ada_acc = sbuf(stack, "ada_acc", [D])
        gate = sbuf(stack, "gate", [2, D])
        ident = sbuf(stack, "ident", [P])
        ones = sbuf(stack, "ones", [P])
        ccol = sbuf(stack, "ccol", [KC, 2])
        csil = sbuf(stack, "csil", [KC, 2])
        chl = sbuf(stack, "chl", [KC, 4], F32R)
        mod0 = sbuf(stack, "mod0", [2 * KC, 2])
        adab = sbuf(stack, "adab", [12, KC])
        gcol = sbuf(stack, "gcol", [4, KC])
        shc = sbuf(stack, "shc", [5, KC])
        gsc = sbuf(stack, "gsc", [5, KC])
        eps = sbuf(stack, "eps", [1])
        ss = sbuf(stack, "ss", [16])
        rs = sbuf(stack, "rs", [16])
        bscol = sbuf(stack, "bscol", [4])
        colbuf = sbuf(stack, "colbuf", [10, KC])
        spl = sbuf(stack, "spl", [512])
        PS = stack.enter_context(nc.psum_tensor("PS", [P, 8, 512], F32))

        late = ExitStack()
        abr = sbuf(late, "abr", [4, 4 * H])
        dtb = sbuf(late, "dtb", [2 * H]); alog = sbuf(late, "alog", [2 * H])
        gt = sbuf(late, "gt", [6, 4, 2 * H])
        Q = sbuf(late, "Q", [6, 4, 2, H])
        gamT = sbuf(late, "gamT", [4 * P])
        incl = sbuf(late, "incl", [2, P])
        edge = sbuf(late, "edge", [2, P])
        convw = sbuf(late, "convw", [3, H * 5])

        e1 = ExitStack()
        x1h = sbuf(e1, "x1h", [KC, 2 * L], F32R)
        e0 = ExitStack()
        xtok = sbuf(e0, "xtok", [KC, 2 * L])
        e0.close()
        x1l = sbuf(e1, "x1l", [KC, 2 * L], F32R)
        nrm1 = sbuf(e1, "nrm1", [2, D])
        stage = nrm1[:, :, :].rearrange("p a (b n) -> p (a b) n", n=CB)
        ea = ExitStack()
        arow = sbuf(ea, "arow", [2, 1024])
        ea.close()
        cst = sbuf(e1, "cst", [4, 2 * L])
        abw = spl[:].rearrange("p (k n) -> p k n", k=KC)
        e1.close()

        otok = sbuf(late, "otok", [NT, H, P])
        e2 = ExitStack()
        Qs = sbuf(e2, "Qs", [48, 2])
        sel = sbuf(e2, "sel", [4, P])
        lmask = sbuf(e2, "lmask", [LEVELS, 2, P])
        cbuf = sbuf(e2, "cbuf", [2560])
        ck = cbuf[:, 0:1024].rearrange("p (a n) -> p a n", a=2)
        cv = cbuf[:, 1024:2048].rearrange("p (a n) -> p a n", a=2)
        cq = cbuf[:, 2048:2560].rearrange("p (a n) -> p a n", a=2)
        B = cbuf[:, 0:2048].rearrange("p (s q n) -> p s q n", s=4, q=4)
        qT = sbuf(e2, "qT", [2, L]); kT = sbuf(e2, "kT", [2, 2 * L]);
        ktok = sbuf(e2, "ktok", [2, 4, P]); vtok = sbuf(e2, "vtok", [2, 4, P])
        X = sbuf(e2, "X", [4, 4, P])
        NM = sbuf(e2, "NM", [4, 4, P])
        XT = sbuf(e2, "XT", [4, 4, P])
        PB = sbuf(e2, "PB", [4, 4, P])
        QK = sbuf(e2, "QK", [2, 4, P]); DI = sbuf(e2, "DI", [2, 4, P])
        S = sbuf(e2, "S", [4, P])
        R, VN, VD, EQ = (PB[:, n] for n in range(4))
        e2.close()

        e3 = ExitStack()
        poolT = sbuf(e3, "poolT", [8, L]); osq = sbuf(e3, "osq", [NT, H, P])
        e3.close()
        late.close()
        tail = ExitStack()
        rbuf = sbuf(tail, "rbuf", [NT, CB])
        tmp = sbuf(tail, "tmp", [NT, CB])
        hx = sbuf(tail, "hx", [NT, D])
        xh = sbuf(tail, "xh", [KC, L], F32R)
        xl = sbuf(tail, "xl", [KC, L], F32R)
        b1 = ExitStack()
        zp = sbuf(b1, "zp", [2, NT, H * P])
        zt, pt = zp[:, 0], zp[:, 1]
        onorm = sbuf(b1, "onorm", [P])
        so = sbuf(b1, "so", [NT * H]); ro = sbuf(b1, "ro", [NT * H])
        poolm = sbuf(b1, "poolm", [4, 2, L])
        poolw = sbuf(b1, "poolw", [4, 2, L])
        pscale = sbuf(b1, "pscale", [8])
        b1.close()
        b2 = ExitStack()
        nrm = sbuf(b2, "nrm", [NT, D])
        b2.close()
        b3 = ExitStack()
        hth = sbuf(b3, "hth", [2, SK, L], F32R)
        htl = sbuf(b3, "htl", [2, SK, L], F32R)
        dg = sbuf(b3, "dg", [KC, P])
        b3.close()
        b4 = ExitStack()
        ug = sbuf(b4, "ug", [NT, D])
        vg = sbuf(b4, "vg", [NT, D])
        wsT = sbuf(b4, "wsT", [4, P])
        bst = sbuf(b4, "bst", [NT, 4, 6])
        mv = sbuf(b4, "mv", [NT, 2])
        b4.close()
        b5 = ExitStack()
        fin = sbuf(b5, "fin", [NT, D])
        fg = sbuf(b5, "fg", [D])
        b5.close()
        tail.close()
        lnp = (rbuf, tmp)

        s_qT, s_kT, s_vT = dram("s_q", [H, P, L]), dram("s_k", [H, P, 2 * L]), dram("s_v", [H, P, 2 * L])
        s_zp = dram("s_zp", [2, NT, P, H * P])

        consts = sem("consts")
        small_loaded = sem("small_loaded")
        lmask_loaded = sem("lmask_loaded")
        eps_ready = sem("eps_ready")
        w_loaded = [sem(f"w_loaded{r}") for r in range(RAW)]
        w_high = sem("w_high")
        w_split = sem("w_split")
        w_used = sem("w_used")
        lin_done = sem("lin_done")
        acc_free = [sem("acc_free0"), sem("acc_free1")]
        csil_ready = sem("csil_ready")
        cs_high, cs_split = sem("cs_high"), sem("cs_split")
        arow_ready = sem("arow_ready")
        a0_half, a0_done = sem("a0_half"), sem("a0_done")
        cols_ready = sem("cols_ready")
        ada_loaded = [sem("ada_loaded0"), sem("ada_loaded1")]
        ada_used = sem("ada_used")
        ada_summed = sem("ada_summed")
        sum_done, sum_read = sem("sum_done"), sem("sum_read")
        diag_ready, bc_done, gate_ready = sem("diag_ready"), sem("bc_done"), sem("gate_ready")
        h_loaded = [sem("h_loaded0"), sem("h_loaded1")]
        pos_loaded, h_ready = sem("pos_loaded"), sem("h_ready")
        sq_done, rt_done, nrm_ready = sem("sq_done"), sem("rt_done"), sem("nrm_ready")
        xp_done = sem("xp_done")
        xs_ready, spl_ready = sem("xs_ready"), sem("spl_ready")
        xh_ready, xt_ready = sem("xh_ready"), sem("xt_ready")
        fm_done, fm_read = sem("fm_done"), sem("fm_read")
        conv_done, silu_done = sem("conv_done"), sem("silu_done")
        fm_stored = [sem("fm_stored0"), sem("fm_stored1")]
        zp_stored = [sem("zp_stored0"), sem("zp_stored1")]
        ab_loaded, ab_high, ab_split = sem("ab_loaded"), sem("ab_high"), sem("ab_split")
        ab_done, abT_ready = sem("ab_done"), sem("abT_ready")
        abr_done, ab_ready = sem("abr_done"), sem("ab_ready")
        ex_ready, lx_ready, g_ready = sem("ex_ready"), sem("lx_ready"), sem("g_ready")
        gam_done, gam_ready, gamT_ready = sem("gam_done"), sem("gam_ready"), sem("gamT_ready")
        q_dve, q_ready = sem("q_dve"), sem("q_ready")
        pair_in, pair_free = sem("pair_in"), sem("pair_free")
        squares_ready, nsum_done = sem("squares_ready"), sem("nsum_done")
        norm_log, norm_root, kq_normed = sem("norm_log"), sem("norm_root"), sem("kq_normed")
        tok_done, tok_read = sem("tok_done"), sem("tok_read")
        sel_ready, row_done = sem("sel_ready"), sem("row_done")
        kk_done = sem("kk_done")
        dif_ready, dec_ready = sem("dif_ready"), sem("dec_ready")
        di_ready, nm_ready, qk_ready = sem("di_ready"), sem("nm_ready"), sem("qk_ready")
        b_ready, mm1_done, p_ready, mm2_done = sem("b_ready"), sem("mm1_done"), sem("p_ready"), sem("mm2_done")
        xT_ready, tr_done, x_ready = sem("xT_ready"), sem("tr_done"), sem("x_ready")
        ks_done, r_ready, y_done = sem("ks_done"), sem("r_ready"), sem("y_done")
        vn_ready, vd_ready, ds_done, s_ready = sem("vn_ready"), sem("vd_ready"), sem("ds_done"), sem("s_ready")
        qs_done, eq_ready, ov_done, o_ready = sem("qs_done"), sem("eq_ready"), sem("ov_done"), sem("o_ready")
        dn_done = sem("dn_done")
        branch_loaded = sem("branch_loaded")
        pool_done, poolT_ready, yb_done = sem("pool_done"), sem("poolT_ready"), sem("yb_done")
        osum_ready, oroot, zs_ready = sem("osum_ready"), sem("oroot"), sem("zs_ready")
        ya_ready, ya_done = sem("ya_ready"), sem("ya_done")
        yh_ready, y_ready = sem("yh_ready"), sem("y_ready")
        hx_loaded, hx_ready = sem("hx_loaded"), sem("hx_ready")
        tmp_ready, hx_added = sem("tmp_ready"), sem("hx_added")
        relu_ready, sqr_ready, mt_done = sem("relu_ready"), sem("sqr_ready"), sem("mt_done")
        hth_ready, ht_ready = sem("hth_ready"), sem("ht_ready")
        v_ready, mv_ready, lroot, v_normed = sem("v_ready"), sem("mv_ready"), sem("lroot"), sem("v_normed")
        ln_loaded = [sem("ln_loaded0"), sem("ln_loaded1")]
        ws_loaded, mix_done = sem("ws_loaded"), sem("mix_done")
        um_ready, um_done = sem("um_ready"), sem("um_done")
        umh_ready, uml_ready = sem("umh_ready"), sem("uml_ready")
        fg_loaded, fin_ready, stored = sem("fg_loaded"), sem("fin_ready"), sem("stored")
        act_step, dve_step = sem("act_step"), sem("dve_step")

        block = stack.enter_context(nc.Block())

        AT_OUT = [4 + 7 * k // 4 for k in range(16)]
        AT64 = [8 + 3 * k for k in range(16)]
        AT_TAIL = [8 + 5 * k // 2 for k in range(16)]
        AT_OIN = {9: [13 + 2 * k for k in range(16)]}
        ADA = [(0, 2), (0, 3), (0, 4), (0, 5), (1, 3), (1, 0), (1, 1), (1, 2), (1, 4), (1, 5)]
        HX = {2: 8, 3: 72, 4: 80, 5: 144}

        def halves(ap, lv, which):
            return ap.rearrange("p (b h w) -> p b h w", h=2, w=2 ** lv)[:, :, which, :]

        def load_unit(sp, U, j, src):
            sp.dma_start(raw[:, j % RAW, :].rearrange("p (k n) -> p k n", k=UNIT),
                         src.rearrange("(k p) n -> p k n", p=P)).then_inc(w_loaded[j % RAW], 16)

        def ada_rows(M, k):
            layer, part = ADA[M]
            return A["ada_w"][layer, k * P:(k + 1) * P, part * D:(part + 1) * D]

        @block.sync
        def _(sp):
            for dst, name in ((ident[:], "ident"), (ones[:], "ones"), (ccol[:, :, :], "ccol"), (adab[:, :, :], "adab"),
                              (gcol[:, :, :], "gcol"), (bscol[:], "bscol")):
                sp.dma_start(dst, A[name]).then_inc(consts, 16)

            def load_ada(used, k, src):
                if used is not None:
                    sp.wait_ge(ada_used, used)
                sp.dma_start(ada_raw[:, k % 2, :], src).then_inc(ada_loaded[k % 2], 16)

            def a0(g, k, wait):
                if wait is not None:
                    sp.wait_ge(w_split, wait)
                sp.dma_start(raw[:, k % RAW, :], A["ada_w"][0, k * P:(k + 1) * P, ds(g * 1024, 1024)])\
                  .then_inc(w_loaded[k % RAW], 16)

            for k in range(KC):
                a0(0, k, k - 7 if k >= RAW else None)
            with sp.Fori(1, 4) as g:
                for k in range(KC):
                    a0(g, k, g * KC + k - 7)

            w_in = A["ev_w_in"][0]
            with sp.Fori(0, 4) as b:
                U = Units(U_KV, UPB, b)
                for j in range(UPB):
                    sp.wait_ge(w_split, U.u(j, -7))
                    load_unit(sp, U, j, w_in[j * UNIT * P:(j + 1) * UNIT * P, ds(b * CB + H * P, CB)])

            def phase(base, blocks, src, at=None, units=UPB):
                U = Units(base)
                for b in range(blocks):
                    for c in range(units):
                        j = b * units + c
                        sp.wait_ge(w_split, U.u(j, -7))
                        load_unit(sp, U, j, src(b, c))
                        for M in at or ():
                            for k in range(KC):
                                if at[M][k] == j:
                                    load_ada(16 * M + k - 1, k, ada_rows(M, k))

            def rows(w, c):
                return w[c * UNIT * P:(c + 1) * UNIT * P]

            phase(U_Q, 2, lambda b, c: rows(w_in, c)[:, b * CB:(b + 1) * CB])
            phase(U_ZP, 4, lambda b, c: rows(w_in, c)[:, ZP0 + b * CB:ZP0 + (b + 1) * CB])

            def heads(a):
                for dst, src in ((ck, s_kT), (cq, s_qT), (cv, s_vT)):
                    sp.dma_start(dst, src[a, :, :].rearrange("h p n -> p h n")).then_inc(pair_in, 16)

            sp.wait_ge(h_ready, 2)
            sp.wait_ge(ab_done, 1)
            for k in range(2):
                load_ada(None, k, ada_rows(0, k))
            for p in range(2):
                sp.wait_ge(fm_stored[p], 16 * 3)
                sp.wait_ge(zp_stored[p], 16 * 2)
            heads(slice(0, 2))
            for k in range(2, KC):
                load_ada(k - 1, k, ada_rows(0, k))
            with sp.Fori(1, 4) as i:
                for k in range(2):
                    load_ada(i * KC + k - 1, k, A["ada_w"][0, k * P:(k + 1) * P, ds(i * D + 2 * D, D)])
                sp.wait_ge(mm1_done, i * 24)
                heads(ds(i * 2, 2))
                for k in range(2, KC):
                    load_ada(i * KC + k - 1, k, A["ada_w"][0, k * P:(k + 1) * P, ds(i * D + 2 * D, D)])
            phase(U_OUT, 4, lambda b, c: rows(A["ev_w_out"][0], c)[:, b * CB:(b + 1) * CB], {4: AT_OUT})

            def mlp(layer, base, ada):
                w1, w2 = A["mlp_w1"][layer], A["mlp_w2"][layer]

                def up(U, j0, slab, b):
                    for c in range(UPB):
                        j = j0 + 8 * b + c
                        sp.wait_ge(w_split, U.u(j, -7))
                        load_unit(sp, U, j, w1[c * UNIT * P:(c + 1) * UNIT * P, ds(slab * SLAB + b * CB, CB)])
                        yield j

                def down(U, j0, slab, b):
                    for c in range(SK // UNIT):
                        j = j0 + 4 * b + c
                        sp.wait_ge(w_split, U.u(j, -7))
                        load_unit(sp, U, j, w2[ds(slab * SLAB + c * UNIT * P, UNIT * P), b * CB:(b + 1) * CB])
                        yield j

                def turn(U, slab, i, two):
                    for h in range(2):
                        for b in range(2 if (two or h == 0) else 0):
                            yield from up(U, 32 * h, slab + h + 1, b)
                        for b in range(4):
                            yield from down(U, 32 * h + (16 if (two or h == 0) else 0), slab + h, b)

                U = Units(base)
                for b in range(2):
                    for _ in up(U, 0, 0, b):
                        pass
                with sp.Fori(0, 3) as i:
                    for j in turn(Units(base + 16, 64, i), i * 2, i, True):
                        if ada and j in AT64:
                            k = AT64.index(j)
                            load_ada(i * KC + 5 * KC + k - 1, k,
                                     A["ada_w"][1, k * P:(k + 1) * P, ds(i * D, D)])
                for j in turn(Units(base + 16 + 192), 6, None, False):
                    if ada and j in AT_TAIL:
                        k = AT_TAIL.index(j)
                        load_ada(16 * 8 + k - 1, k, ada_rows(8, k))

            mlp(0, U_MLP0, True)
            phase(U_OIN, 8, lambda b, c: rows(A["od_w_in"][0], c)[:, b * CB:(b + 1) * CB], AT_OIN)
            phase(U_OOUT, 4, lambda b, c: rows(A["od_w_out"][0], c)[:, b * CB:(b + 1) * CB])
            mlp(1, U_MLP1, False)
            for t in range(NT):
                sp.wait_ge(fin_ready, t + 1)
                sp.dma_start(out[0, t * P:(t + 1) * P, :], fin[:, t, :]).then_inc(stored, 16)
            sp.wait_ge(stored, 16 * NT)

        @block.scalar
        def _(act):
            step = Chain(act, act_step)
            act.sem_inc(fm_read, 2)

            def high(U, j):
                act.wait_ge(w_loaded[j % RAW], U.r16(j, 1))
                act.wait_ge(w_used, U.u(j, 1))
                act.copy(wh[:, j % SPLIT, :], raw[:, j % RAW, :]).then_inc(w_high, 1)

            def highs(U, *js):
                for j in range(*js):
                    high(U, j)

            for t in range(NT):
                act.dma_start(nrm1[:, t, :], A["x"][0, t * P:(t + 1) * P, :]).then_inc(h_loaded[t], 16)
                act.dma_start(ada_raw[:, t, :], A["pos"][t * P:(t + 1) * P, :]).then_inc(pos_loaded, 16)
            act.dma_start(abw, A["ev_w_in"][0][:, QKV:QKV + 4 * H].rearrange("(k p) n -> p k n", p=P))\
               .then_inc(ab_loaded, 16)
            for dst, name in ((incl[:, :, :], "incl"), (edge[:, :, :], "edge"), (convw[:, :, :], "convw")):
                act.dma_start(dst, A[name]).then_inc(small_loaded, 16)
            for dst, name in ((dtb[:], "ev_dt_bias"), (alog[:], "ev_a_log")):
                act.dma_start(dst, A[name].rearrange("o d h -> (o d h)").partition_broadcast(P)).then_inc(small_loaded, 16)
            act.wait_ge(consts, 16 * 6)
            act.activation(csil[:, :, :], ccol[:, :, :], ACT.Silu).then_inc(csil_ready, 1)
            act.wait_ge(csil_ready, 1)
            act.copy(chl[:, :, 0:2], csil[:, :, :]).then_inc(cs_high, 1)
            act.sem_inc(xs_ready, 2)

            def root(c, t, src, junk):
                col = 2 * c + t
                act.activation(junk, src, ACT.Square, accum_out=ss[:, col:col + 1]).then_inc(sq_done, 1)
                act.wait_ge(sq_done, col + 1)
                act.activation(ss[:, col:col + 1], ss[:, col:col + 1], ACT.Sqrt, bias=eps[:, 0:1], scale=1.0 / D)\
                   .then_inc(rt_done, 1)

            def roots1(c):
                for t in range(NT):
                    if c == 0:
                        act.wait_ge(h_ready, t + 1)
                    else:
                        act.wait_ge(h_loaded[t], 32)
                    root(c, t, nrm1[:, t, :].rearrange("p (a n) -> p a n", n=L), xtok[:, 0:8, c * L:(c + 1) * L])

            def take_tokens(c):
                for kp in range(KC // 2):
                    act.wait_ge(xp_done, 8 * c + kp + 1)
                    act.copy(xtok[:, 2 * kp:2 * kp + 2, c * L:(c + 1) * L],
                             PS[:, 6 + kp % 2, :].rearrange("p (k n) -> p k n", k=2)).then_inc(xs_ready, 1)

            U = Units(U_A0)
            act.wait_ge(eps_ready, 1)
            highs(U, 0, 6)
            roots1(0)
            highs(U, 6, 20)
            take_tokens(0)
            for t in range(NT):
                act.dma_start(nrm1[:, t, :], A["ctx"][0, t * P:(t + 1) * P, :]).then_inc(h_loaded[t], 16)
            highs(U, 20, 36)
            roots1(1)
            highs(U, 36, 52)
            take_tokens(1)
            highs(U, 52, 64)

            def split_high(c, dst, cols):
                for kp in range(KC // 2):
                    act.wait_ge(xp_done, 8 * c + kp + 1)
                    for h in range(2):
                        k = 2 * kp + h
                        ins = act.activation(dst[:, k, cols], PS[:, 4 + kp % 4, h * L:(h + 1) * L], ACT.Identity,
                                             bias=shc[:, c, k:k + 1], scale=gsc[:, c, k:k + 1])
                    ins.then_inc(xh_ready, 1)

            act.wait_ge(cols_ready, 1)
            act.wait_ge(xs_ready, 18)
            U = Units(U_KV)
            for j in range(4):
                for k in range(4 * j, 4 * j + 4):
                    for c in range(2):
                        ins = act.activation(x1h[:, k, c * L:(c + 1) * L], xtok[:, k, c * L:(c + 1) * L], ACT.Identity,
                                             bias=shc[:, c, k:k + 1], scale=gsc[:, c, k:k + 1])
                    ins.then_inc(xh_ready, 1)
                high(U, j)

            def fm_take(f, width):
                p = f % 2
                act.wait_ge(fm_done, f + 1)
                if f >= 2:
                    act.wait_ge(fm_stored[p], 16 * (f // 2))
                act.copy(stage[:, 4 * p:4 * p + 4, 0:width], PS[:, 4 * p:4 * p + 4, 0:width]).then_inc(fm_read, 1)

            def fm_store(f, width, dst, h0):
                p = f % 2
                act.wait_ge(conv_done, 2 * f + 2)
                heads = stage[:, 4 * p:4 * p + 4, 0:width]
                act.activation(heads, cst[:, :, 0:width], ACT.Silu).then_inc(silu_done, 1)
                act.wait_ge(silu_done, f + 1)
                act.dma_start(dst[h0:h0 + 4, :, :].rearrange("h p n -> p h n"), heads).then_inc(fm_stored[p], 16)

            stores = [(2 * L, s_kT, 0), (2 * L, s_kT, 4), (2 * L, s_vT, 0), (2 * L, s_vT, 4), (L, s_qT, 0), (L, s_qT, 4)]
            for f in range(6):
                highs(U, 8 * f + 4, 8 * f + 12)
                if f >= 1:
                    fm_store(f - 1, *stores[f - 1])
                fm_take(f, stores[f][0])

            act.wait_ge(ab_loaded, 16)
            act.copy(abh[:, :, :], abw).then_inc(ab_high, 1)
            U = Units(U_ZP)
            act.wait_ge(small_loaded, 16 * 5)
            for n in range(4):
                if n == 0:
                    act.wait_ge(ab_done, 1)
                    act.copy(gamT[0:4 * H, :], PS[0:4 * H, 4, :]).then_inc(abT_ready, 1)
                highs(U, 8 * n + 4, min(8 * n + 12, 32))
                if n == 0:
                    fm_store(5, *stores[5])
                    act.wait_ge(abr_done, 1)
                    act.copy(abr[:, :, :], PS[:, 5, 0:4 * 4 * H].rearrange("p (t n) -> p t n", t=4)).then_inc(ab_ready, 1)
                    act.wait_ge(ab_ready, 1)
                    act.activation(Q[:, 1, :, :, :].rearrange("p t d h -> p t (d h)"), abr[:, :, 2 * H:4 * H], ACT.Sigmoid)
                    step(act.activation(alog[:], alog[:], ACT.Exp))
                    act.wait_ge(ex_ready, 1)
                    act.activation(gt[:, 1], gt[:, 1], ACT.Exp).then_inc(lx_ready, 1)
                act.wait_ge(lin_done, n + 1)
                if n < 2:
                    act.wait_ge(fm_stored[n], 48)
                else:
                    act.wait_ge(zp_stored[n % 2], 16)
                q = 4 * (n % 2)
                for t in range(NT):
                    act.copy(stage[:, q + t, :], PS[:, 2 * (n % 2) + t, :]).then_inc(acc_free[n % 2], 1)
                act.wait_ge(acc_free[n % 2], 2 * (n // 2) + 2)
                act.dma_start(s_zp[n // 2, :, :, (n % 2) * CB:(n % 2 + 1) * CB].rearrange("t p n -> p t n"),
                              stage[:, q:q + NT, :]).then_inc(zp_stored[n % 2], 16)
                if n == 2:
                    act.wait_ge(q_dve, 1)
                    act.activation(Q[:, 5, :, :, :].rearrange("p t d h -> p (t d h)"), Q[:, 0, :, :, :].rearrange("p t d h -> p (t d h)"), ACT.Exp)
                    act.activation(gt[:, 2], gt[:, 2], ACT.Exp)
                    act.activation(Q[:, 4, :, :, :].rearrange("p t d h -> p (t d h)"), gt[:, 3].rearrange("p t n -> p (t n)"), ACT.Exp)\
                       .then_inc(q_ready, 1)
                    act.wait_ge(gam_done, 3)
                    act.copy(gamT[0:16, :], PS[0:16, 6, :]).then_inc(gamT_ready, 1)

            act.wait_ge(zp_stored[0], 32)
            act.wait_ge(zp_stored[1], 32)
            act.dma_start(lmask[:, :, :, :], A["lmask"]).then_inc(lmask_loaded, 16)

            with act.Fori(0, H // 2) as i:
                act.wait_ge(pair_free, i * 4 + 4)
                act.wait_ge(pair_in, i * 48 + 48)
                for dst, src in ((kT, ck), (qT, cq)):
                    act.activation(dst[:, :, :], src, ACT.Square).then_inc(squares_ready, 1)
                for n, (dst, src) in enumerate(((kT[:, :, :], PS[:, 0:2, :]), (qT[:, :, :], PS[:, 2, :].rearrange("p (a n) -> p a n", a=2)))):
                    act.wait_ge(nsum_done, i * 2 + n + 1)
                    act.activation(dst, src, ACT.Ln, bias=eps[:, 0:1]).then_inc(norm_log, 1)
                for n, dst in enumerate((kT[:, :, :], qT[:, :, :])):
                    act.wait_ge(norm_log, i * 2 + n + 1)
                    act.activation(dst, dst, ACT.Exp, scale=-0.5).then_inc(norm_root, 1)
                act.wait_ge(tok_done, i * 2 + 1)
                act.copy(vtok[:, :, :, :].rearrange("p a t n -> p a (t n)"), PS[:, 6:8, :]).then_inc(tok_read, 1)
                act.wait_ge(tok_done, i * 2 + 2)
                act.copy(ktok[:, :, :, :].rearrange("p a t n -> p a (t n)"), PS[:, 4:6, :]).then_inc(tok_read, 1)
                act.wait_ge(dif_ready, i + 1)
                act.activation(X[:, :, :, :].rearrange("p s q n -> p (s q n)"), X[:, :, :, :].rearrange("p s q n -> p (s q n)"), ACT.Exp)\
                   .then_inc(dec_ready, 1)

                def take_x(lv, s):
                    if lv == 0 and s == 2:
                        act.wait_ge(di_ready, i + 1)
                    act.wait_ge(tr_done, i * 24 + 4 * lv + s + 1)
                    act.copy(X[:, s], PS[:, s + (4 if lv == 0 else 0), :].rearrange("p (q n) -> p q n", q=4)).then_inc(x_ready, 1)

                for s in range(4):
                    take_x(0, s)
                for lv in range(1, LEVELS):
                    for s in range(4):
                        act.wait_ge(mm1_done, i * 24 + 4 * (lv - 1) + s + 1)
                        act.copy(PB[:, s], PS[:, s, :].rearrange("p (q n) -> p q n", q=4)).then_inc(p_ready, 1)
                    if lv < LEVELS - 1:
                        for s in range(4):
                            take_x(lv, s)
                for s in (2, 3):
                    act.wait_ge(vd_ready, i * 4 + s + 1)
                    for q in range(4):
                        t = TILE[q // 2][s]
                        ins = act.activation(VN[:, q], PS[:, 2, q * P:(q + 1) * P], ACT.Copy,
                                             scale=Qs[:, 8 + 2 * t + q // 2, q % 2:q % 2 + 1])
                    ins.then_inc(vn_ready, 1)
                    act.wait_ge(qs_done, i * 2 + s - 1)
                    if s == 3:
                        act.wait_ge(o_ready, i * 2 + 1)
                    for q in range(4):
                        t = TILE[q // 2][s]
                        ins = act.activation(EQ[:, q], PS[:, 1, q * P:(q + 1) * P], ACT.Copy,
                                             scale=Qs[:, 40 + 2 * t + q // 2, q % 2:q % 2 + 1])
                    ins.then_inc(eq_ready, 1)
                act.wait_ge(vn_ready, i * 2 + 2)
                act.wait_ge(eq_ready, i * 2 + 2)
                act.sem_inc(pair_free, 1)

            act.wait_ge(dn_done, 1)
            act.dma_start(zp[:, :, :, :].rearrange("p s t n -> p (s t) n"), s_zp.rearrange("s t p n -> p (s t) n")).then_inc(branch_loaded, 16)
            for dst, name in ((poolm[:, :, :, :], "poolm"), (poolw[:, :, :, :], "poolw"), (pscale[:], "pscale")):
                act.dma_start(dst, A[name]).then_inc(branch_loaded, 16)
            act.dma_start(onorm[:], A["ev_onorm_g"].rearrange("o n -> (o n)").partition_broadcast(P)).then_inc(branch_loaded, 16)
            highs(Units(U_OUT), 0, 4)
            act.wait_ge(bc_done, 1)
            act.copy(gate[:, 0, :], PS[:, 4:8, :].rearrange("p b n -> p (b n)")).then_inc(gate_ready, 1)
            act.wait_ge(osum_ready, 1)
            act.activation(ro[:], so[:], ACT.Sqrt, bias=eps[:, 0:1], scale=1.0 / P).then_inc(oroot, 1)
            act.wait_ge(branch_loaded, 16 * 5)
            act.activation(zt, zt, ACT.Silu).then_inc(zs_ready, 1)
            act.wait_ge(pool_done, 1)
            act.copy(poolT[:, :, :].rearrange("p c n -> p (c n)"), PS[:, 0:4, :].rearrange("p b n -> p (b n)")).then_inc(poolT_ready, 1)
            act.wait_ge(yb_done, 1)
            for c in range(8):
                act.activation(xh[:, 8 + c, :], PS[:, 4 + c // 2, (c % 2) * L:(c % 2 + 1) * L], ACT.Copy,
                               scale=pscale[:, c:c + 1]).then_inc(yh_ready, 1)
            act.wait_ge(ya_done, 1)
            for c in range(8):
                act.copy(xh[:, c, :], PS[:, c // 2, (c % 2) * L:(c % 2 + 1) * L]).then_inc(yh_ready, 1)
            act.wait_ge(y_ready, 16)
            for t in range(NT):
                act.dma_start(hx[:, t, :], A["x"][0, t * P:(t + 1) * P, :]).then_inc(hx_loaded, 16)
                act.dma_start(zp[:, t, :, :].rearrange("p a n -> p (a n)"), A["pos"][t * P:(t + 1) * P, :]).then_inc(hx_loaded, 16)

            def take_gate(n, g):
                act.wait_ge(bc_done, n + 1)
                act.copy(gate[:, g, :], PS[:, 4:8, :].rearrange("p b n -> p (b n)")).then_inc(gate_ready, 1)

            highs(Units(U_OUT), 4, 8)
            take_gate(1, 1)
            highs(Units(U_OUT), 8, 32)

            def normalise(c, U):
                highs(U, 0, 4)
                act.wait_ge(hx_added, HX[c])
                for t in range(NT):
                    root(c, t, hx[:, t, :], PS[:, 0:4, :].rearrange("p b n -> p (b n)"))
                act.wait_ge(cols_ready, c)
                split_high(c, xh, slice(0, L))

            def relus(T, layer, tau, n):
                act.wait_ge(lin_done, T(n, 1))
                first = tau == 0 and T.i is None and layer == 0
                if not first:
                    act.wait_ge(mt_done, T.tau(tau, 0))
                for t in range(NT):
                    act.activation(rbuf[:, t, :], PS[:, 2 * (n % 2) + t, :], ACT.Relu).then_inc(relu_ready, 1)

            def mids(T, tau, buf):
                for t in range(NT):
                    act.wait_ge(mt_done, T.tau(tau, 1 + t))
                    act.copy(hth[:, buf, 4 * (tau % 2):4 * (tau % 2) + 4, t * P:(t + 1) * P],
                             PS[:, 4 + t, :].rearrange("p (c n) -> p c n", c=4)).then_inc(hth_ready, 1)

            def mlp(layer, base, n0):
                U, T = Units(base), Turn(n0, layer)
                highs(U, 4, 12)
                relus(T, layer, 0, 0)
                highs(U, 12, 16)
                U = Units(base + 16)
                highs(U, 0, 2)
                mids(T, 0, 0)
                highs(U, 2, 4)
                relus(T, layer, 1, 1)
                highs(U, 4, 8)
                mids(T, 1, 0)

                def pair(U, T, j0, tau, n, buf):
                    highs(U, j0, j0 + 12)
                    relus(T, layer, tau, n)
                    highs(U, j0 + 12, j0 + 18)
                    mids(T, tau, buf)
                    highs(U, j0 + 18, j0 + 20)
                    relus(T, layer, tau + 1, n + 1)
                    highs(U, j0 + 20, j0 + 26)
                    mids(T, tau + 1, buf)
                    highs(U, j0 + 26, j0 + 32)

                with act.Fori(0, 3) as i:
                    U, T = Units(base + 16, 64, i), Turn(n0 + 2, layer, i)
                    highs(U, 8, 12)
                    relus(T, layer, 2, 0)
                    highs(U, 12, 18)
                    mids(T, 2, 1)
                    highs(U, 18, 20)
                    relus(T, layer, 3, 1)
                    highs(U, 20, 26)
                    mids(T, 3, 1)
                    highs(U, 26, 32)
                    pair(U, T, 32, 4, 6, 0)
                    highs(U, 64, 72)
                U, T = Units(base + 16 + 192), Turn(n0 + 2, layer, 3)
                highs(U, 8, 12)
                relus(T, layer, 2, 0)
                highs(U, 12, 18)
                mids(T, 2, 1)
                highs(U, 18, 20)
                relus(T, layer, 3, 1)
                highs(U, 20, 26)
                mids(T, 3, 1)
                if layer == 0:
                    highs(U, 26, 34)
                    take_gate(2, 0)
                    highs(U, 34, 48)
                else:
                    highs(U, 26, 48)

            normalise(2, Units(U_MLP0))
            mlp(0, U_MLP0, N_MLP0)
            normalise(3, Units(U_OIN))

            U = Units(U_OIN)
            act.dma_start(wsT[:, :, :], A["wsT"]).then_inc(ws_loaded, 16)
            for n in range(8):
                highs(U, 8 * n + 4, min(8 * n + 12, 64))
                act.wait_ge(lin_done, N_OIN + n + 1)
                if n == 0:
                    act.wait_ge(xp_done, 32)
                dst = (ug, vg)[n // 4]
                for t in range(NT):
                    act.activation(dst[:, t, (n % 4) * CB:(n % 4 + 1) * CB], PS[:, 2 * (n % 2) + t, :], ACT.Gelu)\
                       .then_inc(acc_free[n % 2], 1)
                act.wait_ge(acc_free[n % 2], 2 * ((N_OIN + n) // 2) + 2)
                if n >= 4:
                    act.sem_inc(v_ready, 1)
            act.wait_ge(mv_ready, 1)
            act.activation(mv[:, :, 1:2].rearrange("p t o -> p (t o)"), mv[:, :, 1:2].rearrange("p t o -> p (t o)"), ACT.Sqrt,
                           bias=eps[:, 0:1]).then_inc(lroot, 1)
            for g in range(4):
                if g >= 2:
                    act.wait_ge(v_normed, g - 1)
                for n, name in enumerate(("od_ln_g", "od_ln_b")):
                    act.dma_start(lnp[g % 2][:, n, :], A[name][0, g * CB:(g + 1) * CB].partition_broadcast(P)).then_inc(ln_loaded[g % 2], 16)
            highs(Units(U_OOUT), 0, 4)
            for kp in range(8):
                act.wait_ge(um_done, kp + 1)
                act.copy(xh[:, 2 * kp:2 * kp + 2, :].rearrange("p k n -> p (k n)"), PS[:, 4 + kp % 4, :]).then_inc(umh_ready, 1)
            highs(Units(U_OOUT), 4, 16)
            take_gate(3, 1)
            highs(Units(U_OOUT), 16, 32)
            normalise(4, Units(U_MLP1))
            mlp(1, U_MLP1, N_MLP1)
            act.wait_ge(hx_added, HX[5])
            act.dma_start(fg[:], A["final_g"].partition_broadcast(P)).then_inc(fg_loaded, 16)
            for t in range(NT):
                root(5, t, hx[:, t, :], PS[:, 0:4, :].rearrange("p b n -> p (b n)"))

        @block.gpsimd
        def _(pool):
            pool.memset(eps[:], EPS).then_inc(eps_ready, 1)
            pool.sem_inc(pair_free, 4)

            with pool.Fori(0, H // 2) as i:
                pool.wait_ge(lmask_loaded, 16)
                pool.wait_ge(dec_ready, i + 1)
                for s in range(2):
                    ins = pool.tensor_tensor(DI[:, s].rearrange("p (d a) n -> p d a n", d=2),
                                             X[:, 2 + s].rearrange("p (d a) n -> p d a n", d=2),
                                             incl[:, :, :].unsqueeze(2).broadcast_to([P, 2, 2, P]), ALU.mult)
                ins.then_inc(di_ready, 1)
                for lv in range(1, LEVELS):
                    for s in range(4):
                        pool.wait_ge(nm_ready, i * 4 + s + 1)
                        if lv > 1:
                            pool.wait_ge(mm1_done, i * 24 + 4 * (lv - 2) + s + 1)
                        pool.tensor_tensor(B[:, s].rearrange("p (d a) n -> p d a n", d=2),
                                           NM[:, s].rearrange("p (d a) n -> p d a n", d=2),
                                           lmask[:, lv].unsqueeze(2).broadcast_to([P, 2, 2, P]), ALU.mult).then_inc(b_ready, 1)
                pool.wait_ge(b_ready, i * 24 + 24)
                pool.sem_inc(pair_free, 1)

            for t in range(NT):
                pool.wait_ge(hx_loaded, 64)
                pool.tensor_tensor(hx[:, t, :], hx[:, t, :], zp[:, t].rearrange("p a n -> p (a n)"), ALU.add).then_inc(hx_ready, 1)
            pool.wait_ge(hx_ready, 2)

            def add(e_count, cols, n):
                for t in range(NT):
                    pool.wait_ge(tmp_ready, e_count(1 + t))
                    pool.sem_inc(acc_free[n % 2], 1)
                    pool.tensor_tensor(hx[:, t, cols], hx[:, t, cols], tmp[:, t, :], ALU.add).then_inc(hx_added, 1)

            def square(T, tau, n):
                for t in range(NT):
                    pool.wait_ge(relu_ready, T.tau(tau, 1 + t))
                    pool.sem_inc(acc_free[n % 2], 1)
                    pool.tensor_tensor(rbuf[:, t, :], rbuf[:, t, :], rbuf[:, t, :], ALU.mult).then_inc(sqr_ready, 1)

            for b in range(4):
                add(lambda off: 2 * b + off, slice(b * CB, (b + 1) * CB), N_OUT + b)

            def mlp(layer):
                def downs(T, e, which):
                    for b in which:
                        add(lambda off: T.e(e + b, off), slice(b * CB, (b + 1) * CB), b)

                T = Turn(0, layer)
                square(T, 0, 0)
                square(T, 1, 1)
                with pool.Fori(0, 3) as i:
                    T = Turn(0, layer, i)
                    for h in range(2):
                        square(T, 2 + 2 * h, 0)
                        square(T, 3 + 2 * h, 1)
                        downs(T, 4 * h, range(4))
                T = Turn(0, layer, 3)
                square(T, 2, 0)
                square(T, 3, 1)
                downs(T, 0, range(4))
                downs(T, 4, range(4))

            mlp(0)
            for b in range(4):
                add(lambda off: 72 + 2 * b + off, slice(b * CB, (b + 1) * CB), N_OOUT + b)
            mlp(1)

        @block.vector
        def _(dve):
            step = Chain(dve, dve_step)

            def split(U, *js):
                for j in range(*js):
                    dve.wait_ge(w_high, U.u(j, 1))
                    dve.tensor_tensor(wl[:, j % SPLIT, :], raw[:, j % RAW, :], wh[:, j % SPLIT, :].bitcast(F32), ALU.subtract)\
                       .then_inc(w_split, 1)

            dve.sem_inc(sum_read, 1)

            def ada(M, k, i=None):
                def count(per, off):
                    return M * per + off if i is None else i * per + M * per + off
                dve.wait_ge(ada_loaded[k % 2], count(128, 16 * (k // 2 + 1)))
                if k == 0:
                    dve.wait_ge(ada_summed, count(1, 1))
                    dve.tensor_scalar(ada_acc[:], ada_raw[:, 0, :], csil[:, 0, 0:1], None, ALU.mult).then_inc(ada_used, 1)
                else:
                    dve.wait_ge(ada_used, count(KC, k))
                    dve.scalar_tensor_tensor(ada_acc[:], ada_raw[:, k % 2, :], csil[:, k, 0:1], ada_acc[:], ALU.mult, ALU.add)\
                       .then_inc(ada_used, 1)

            def adas(at, j, M):
                for k in range(KC):
                    if at[k] == j:
                        ada(M, k)

            def take_sum(M):
                dve.wait_ge(sum_done, M + 1)
                step(dve.tensor_copy(colbuf[:, M, :], PS[:, 6, 0:KC]))
                dve.sem_inc(sum_read, 1)

            def diagonals(M, layer, part, dst=None):
                step(dve.tensor_tensor(colbuf[:, M, :], colbuf[:, M, :], adab[:, 6 * layer + part, :], ALU.add))
                dst = ada_acc[:].rearrange("p (k n) -> p k n", k=KC) if dst is None else dst
                dve.tensor_tensor(dst, ident[:].unsqueeze(1).broadcast_to([P, KC, P]),
                                  colbuf[:, M, :].unsqueeze(2).broadcast_to([P, KC, P]), ALU.mult).then_inc(diag_ready, 1)

            def cols(c, scale, src):
                dst = gsc if scale else shc
                part = (0 if c < 2 or c == 3 else 3) + scale
                layer = 0 if c < 3 else 1
                step(dve.tensor_tensor(dst[:, c, :], src, adab[:, 6 * layer + part, :], ALU.add))
                if scale:
                    step(dve.scalar_tensor_tensor(dst[:, c, :], dst[:, c, :], 1.0, gcol[:, max(c - 1, 0), :], ALU.add, ALU.mult))

            for t in range(NT):
                dve.wait_ge(h_loaded[t], 16)
                dve.wait_ge(pos_loaded, 32)
                dve.tensor_tensor(nrm1[:, t, :], nrm1[:, t, :], ada_raw[:, t, :], ALU.add).then_inc(h_ready, 1)
            dve.wait_ge(consts, 16 * 6)
            dve.wait_ge(csil_ready, 1)
            dve.wait_ge(cs_high, 1)
            dve.tensor_tensor(chl[:, :, 2:4], csil[:, :, :], chl[:, :, 0:2].bitcast(F32), ALU.subtract).then_inc(cs_split, 1)

            def normalise(c, src, dst):
                for t in range(NT):
                    col = 2 * c + t
                    dve.wait_ge(rt_done, col + 1)
                    step(dve.reciprocal(rs[:, col:col + 1], ss[:, col:col + 1]))
                    dve.tensor_scalar(dst[:, t, :], src[:, t, :], rs[:, col:col + 1], None, ALU.mult).then_inc(nrm_ready, 1)

            def split_low(c, high, dst, cols):
                for kp in range(KC // 2):
                    dve.wait_ge(xh_ready, 8 * c + kp + 1)
                    for h in range(2):
                        k = 2 * kp + h
                        ins = dve.tensor_scalar(spl[:, h * L:(h + 1) * L], PS[:, 4 + kp % 4, h * L:(h + 1) * L],
                                                gsc[:, c, k:k + 1], shc[:, c, k:k + 1], ALU.mult, ALU.add)
                    step(ins)
                    dve.tensor_tensor(dst[:, 2 * kp:2 * kp + 2, cols], spl[:].rearrange("p (k n) -> p k n", k=2),
                                      high[:, 2 * kp:2 * kp + 2, cols].bitcast(F32), ALU.subtract).then_inc(xt_ready, 1)
                    dve.wait_ge(xt_ready, 8 * c + kp + 1)

            dve.wait_ge(consts, 16 * 6)
            dve.wait_ge(csil_ready, 1)
            def take_row(g):
                dve.wait_ge(w_used, SPLIT + KC * (g + 1))
                dve.tensor_copy(arow[0:4, g % 2, :].rearrange("p (b n) -> p b n", b=2), PS[0:4, 2 * (g % 2):2 * (g % 2) + 2, :])\
                   .then_inc(arow_ready, 1)

            U = Units(U_A0)
            split(U, 0, 8)
            dve.wait_ge(h_ready, 2)
            normalise(0, nrm1, nrm1)
            split(U, 8, 16)
            take_row(0)
            split(U, 16, 32)
            take_row(1)
            split(U, 32, 40)
            normalise(1, nrm1, nrm1)
            split(U, 40, 48)
            take_row(2)
            split(U, 48, 64)
            take_row(3)
            dve.wait_ge(a0_done, 1)
            step(dve.tensor_copy(mod0[:, :, :], PS[:, 4, 0:4 * KC].rearrange("p (j c) -> p j c", c=2)))
            for c in range(2):
                cols(c, 0, mod0[:, 0:KC, c])
                cols(c, 1, mod0[:, KC:2 * KC, c])
            dve.sem_inc(cols_ready, 1)

            dve.wait_ge(xs_ready, 18)
            scratch = nrm1[:, :, :].rearrange("p a (b c n) -> p (a b) c n", b=4, c=2)

            def scaled(k):
                for c in range(2):
                    ins = dve.tensor_scalar(scratch[:, k % 8, c, :], xtok[:, k, c * L:(c + 1) * L],
                                            gsc[:, c, k:k + 1], shc[:, c, k:k + 1], ALU.mult, ALU.add)
                ins.then_inc(spl_ready, 1)

            scaled(0)
            for k in range(KC):
                if k < KC - 1:
                    if k >= 7:
                        dve.wait_ge(xt_ready, k - 6)
                    scaled(k + 1)
                dve.wait_ge(spl_ready, k + 1)
                dve.wait_ge(xh_ready, k + 1)
                dve.tensor_tensor(x1l[:, k, :], scratch[:, k % 8].rearrange("p c n -> p (c n)"), x1h[:, k, :].bitcast(F32), ALU.subtract)\
                   .then_inc(xt_ready, 1)
                if k % 4 == 3:
                    split(Units(U_KV), k // 4, k // 4 + 1)
            split(Units(U_KV), 4, 12)

            def convolve(f, pair, kind, h0, width):
                dve.wait_ge(fm_read, f + 3)
                if f >= 1 and pair == 0:
                    dve.wait_ge(silu_done, f)
                for n, tap in enumerate((2, 0, 1, 3, 4)):
                    for a in (2 * pair, 2 * pair + 1):
                        w = convw[:, kind, 5 * (h0 + a) + tap:5 * (h0 + a) + tap + 1]
                        s3 = stage[:, 4 * (f % 2) + a, 0:width].rearrange("p (s n) -> p s n", n=L)
                        d3 = cst[:, a, 0:width].rearrange("p (s n) -> p s n", n=L)
                        off = tap - 2
                        lo, hi = max(0, -off), L - max(0, off)
                        if n == 0:
                            ins = dve.tensor_scalar(d3, s3, w, None, ALU.mult)
                        else:
                            ins = dve.scalar_tensor_tensor(d3[:, :, lo:hi], s3[:, :, lo + off:hi + off], w, d3[:, :, lo:hi],
                                                           ALU.mult, ALU.add)
                    if n < 4:
                        step(ins)
                    else:
                        ins.then_inc(conv_done, 1)

            dve.wait_ge(small_loaded, 16 * 5)
            for f in range(6):
                for pair in range(2):
                    if f == 5 and pair == 0:
                        dve.wait_ge(ab_high, 1)
                        dve.tensor_tensor(abl[:, :, :], abw, abh[:, :, :].bitcast(F32), ALU.subtract).then_inc(ab_split, 1)
                    convolve(f, pair, (1, 1, 2, 2, 0, 0)[f], 4 * (f % 2), 2 * L if f < 4 else L)
                    split(Units(U_KV), 8 * f + 12 + 4 * pair, 8 * f + 16 + 4 * pair)

            dve.wait_ge(ab_ready, 1)
            step(dve.tensor_tensor(gt[:, 0], abr[:, :, 0:2 * H], dtb[:].unsqueeze(1).broadcast_to([P, 4, 2 * H]), ALU.add))
            step(dve.tensor_scalar(gt[:, 1], gt[:, 0], -1.0, None, ALU.mult))
            dve.tensor_tensor(gt[:, 1], gt[:, 1], gt[:, 0], ALU.min).then_inc(ex_ready, 1)
            dve.wait_ge(lx_ready, 1)
            step(dve.tensor_scalar(gt[:, 2], gt[:, 1], 2.0, None, ALU.add))
            step(dve.reciprocal(gt[:, 2], gt[:, 2]))
            step(dve.tensor_tensor(gt[:, 2], gt[:, 2], gt[:, 1], ALU.mult))
            step(dve.tensor_tensor(gt[:, 3], gt[:, 2], gt[:, 2], ALU.mult))
            step(dve.tensor_scalar(gt[:, 4], gt[:, 3], 1.0 / 17, None, ALU.mult))
            for odd in (15, 13, 11, 9, 7, 5, 3):
                step(dve.scalar_tensor_tensor(gt[:, 4], gt[:, 4], 1.0 / odd, gt[:, 3], ALU.add, ALU.mult))
            step(dve.scalar_tensor_tensor(gt[:, 4], gt[:, 4], 1.0, gt[:, 2], ALU.add, ALU.mult))
            step(dve.tensor_scalar(gt[:, 0], gt[:, 0], 0.0, None, ALU.max))
            step(dve.scalar_tensor_tensor(gt[:, 4], gt[:, 4], 2.0, gt[:, 0], ALU.mult, ALU.add))
            dve.scalar_tensor_tensor(gt[:, 5], gt[:, 4], -1.0, alog[:].unsqueeze(1).broadcast_to([P, 4, 2 * H]), ALU.mult, ALU.mult)\
               .then_inc(g_ready, 1)
            U = Units(U_ZP)
            split(U, 12, 20)
            dve.wait_ge(gam_done, 1)
            q0 = Q[:, 0].rearrange("p t d h -> p t (d h)")
            dve.tensor_copy(q0, PS[:, 5, 0:64].rearrange("p (t n) -> p t n", t=4)).then_inc(gam_ready, 1)
            split(U, 20, 28)
            dve.wait_ge(gam_done, 2)
            dve.wait_ge(gam_ready, 1)
            step(dve.tensor_copy(gt[:, 3], PS[:, 7, 0:64].rearrange("p (t n) -> p t n", t=4)))
            step(dve.tensor_tensor(gt[:, 2], gt[:, 3], q0, ALU.subtract))
            dve.tensor_scalar(gt[:, 2], gt[:, 2], 0.0, None, ALU.min).then_inc(q_dve, 1)
            split(U, 28, 32)
            dve.wait_ge(q_ready, 1)
            step(dve.tensor_scalar(Q[:, 2], Q[:, 5], -1.0, None, ALU.mult))
            step(dve.tensor_tensor(Q[:, 3].rearrange("p t d h -> p t (d h)"), Q[:, 1].rearrange("p t d h -> p t (d h)"), gt[:, 2], ALU.mult))

            with dve.Fori(0, H // 2) as i:
                step.enter(i, 7)
                dve.wait_ge(pair_free, i * 4 + 4)
                step(dve.tensor_copy(Qs[:, :, :], Q[:, :, :, :, :].rearrange("p q t d h -> p (q t d) h")[:, :, ds(i * 2, 2)]))
                for d in range(2):
                    ins = dve.tensor_copy(sel[0:16, 2 * d:2 * d + 2, :],
                                          ident[0:16, ds(i * 2 + 8 * d, 2)].unsqueeze(2).broadcast_to([16, 2, P]))
                ins.then_inc(sel_ready, 1)
                ada(0, 0, i)
                dve.wait_ge(norm_root, i * 2 + 1)
                dve.tensor_tensor(kT[:, :, :], kT[:, :, :], ck, ALU.mult).then_inc(kq_normed, 1)
                dve.wait_ge(norm_root, i * 2 + 2)
                dve.scalar_tensor_tensor(qT[:, :, :], qT[:, :, :], float(P) ** -0.5, cq, ALU.mult, ALU.mult).then_inc(kq_normed, 1)
                ada(0, 1, i)
                ada(0, 2, i)
                dve.wait_ge(row_done, i + 1)
                for s in range(4):
                    for q in range(4):
                        t = TILE[q // 2][s]
                        ins = dve.tensor_scalar(X[:, s, q, :], PS[:, 4 + q, t * P:(t + 1) * P],
                                                Qs[:, 2 * t + q // 2, q % 2:q % 2 + 1], 0.0, ALU.subtract, ALU.min)
                ins.then_inc(dif_ready, 1)
                ada(0, 3, i)
                dve.wait_ge(dec_ready, i + 1)
                dve.wait_ge(kk_done, i + 1)
                dve.wait_ge(lmask_loaded, 16)
                for s in range(4):
                    for q in range(4):
                        t = TILE[q // 2][s]
                        ins = dve.scalar_tensor_tensor(NM[:, s, q, :], X[:, s, q, :], Qs[:, 8 + 2 * t + q // 2, q % 2:q % 2 + 1],
                                                       PS[:, q % 2, t * P:(t + 1) * P], ALU.mult, ALU.mult)
                    ins.then_inc(nm_ready, 1)
                    dve.wait_ge(nm_ready, i * 4 + s + 1)
                    step(dve.tensor_tensor(XT[:, s].rearrange("p (d a) n -> p d a n", d=2),
                                           NM[:, s].rearrange("p (d a) n -> p d a n", d=2),
                                           lmask[:, 0].unsqueeze(2).broadcast_to([P, 2, 2, P]), ALU.mult))
                    dve.scalar_tensor_tensor(XT[:, s], XT[:, s], -1.0, ident[:].unsqueeze(1).broadcast_to([P, 4, P]), ALU.mult, ALU.add)\
                       .then_inc(xT_ready, 1)
                dve.wait_ge(di_ready, i + 1)
                for s in range(2):
                    for d in range(2):
                        t = TILE[d][2 + s]
                        ins = dve.tensor_tensor(QK[:, s, 2 * d:2 * d + 2, :], DI[:, s, 2 * d:2 * d + 2, :],
                                                PS[:, 2, :].rearrange("p (a t n) -> p a t n", a=2, t=2)[:, :, t, :], ALU.mult)
                ins.then_inc(qk_ready, 1)
                for lv in range(1, LEVELS):
                    for s in range(4):
                        dve.wait_ge(mm2_done, i * 24 + 4 * (lv - 1) + s + 1)
                        for d in range(2):
                            xt = halves(XT[:, s, 2 * d:2 * d + 2, :].rearrange("p q n -> p (q n)"), lv, 1 - d)
                            ins = dve.tensor_tensor(xt, xt, halves(PS[:, 4 + s, 2 * d * P:2 * (d + 1) * P], lv, 1 - d), ALU.subtract)
                        ins.then_inc(xT_ready, 1)
                    for k in range(2 * lv + 2, 2 * lv + 4):
                        ada(0, k, i)
                for s in range(4):
                    if s >= 1:
                        dve.wait_ge(ks_done, i * 3 + s)
                        for q in range(4):
                            t = TILE[q // 2][s]
                            ins = dve.scalar_tensor_tensor(R[:, q], PS[:, 0, q * P:(q + 1) * P], Qs[:, 16 + 2 * t + q // 2, q % 2:q % 2 + 1],
                                                           vtok[:, q % 2, t, :], ALU.mult, ALU.add)
                        ins.then_inc(r_ready, 1)
                    dve.wait_ge(y_done, i * 4 + s + 1)
                    for q in range(4):
                        t = TILE[q // 2][s]
                        ins = dve.tensor_scalar(VD[:, q], PS[:, 2, q * P:(q + 1) * P], Qs[:, 24 + 2 * t + q // 2, q % 2:q % 2 + 1],
                                                None, ALU.mult)
                    ins.then_inc(vd_ready, 1)
                    dve.wait_ge(ds_done, i * 4 + s + 1)
                    if s >= 1:
                        dve.wait_ge(s_ready, i * 4 + s)
                    for q in range(4) if s >= 1 else ():
                        t = TILE[q // 2][s]
                        ins = dve.scalar_tensor_tensor(S[:, q], S[:, q], Qs[:, 32 + 2 * t + q // 2, q % 2:q % 2 + 1],
                                                       PS[:, 4, q * P:(q + 1) * P], ALU.mult, ALU.add)
                    if s == 0:
                        ins = dve.tensor_copy(S[:, :, :], PS[:, 4, :].rearrange("p (q n) -> p q n", q=4))
                    ins.then_inc(s_ready, 1)
                    if s == 3:
                        dve.wait_ge(sum_done, i + 1)
                        step(dve.tensor_copy(colbuf[:, ds(i, 1), :], PS[:, 6, 0:KC].unsqueeze(1)))
                        dve.sem_inc(sum_read, 1)
                    if s >= 2:
                        dve.wait_ge(eq_ready, i * 2 + s - 1)
                        dve.wait_ge(ov_done, i * 2 + s - 1)
                        ov = PS[:, 3, :].rearrange("p (q n) -> p q n", q=4)
                        if s == 2:
                            for d in range(2):
                                ins = dve.tensor_tensor(otok[:, TILE[d][s], ds(i * 2, 2), :], EQ[:, 2 * d:2 * d + 2], ov[:, 2 * d:2 * d + 2], ALU.add)
                            ins.then_inc(o_ready, 1)
                        else:
                            step(dve.tensor_tensor(EQ, EQ, ov, ALU.add))
                            dve.wait_ge(o_ready, i * 2 + 1)
                            for d in range(2):
                                o = otok[:, TILE[d][s], ds(i * 2, 2), :]
                                ins = dve.tensor_tensor(o, o, EQ[:, 2 * d:2 * d + 2], ALU.add)
                            ins.then_inc(o_ready, 1)
                dve.wait_ge(o_ready, i * 2 + 2)
                dve.wait_ge(s_ready, i * 4 + 4)
                dve.sem_inc(pair_free, 1)
                step.leave(H // 2)
            dve.wait_ge(pair_free, 20)
            dve.sem_inc(dn_done, 1)

            cols(2, 0, colbuf[:, 1, :])
            cols(2, 1, colbuf[:, 2, :])
            dve.sem_inc(cols_ready, 1)
            dve.wait_ge(ada_summed, 5)
            diagonals(0, 0, 2)
            split(Units(U_OUT), 0, 4)

            o2 = otok[:, :, :, :].rearrange("p t h n -> p (t h) n")
            s2 = osq[:, :, :, :].rearrange("p t h n -> p (t h) n")
            step(dve.tensor_tensor(s2, o2, o2, ALU.mult))
            dve.tensor_reduce(so[:], s2, AX.X, ALU.add).then_inc(osum_ready, 1)
            dve.wait_ge(oroot, 1)
            step(dve.reciprocal(ro[:], ro[:]))
            step(dve.tensor_tensor(o2, o2, ro[:].unsqueeze(2).broadcast_to([P, NT * H, P]), ALU.mult))
            dve.wait_ge(branch_loaded, 16 * 5)
            step(dve.tensor_tensor(o2, o2, onorm[:].unsqueeze(1).broadcast_to([P, NT * H, P]), ALU.mult))
            dve.wait_ge(zs_ready, 1)
            dve.tensor_tensor(o2, o2, zt.rearrange("p t (h n) -> p (t h) n", h=H), ALU.mult).then_inc(ya_ready, 1)

            def y_low(c, n, bank, scale):
                dve.wait_ge(yh_ready, n // 2 * 2 + 2)
                src = PS[:, bank + (c % 8) // 2, (c % 2) * L:(c % 2 + 1) * L]
                if scale:
                    step(dve.tensor_scalar(spl[:, 0:L], src, pscale[:, c - 8:c - 7], None, ALU.mult))
                    src = spl[:, 0:L]
                dve.tensor_tensor(xl[:, c, :], src, xh[:, c, :].bitcast(F32), ALU.subtract).then_inc(y_ready, 1)
                dve.wait_ge(y_ready, n + 1)

            for c in range(8):
                y_low(8 + c, c, 4, True)
            for c in range(8):
                y_low(c, 8 + c, 0, False)

            def gated(e_count, done, n, g, b):
                dve.wait_ge(lin_done, done)
                for t in range(NT):
                    w = e_count(t - 1)
                    if not isinstance(w, int) or w >= 1:
                        dve.wait_ge(hx_added, w)
                    dve.tensor_tensor(tmp[:, t, :], PS[:, 2 * (n % 2) + t, :], gate[:, g, b * CB:(b + 1) * CB], ALU.mult)\
                       .then_inc(tmp_ready, 1)

            U = Units(U_OUT)
            dve.wait_ge(bc_done, 1)
            diagonals(3, 0, 5, poolm[:, :, :, :].rearrange("p g t (a n) -> p (g t a) n", n=P))
            dve.wait_ge(gate_ready, 1)
            for j in range(4, 32):
                split(U, j, j + 1)
                adas(AT_OUT, j, 4)
                if j % 8 == 3 and j > 8:
                    b = j // 8 - 1
                    gated(lambda off: 2 * b + off, N_OUT + b + 1, N_OUT + b, 0, b)
            gated(lambda off: 6 + off, N_OUT + 4, N_OUT + 3, 0, 3)

            def mid_low(T, tau, buf):
                for t in range(NT):
                    dve.wait_ge(hth_ready, T.tau(tau, 1 + t))
                    hs = (slice(None), buf, slice(4 * (tau % 2), 4 * (tau % 2) + 4), slice(t * P, (t + 1) * P))
                    dve.tensor_tensor(htl[hs], PS[:, 4 + t, :].rearrange("p (c n) -> p c n", c=4), hth[hs].bitcast(F32), ALU.subtract)\
                       .then_inc(ht_ready, 1)

            def mlp(layer, base, n0):
                def down(T, e, n, b):
                    gated(lambda off: T.e(e + b, off), T(n, 1), n, 1, b)

                def units(U, j0, j1, i=None):
                    for j in range(j0, j1):
                        split(U, j, j + 1)
                        if layer == 0 and i is not None and j in AT64:
                            ada(5, AT64.index(j), i)

                U, T = Units(base), Turn(n0, layer)
                dve.wait_ge(gate_ready, 2 if layer == 0 else 4)
                split(U, 4, 12)
                if layer == 0:
                    take_sum(4)
                    cols(4, 0, colbuf[:, 4, :])
                split(U, 12, 16)
                U = Units(base + 16)
                split(U, 0, 2)
                mid_low(T, 0, 0)
                split(U, 2, 8)
                mid_low(T, 1, 0)
                with dve.Fori(0, 3) as i:
                    U, T = Units(base + 16, 64, i), Turn(n0 + 2, layer, i)
                    units(U, 8, 18, i)
                    mid_low(T, 2, 1)
                    units(U, 18, 24, i)
                    down(T, 0, 2, 0)
                    units(U, 24, 26, i)
                    mid_low(T, 3, 1)
                    units(U, 26, 28, i)
                    down(T, 0, 3, 1)
                    units(U, 28, 32, i)
                    down(T, 0, 4, 2)
                    units(U, 32, 36, i)
                    down(T, 0, 5, 3)
                    units(U, 36, 50, i)
                    mid_low(T, 4, 0)
                    units(U, 50, 56, i)
                    down(T, 4, 8, 0)
                    units(U, 56, 58, i)
                    mid_low(T, 5, 0)
                    units(U, 58, 60, i)
                    down(T, 4, 9, 1)
                    units(U, 60, 64, i)
                    if layer == 0:
                        dve.wait_ge(sum_done, i + 6)
                        dve.tensor_copy(colbuf[:, ds(i + 5, 1), :], PS[:, 6, 0:KC].unsqueeze(1)).then_inc(sum_read, 1)
                    down(T, 4, 10, 2)
                    units(U, 64, 68, i)
                    down(T, 4, 11, 3)
                    units(U, 68, 72, i)
                U, T = Units(base + 16 + 192), Turn(n0 + 2, layer, 3)
                if layer == 0:
                    dve.wait_ge(sum_read, 9)
                    cols(3, 0, colbuf[:, 5, :])
                    cols(3, 1, colbuf[:, 6, :])
                    dve.sem_inc(cols_ready, 1)
                    diagonals(7, 1, 2, dg[:, :, :])

                def tail_units(j0, j1):
                    for j in range(j0, j1):
                        split(U, j, j + 1)
                        if layer == 0:
                            adas(AT_TAIL, j, 8)

                tail_units(8, 18)
                mid_low(T, 2, 1)
                tail_units(18, 24)
                down(T, 0, 2, 0)
                tail_units(24, 26)
                mid_low(T, 3, 1)
                tail_units(26, 28)
                down(T, 0, 3, 1)
                tail_units(28, 32)
                down(T, 0, 4, 2)
                tail_units(32, 36)
                down(T, 0, 5, 3)
                tail_units(36, 40)
                down(T, 4, 6, 0)
                tail_units(40, 44)
                down(T, 4, 7, 1)
                tail_units(44, 48)
                down(T, 4, 8, 2)
                down(T, 4, 9, 3)

            def norm_hx(c, U):
                split(U, 0, 4)
                normalise(c, hx, nrm)
                dve.wait_ge(cols_ready, c)
                split_low(c, xh, xl, slice(0, L))

            norm_hx(2, Units(U_MLP0))
            mlp(0, U_MLP0, N_MLP0)
            norm_hx(3, Units(U_OIN))

            def stats(n):
                dve.wait_ge(v_ready, n - 3)
                for t in range(NT):
                    ins = dve.bn_stats(bst[:, t, n - 4, :], vg[:, t, (n - 4) * CB:(n - 3) * CB])
                return ins

            U = Units(U_OIN)
            for j in range(4, 64):
                split(U, j, j + 1)
                if j == 12:
                    take_sum(8)
                    cols(4, 1, colbuf[:, 8, :])
                    dve.sem_inc(cols_ready, 1)
                for M in AT_OIN:
                    adas(AT_OIN[M], j, M)
                if j % 8 == 3 and j >= 43:
                    stats(j // 8 - 1)
            step(stats(7))
            for t in range(NT):
                ins = dve.bn_aggr(mv[:, t, :], bst[:, t, :, :].rearrange("p a b -> p (a b)"))
            ins.then_inc(mv_ready, 1)
            dve.wait_ge(lroot, 1)
            step(dve.reciprocal(mv[:, :, 1:2].rearrange("p t o -> p (t o)"), mv[:, :, 1:2].rearrange("p t o -> p (t o)")))
            for g in range(4):
                cs = slice(g * CB, (g + 1) * CB)
                for t in range(NT):
                    ins = dve.tensor_scalar(vg[:, t, cs], vg[:, t, cs], mv[:, t, 0:1], mv[:, t, 1:2], ALU.subtract, ALU.mult)
                step(ins)
                dve.wait_ge(ln_loaded[g % 2], 32 * (g // 2 + 1))
                for n, op in ((0, ALU.mult), (1, ALU.add)):
                    ins = dve.tensor_tensor(vg[:, :, cs], vg[:, :, cs], lnp[g % 2][:, n, :].unsqueeze(1).broadcast_to([P, NT, CB]), op)
                    if n == 0:
                        step(ins)
                    else:
                        ins.then_inc(v_normed, 1)
            for g in range(4):
                for t in range(NT):
                    dve.wait_ge(mix_done, 2 * g + t + 1)
                    cs = slice(g * CB, (g + 1) * CB)
                    dve.scalar_tensor_tensor(ug[:, t, cs], PS[:, (2 * g + t) % 4, :], bscol[:, g:g + 1], ug[:, t, cs], ALU.add, ALU.mult)\
                       .then_inc(um_ready, 1)
            split(Units(U_OOUT), 0, 4)
            for kp in range(8):
                dve.wait_ge(umh_ready, kp + 1)
                dve.tensor_tensor(xl[:, 2 * kp:2 * kp + 2, :].rearrange("p k n -> p (k n)"), PS[:, 4 + kp % 4, :],
                                  xh[:, 2 * kp:2 * kp + 2, :].rearrange("p k n -> p (k n)").bitcast(F32), ALU.subtract).then_inc(uml_ready, 1)
            U = Units(U_OOUT)
            dve.wait_ge(gate_ready, 3)
            for j in range(4, 32):
                split(U, j, j + 1)
                if j == 11:
                    take_sum(9)
                    dve.wait_ge(ada_summed, 11)
                    diagonals(9, 1, 5)
                if j % 8 == 3 and j > 8:
                    b = j // 8 - 1
                    gated(lambda off: 72 + 2 * b + off, N_OOUT + b + 1, N_OOUT + b, 0, b)
            gated(lambda off: 78 + off, N_OOUT + 4, N_OOUT + 3, 0, 3)
            norm_hx(4, Units(U_MLP1))
            mlp(1, U_MLP1, N_MLP1)

            for t in range(NT):
                dve.wait_ge(rt_done, 11 + t)
                step(dve.reciprocal(rs[:, 10 + t:11 + t], ss[:, 10 + t:11 + t]))
                dve.wait_ge(fg_loaded, 16)
                dve.scalar_tensor_tensor(fin[:, t, :], hx[:, t, :], rs[:, 10 + t:11 + t], fg[:], ALU.mult, ALU.mult).then_inc(fin_ready, 1)


        @block.tensor
        def _(pe):
            pe.sem_inc(w_used, SPLIT)

            def mm(dst, lhsT, rhs, start=True, stop=True, **kw):
                return pe.matmul(dst, lhsT, rhs, start=start, stop=stop, **kw)

            def tok(U, j0, n, x, last=UPB, part=lambda j, h: 2 * j + h, ready=None, after=None, done=True):
                xa, xb = x
                for j in range(last):
                    pe.wait_ge(w_split, U.u(j0 + j, 1))
                    if ready is not None:
                        pe.wait_ge(ready[0], ready[1] + j + 1)
                    r = (j0 + j) % SPLIT
                    for h in range(UNIT):
                        k = part(j, h)
                        hi, lo = wh[:, r, h * CB:(h + 1) * CB], wl[:, r, h * CB:(h + 1) * CB]
                        for t in range(NT):
                            dst = PS[:, 2 * (n % 2) + t, :]
                            a, b = xa(k, t), xb(k, t)
                            mm(dst, a, hi, start=(j == 0 and h == 0), stop=False)
                            mm(dst, a, lo, start=False, stop=False)
                            ins = mm(dst, b, hi, start=False, stop=(j == last - 1 and h == 1))
                    ins.then_inc(w_used, 1)
                    if after and j in after:
                        after[j]()
                if done:
                    pe.wait_ge(w_used, U.u(j0 + last, SPLIT))
                    pe.sem_inc(lin_done, 1)

            pe.sem_inc(ada_summed, 1)

            def col_sum(M, i=None, quarter=None):
                def count(per, off):
                    return M * per + off if i is None else i * per + M * per + off

                def go():
                    if not quarter:
                        pe.wait_ge(ada_used, count(KC, KC))
                        pe.wait_ge(sum_read, count(1, 1))
                    for k in range(KC) if quarter is None else range(4 * quarter, 4 * quarter + 4):
                        ins = mm(PS[:, 6, k:k + 1], ada_acc[:, k * P:(k + 1) * P], ones[:, 0:1])
                    if quarter in (0, 1, 2):
                        return
                    ins.then_inc(sum_done, 1)
                    pe.wait_ge(sum_done, count(1, 1))
                    pe.sem_inc(ada_summed, 1)
                return go

            def spread(n):
                def go():
                    pe.wait_ge(diag_ready, n + 1)
                    if n == 3:
                        pe.wait_ge(uml_ready, 8)
                    for b in range(4):
                        src = {1: poolm[:, b, :, :].rearrange("p t n -> p (t n)"),
                               2: dg[:, 4 * b:4 * b + 4, :].rearrange("p k n -> p (k n)")}.get(n, ada_acc[:, b * CB:(b + 1) * CB])
                        ins = mm(PS[:, 4 + b, :], ones[:], src)
                    ins.then_inc(bc_done, 1)
                return go

            pe.wait_ge(consts, 16 * 6)
            pe.wait_ge(cs_split, 1)
            with pe.Fori(0, 2) as i:
                for g in range(2):
                    for k in range(KC):
                        pe.wait_ge(w_split, i * 2 * KC + g * KC + k + 1)
                        for b in range(2):
                            for w in (wh, wl):
                                ins = mm(PS[0:4, 2 * g + b, :], chl[:, k, :], w[:, k % SPLIT, b * CB:(b + 1) * CB],
                                         start=(k == 0 and w is wh), stop=(k == KC - 1 and w is wl))
                        ins.then_inc(w_used, 1)
                    pe.wait_ge(arow_ready, i * 2 + g + 1)
                    for j in range(8):
                        for h in range(2):
                            ins = mm(PS[:, 4, ds(i * 32 + 16 * g + 2 * j, 2)], arow[0:4, g, j * P:(j + 1) * P],
                                     ident[0:4, 2 * h:2 * h + 2], start=(h == 0), stop=(h == 1))
                    if g == 0:
                        pe.wait_ge(nrm_ready, i * 2 + 2)
                        for kp in range(KC // 2):
                            pe.wait_ge(xs_ready, i * 8 + kp + 1)
                            for k in (2 * kp, 2 * kp + 1):
                                for t in range(NT):
                                    at = (k % 2) * L + t * P
                                    tr = pe.transpose(PS[:, 6 + kp % 2, at:at + P], nrm1[:, t, k * P:(k + 1) * P], ident[:])
                            tr.then_inc(xp_done, 1)
                    else:
                        ins.then_inc(a0_half, 1)
            pe.wait_ge(a0_half, 2)
            pe.sem_inc(a0_done, 1)

            def transposes(c, src, ready=None):
                pe.wait_ge(nrm_ready, 2 * c + 2)
                for kp in range(KC // 2):
                    w = 8 * c + kp - 3
                    if w >= 1:
                        pe.wait_ge(xt_ready, w)
                    for h in range(2):
                        for t in range(NT):
                            k = 2 * kp + h
                            ins = pe.transpose(PS[:, 4 + kp % 4, h * L + t * P:h * L + (t + 1) * P], src[:, t, k * P:(k + 1) * P], ident[:])
                    ins.then_inc(xp_done, 1)

            def fm(U, f, width):
                p = 4 * (f % 2)
                for j in range(UPB):
                    pe.wait_ge(w_split, U.u(8 * (f % 2) + j, 1))
                    pe.wait_ge(xt_ready, 2 * j + 2)
                    for h in range(UNIT):
                        k = UNIT * j + h
                        for s in range(4):
                            dst = PS[:, p + s, 0:width]
                            c = h * CB + s * P
                            hi, lo = wh[:, j % SPLIT, c:c + P], wl[:, j % SPLIT, c:c + P]
                            mm(dst, hi, x1h[:, k, 0:width], start=(k == 0), stop=False)
                            mm(dst, hi, x1l[:, k, 0:width], start=False, stop=False)
                            ins = mm(dst, lo, x1h[:, k, 0:width], start=False, stop=(k == KC - 1))
                    ins.then_inc(w_used, 1)
                pe.wait_ge(w_used, U.u(8 * (f % 2) + 8, SPLIT))
                pe.sem_inc(fm_done, 1)

            pe.wait_ge(cols_ready, 1)
            with pe.Fori(0, 2) as i:
                for f in range(2):
                    pe.wait_ge(fm_read, i * 2 + f + 1)
                    fm(Units(U_KV, 16, i), f, 2 * L)
            for f in range(2):
                pe.wait_ge(fm_read, 5 + f)
                fm(Units(U_Q), f, L)
            pe.wait_ge(fm_read, 8)

            def x1(t):
                return slice(t * P, (t + 1) * P)
            xx = (lambda k, t: x1h[:, k, x1(t)], lambda k, t: x1l[:, k, x1(t)])
            pe.wait_ge(ab_split, 1)
            dst = PS[0:4 * H, 4, :]
            for k in range(KC):
                mm(dst, abh[:, k, :], x1h[:, k, :], start=(k == 0), stop=False)
                mm(dst, abh[:, k, :], x1l[:, k, :], start=False, stop=False)
                ins = mm(dst, abl[:, k, :], x1h[:, k, :], start=False, stop=(k == KC - 1))
            ins.then_inc(ab_done, 1)

            def ab_columns():
                pe.wait_ge(abT_ready, 1)
                for t in range(4):
                    ins = pe.transpose(PS[:, 5, t * 4 * H:(t + 1) * 4 * H], gamT[0:4 * H, t * P:(t + 1) * P], ident[0:4 * H, 0:4 * H])
                ins.then_inc(abr_done, 1)

            def cumulate():
                pe.wait_ge(g_ready, 1)
                for t in range(4):
                    for d in range(2):
                        c = t * 2 * H + d * H
                        ins = mm(PS[:, 5, c:c + H], incl[:, d, :], gt[:, 5, t, d * H:(d + 1) * H])
                ins.then_inc(gam_done, 1)

            def edges():
                pe.wait_ge(gam_ready, 1)
                for t in range(4):
                    for d in range(2):
                        c = t * 2 * H + d * H
                        ins = mm(PS[:, 7, c:c + H], edge[:, d, :], Q[:, 0, t, d, :])
                ins.then_inc(gam_done, 1)
                for t in range(4):
                    ins = pe.transpose(PS[0:16, 6, t * P:(t + 1) * P], Q[:, 0, t, :, :].rearrange("p d h -> p (d h)"), ident[:])
                ins.then_inc(gam_done, 1)

            for n in range(4):
                if n >= 2:
                    pe.wait_ge(acc_free[n % 2], 2 * (n // 2))
                tok(Units(U_ZP), 8 * n, n, xx, after={0: {1: ab_columns}, 1: {0: cumulate}, 2: {0: edges}}.get(n))
            pe.wait_ge(gamT_ready, 1)
            pe.wait_ge(acc_free[0], 4)
            pe.wait_ge(acc_free[1], 4)

            with pe.Fori(0, H // 2) as i:
                pe.wait_ge(pair_free, i * 4 + 4)
                for n, (src, bank) in enumerate(((kT, 0), (qT, 2))):
                    pe.wait_ge(squares_ready, i * 2 + n + 1)
                    for a in range(2):
                        dst = PS[:, a, :] if n == 0 else PS[:, 2, a * L:(a + 1) * L]
                        ins = mm(dst, ones[:], src[:, a, :])
                    ins.then_inc(nsum_done, 1)
                pe.wait_ge(pair_in, i * 48 + 48)
                for a in range(2):
                    for t in range(4):
                        ins = pe.transpose(PS[:, 6 + a, t * P:(t + 1) * P], cv[:, a, t * P:(t + 1) * P], ident[:])
                ins.then_inc(tok_done, 1)
                pe.wait_ge(kq_normed, i * 2 + 1)
                for a in range(2):
                    for t in range(4):
                        ins = pe.transpose(PS[:, 4 + a, t * P:(t + 1) * P], kT[:, a, t * P:(t + 1) * P], ident[:])
                ins.then_inc(tok_done, 1)
                for a in range(2):
                    for t in range(4):
                        k = kT[:, a, t * P:(t + 1) * P]
                        mm(PS[:, a, t * P:(t + 1) * P], k, k)
                pe.wait_ge(kq_normed, i * 2 + 2)
                for a in range(2):
                    for t in range(2):
                        ins = mm(PS[:, 2, a * L + t * P:a * L + (t + 1) * P], kT[:, a, t * P:(t + 1) * P], qT[:, a, t * P:(t + 1) * P])
                ins.then_inc(kk_done, 1)
                pe.wait_ge(sel_ready, i + 1)
                pe.wait_ge(tok_read, i * 2 + 2)
                for q in range(4):
                    ins = mm(PS[:, 4 + q, :], sel[0:16, q, :], gamT[0:16, :])
                ins.then_inc(row_done, 1)

                def flip(lv, s):
                    pe.wait_ge(xT_ready, i * 28 + 4 * lv + s + 1)
                    for q in range(4):
                        ins = pe.transpose(PS[:, s + (4 if lv == 0 else 0), q * P:(q + 1) * P], XT[:, s, q, :], ident[:])
                    ins.then_inc(tr_done, 1)

                for s in range(4):
                    flip(0, s)
                pe.wait_ge(qk_ready, i + 1)
                for lv in range(1, LEVELS):
                    for s in range(4):
                        pe.wait_ge(b_ready, i * 24 + 4 * (lv - 1) + s + 1)
                        pe.wait_ge(x_ready, i * 24 + 4 * (lv - 1) + s + 1)
                        for q in range(4):
                            ins = mm(PS[:, s, q * P:(q + 1) * P], B[:, s, q, :], X[:, s, q, :])
                        ins.then_inc(mm1_done, 1)
                    for s in range(4):
                        pe.wait_ge(p_ready, i * 24 + 4 * (lv - 1) + s + 1)
                        pe.wait_ge(xT_ready, i * 28 + 4 * (lv - 1) + s + 1)
                        for q in range(4):
                            ins = mm(halves(PS[:, 4 + s, q * P:(q + 1) * P], lv, 1 - q // 2), PB[:, s, q, :],
                                     halves(XT[:, s, q, :], lv, 1 - q // 2))
                        ins.then_inc(mm2_done, 1)
                    if lv < LEVELS - 1:
                        for s in range(4):
                            flip(lv, s)

                pe.wait_ge(xT_ready, i * 28 + 28)
                for s in range(4):
                    if s >= 1:
                        pe.wait_ge(s_ready, i * 4 + s)
                        for q in range(4):
                            t = TILE[q // 2][s]
                            ins = mm(PS[:, 0, q * P:(q + 1) * P], kT[:, q % 2, t * P:(t + 1) * P], S[:, q])
                        ins.then_inc(ks_done, 1)
                    col_sum(0, i, s)()
                    if s >= 2:
                        if s == 3:
                            pe.wait_ge(eq_ready, i * 2 + 1)
                        for q in range(4):
                            t = TILE[q // 2][s]
                            ins = mm(PS[:, 1, q * P:(q + 1) * P], qT[:, q % 2, t * P:(t + 1) * P], S[:, q])
                        ins.then_inc(qs_done, 1)
                    if s >= 1:
                        pe.wait_ge(r_ready, i * 3 + s)
                    for q in range(4):
                        rhs = R[:, q] if s >= 1 else vtok[:, q % 2, TILE[q // 2][s], :]
                        ins = mm(PS[:, 2, q * P:(q + 1) * P], XT[:, s, q, :], rhs)
                    ins.then_inc(y_done, 1)
                    pe.wait_ge(vd_ready, i * 4 + s + 1)
                    for q in range(4):
                        t = TILE[q // 2][s]
                        ins = mm(PS[:, 4, q * P:(q + 1) * P], ktok[:, q % 2, t, :], VD[:, q])
                    ins.then_inc(ds_done, 1)
                    if s >= 2:
                        pe.wait_ge(vn_ready, i * 2 + s - 1)
                        if s == 3:
                            pe.wait_ge(o_ready, i * 2 + 1)
                        for q in range(4):
                            ins = mm(PS[:, 3, q * P:(q + 1) * P], QK[:, s - 2, q], VN[:, q])
                        ins.then_inc(ov_done, 1)
                pe.wait_ge(s_ready, i * 4 + 4)
                pe.wait_ge(o_ready, i * 2 + 2)
                pe.sem_inc(pair_free, 1)

            pe.wait_ge(dn_done, 1)
            spread(0)()
            pe.wait_ge(branch_loaded, 16 * 5)
            for c in range(8):
                for t in range(NT):
                    ins = mm(PS[:, c // 2, (c % 2) * L:(c % 2 + 1) * L], pt[:, t, c * P:(c + 1) * P], poolm[:, c // 2, t, :],
                             start=(t == 0), stop=(t == 1))
            ins.then_inc(pool_done, 1)
            pe.wait_ge(poolT_ready, 1)
            pe.wait_ge(gate_ready, 1)
            for c in range(8):
                g = c // 2
                for h in range(2):
                    ins = mm(PS[:, 4 + g, (c % 2) * L:(c % 2 + 1) * L], poolw[:, g, h, (c % 2) * P:(c % 2 + 1) * P], poolT[:, 2 * g + h, :],
                             start=(h == 0), stop=(h == 1))
            ins.then_inc(yb_done, 1)
            pe.wait_ge(ya_ready, 1)
            for h in range(H):
                for t in range(NT):
                    ins = pe.transpose(PS[:, h // 2, (h % 2) * L + t * P:(h % 2) * L + (t + 1) * P], otok[:, t, h, :], ident[:])
            ins.then_inc(ya_done, 1)

            xx = (lambda k, t: xh[:, k, x1(t)], lambda k, t: xl[:, k, x1(t)])
            pe.wait_ge(y_ready, 16)
            for n in range(N_OUT, N_OUT + 4):
                pe.wait_ge(acc_free[n % 2], 2 * (n // 2))
                tok(Units(U_OUT), 8 * (n - N_OUT), n, xx, after={3: spread(1)} if n == N_OUT else None)

            def mlp(layer, base, n0):
                hl = [(lambda k, t, b=b: hth[:, b, k, x1(t)], lambda k, t, b=b: htl[:, b, k, x1(t)]) for b in range(2)]

                def turnover(T, tau):
                    def go():
                        pe.wait_ge(sqr_ready, T.tau(tau, 2))
                        if not (layer == 0 and tau == 0):
                            pe.wait_ge(ht_ready, T.tau(tau, 0))
                        for t in range(NT):
                            for c in range(4):
                                ins = pe.transpose(PS[:, 4 + t, c * P:(c + 1) * P], rbuf[:, t, c * P:(c + 1) * P], ident[:])
                            ins.then_inc(mt_done, 1)
                    return go

                def up(U, T, j, n, **kw):
                    pe.wait_ge(acc_free[n % 2], T.free(n))
                    tok(U, j, n, xx, **kw)

                def down(U, T, j, n, buf, after=None):
                    pe.wait_ge(acc_free[n % 2], T.free(n))
                    tok(U, j, n, hl[buf], last=SK // UNIT, after=after)

                def pair(U, T, j0, n, tau, buf):
                    up(U, T, j0, n)
                    up(U, T, j0 + 8, n + 1, after={4: turnover(T, tau)})
                    pe.wait_ge(ht_ready, T.tau(tau, 0))
                    down(U, T, j0 + 16, n + 2, 1 - buf)
                    down(U, T, j0 + 20, n + 3, 1 - buf, after={0: turnover(T, tau + 1)})
                    if layer == 0 and T.i is not None and not isinstance(T.i, int) and tau == 4:
                        down(U, T, j0 + 24, n + 4, 1 - buf, after={1: col_sum(5, T.i)})
                    else:
                        down(U, T, j0 + 24, n + 4, 1 - buf)
                    down(U, T, j0 + 28, n + 5, 1 - buf)

                U, T = Units(base), Turn(n0, layer)
                up(U, T, 0, 0, ready=(xt_ready, 16 if layer == 0 else 32), after={7: col_sum(4)} if layer == 0 else None)
                up(U, T, 8, 1, after={4: turnover(T, 0)})
                U, T = Units(base + 16), Turn(n0 + 2, layer)
                pe.wait_ge(sqr_ready, T.tau(1, 2))
                turnover(T, 1)()
                with pe.Fori(0, 3) as i:
                    U, T = Units(base + 16, 64, i), Turn(n0 + 2, layer, i)
                    pair(U, T, 0, 0, 2, 1)
                    pair(U, T, 32, 6, 4, 0)
                U, T = Units(base + 16 + 192), Turn(n0 + 2, layer, 3)
                pair(U, T, 0, 0, 2, 1)
                pe.wait_ge(ht_ready, T.tau(4, 0))
                for b in range(4):
                    down(U, T, 32 + 4 * b, 6 + b, 1, after={0: spread(2)} if layer == 0 and b == 0 else None)

            transposes(2, nrm)
            mlp(0, U_MLP0, N_MLP0)
            transposes(3, nrm)

            for n in range(N_OIN, N_OIN + 8):
                b = n - N_OIN
                pe.wait_ge(acc_free[n % 2], 2 * (n // 2))
                tok(Units(U_OIN), 8 * b, n, xx, ready=(xt_ready, 24) if b == 0 else None, after={0: col_sum(8)} if b == 1 else None)
            pe.wait_ge(ws_loaded, 16)
            pe.wait_ge(acc_free[0], 2 * 32)
            pe.wait_ge(acc_free[1], 2 * 32)
            for g in range(4):
                pe.wait_ge(v_normed, g + 1)
                for t in range(NT):
                    m = 2 * g + t
                    if m >= 4:
                        pe.wait_ge(um_ready, m - 3)
                    mm(PS[:, m % 4, :], wsT[:, g, :], vg[:, t, g * CB:(g + 1) * CB]).then_inc(mix_done, 1)
            for kp in range(8):
                pe.wait_ge(um_ready, 2 * (kp // 2) + 2)
                if kp >= 4:
                    pe.wait_ge(uml_ready, kp - 3)
                for h in range(2):
                    for t in range(NT):
                        k = 2 * kp + h
                        ins = pe.transpose(PS[:, 4 + kp % 4, h * L + t * P:h * L + (t + 1) * P], ug[:, t, k * P:(k + 1) * P], ident[:])
                ins.then_inc(um_done, 1)
            for n in range(N_OOUT, N_OOUT + 4):
                b = n - N_OOUT
                if b == 0:
                    pe.wait_ge(um_ready, 8)
                pe.wait_ge(acc_free[n % 2], 2 * (n // 2))
                tok(Units(U_OOUT), 8 * b, n, xx, ready=(uml_ready, 0) if b == 0 else None, after={0: {7: col_sum(9)}, 1: {4: spread(3)}}.get(b))
            transposes(4, nrm)
            mlp(1, U_MLP1, N_MLP1)


def kernel(**inputs):
    import numpy as np
    import concourse.bacc as bacc
    from concourse.bass_utils import run_bass_kernel_spmd as run

    f = {k: np.ascontiguousarray(v) for k, v in inputs.items()}

    def cols(a, n):
        a = np.asarray(a)
        return np.ascontiguousarray(np.moveaxis(a.reshape(a.shape[:-1] + (n, P)), -1, 0))

    arrays = {name: f[name] for name in ("x", "ctx", "ada_w", "ada_b", "mlp_w1", "mlp_w2", "ev_w_in", "ev_dt_bias", "ev_a_log",
                                         "ev_onorm_g", "ev_w_out", "od_w_in", "od_ln_g", "od_ln_b", "od_w_out", "final_g")}
    arrays["ccol"] = np.ascontiguousarray(np.stack([cols(f["c"][0], KC), cols(f["c_ctx"], KC)], -1))
    arrays["adab"] = cols(f["ada_b"].reshape(12, D), KC)
    arrays["gcol"] = cols(np.stack([f["norm1_g"], f["norm2_g"]], 1).reshape(4, D), KC)
    arrays["bscol"] = np.ascontiguousarray(f["od_bs"][0].T)
    arrays["convw"] = np.ascontiguousarray(f["ev_conv_w"][0].reshape(5, 3, H, P).transpose(3, 1, 2, 0).reshape(P, 3, H * 5))
    arrays["poolw"] = np.ascontiguousarray(f["ev_pool_w"][0].reshape(4, 2, P, 2 * P).transpose(2, 0, 1, 3))
    arrays["pscale"] = cols(f["ev_pool_scale"][0], 8)
    arrays["wsT"] = np.ascontiguousarray(f["od_ws"][0].transpose(2, 0, 1))
    j, i = np.meshgrid(np.arange(P), np.arange(P), indexing="ij")
    arrays["ident"] = np.eye(P, dtype=np.float32)
    arrays["ones"] = np.ones((P, P), np.float32)
    arrays["incl"] = np.stack([i >= j, i <= j], 1).astype(np.float32)
    arrays["edge"] = np.stack([j == P - 1, j == 0], 1).astype(np.float32)
    lv = [((i > j) & (i >> (v + 1) == j >> (v + 1)) & (i >> v != j >> v)).astype(np.float32) for v in range(LEVELS)]
    arrays["lmask"] = np.ascontiguousarray(np.stack([np.stack([m, m.T], 1) for m in lv], 1))
    t = np.arange(L)
    pm = []
    for r in (1, 2, 4, 8):
        hi, lo = np.minimum(t + r + 1, L), np.maximum(t - r, 0)
        m = ((t[None] >= lo[:, None]) & (t[None] < hi[:, None])) / (hi - lo)[:, None].astype(np.float32) - np.eye(L)
        pm.append(m.T.reshape(2, P, L))
    arrays["poolm"] = np.ascontiguousarray(np.stack(pm).transpose(2, 0, 1, 3).astype(np.float32))
    nf = D // 4
    omega = (1.0 / (10000.0 ** (np.arange(nf, dtype=np.float32) / np.float32(nf)))).astype(np.float32)
    ar = (t // 64).astype(np.float32)[:, None] * omega
    ac = (t % 64).astype(np.float32)[:, None] * omega
    arrays["pos"] = np.concatenate([np.sin(ar), np.cos(ar), np.sin(ac), np.cos(ac)], -1).astype(np.float32)

    nc = bacc.Bacc("TRN2", target_bir_lowering=False, num_devices=1)
    A = {n: nc.dram_tensor("in_" + n, a.shape, F32, kind="ExternalInput").ap() for n, a in arrays.items()}
    out = nc.dram_tensor("out", (1, L, D), F32, kind="ExternalOutput").ap()
    build(nc, A, out)
    r = run(nc, [{"in_" + n: a for n, a in arrays.items()}], core_ids=[0])
    return r.results[0]["out"]
```
